# Optimizing a Trainium2 kernel written in Bass

```python
import math
import jax, jax.numpy as jnp
from jax import lax
import numpy as np

D_MODEL = 1024
BATCH = 1
SEQ = 256
DEPTH = 2

N_MIXERS = 2
ROPE_THETA = 500000.0
ROT_DIM = 16
Q_BLOCK = 128
NORM_EPS = 1e-6
NEG_INF = -1e30

DA_HEAD_DIM = 64
DA_V_DIM = 2 * DA_HEAD_DIM
DA_HEADS = D_MODEL // DA_V_DIM

NSA_HEAD_DIM = 64
NSA_HEADS = D_MODEL // NSA_HEAD_DIM
NSA_KV_GROUPS = 2
NSA_HEADS_PER_GROUP = NSA_HEADS // NSA_KV_GROUPS
NSA_CMP_BLOCK = 32
NSA_CMP_STRIDE = 16
NSA_CMP_HIDDEN = 4 * NSA_HEAD_DIM
NSA_SEL_BLOCK = 64
NSA_TOP_N = 16
NSA_WINDOW = 512
NSA_FORCE = 1e4
NSA_IN_DIM = NSA_HEADS * NSA_HEAD_DIM + 6 * NSA_KV_GROUPS * NSA_HEAD_DIM + 3 * NSA_HEADS

MOE_GROUPS = 4
MOE_EXPERTS_PER_GROUP = 8
MOE_EXPERTS = MOE_GROUPS * MOE_EXPERTS_PER_GROUP
MOE_TOP_K = 2
MOE_HIDDEN = D_MODEL // 4


def _rmsnorm(x, g):
    xf = x.astype(jnp.float32)
    y = xf * lax.rsqrt(jnp.mean(xf * xf, axis=-1, keepdims=True) + NORM_EPS)
    return (y * g.astype(jnp.float32)).astype(x.dtype)

def _rope_tables(positions):
    inv_freq = ROPE_THETA ** (-jnp.arange(0, ROT_DIM, 2, dtype=jnp.float32) / ROT_DIM)
    ang = positions.astype(jnp.float32)[..., None] * inv_freq
    return jnp.cos(ang)[:, :, None, :], jnp.sin(ang)[:, :, None, :]

def _rotary(x, cos, sin):
    half = ROT_DIM // 2
    xr = x[..., :ROT_DIM].astype(jnp.float32)
    x1, x2 = xr[..., :half], xr[..., half:]
    rot = jnp.concatenate([x1 * cos - x2 * sin, x2 * cos + x1 * sin], axis=-1).astype(x.dtype)
    return jnp.concatenate([rot, x[..., ROT_DIM:]], axis=-1)

def _masked_softmax(s, mask):
    s = jnp.where(mask, s.astype(jnp.float32), NEG_INF)
    p = jnp.where(mask, jnp.exp(s - jnp.max(s, axis=-1, keepdims=True)), 0.0)
    return p / jnp.maximum(jnp.sum(p, axis=-1, keepdims=True), 1e-30)

def diff_attention(h, cos, sin, w_in, w_out, lam, subln_g, lambda_init):
    B, S, D = h.shape
    H, d = DA_HEADS, DA_HEAD_DIM
    q, k, v = jnp.split(h @ w_in, 3, axis=-1)
    q = _rotary(q.reshape(B, S, 2 * H, d), cos, sin).reshape(B, S, H, 2, d).transpose(3, 0, 2, 1, 4)
    k = _rotary(k.reshape(B, S, 2 * H, d), cos, sin).reshape(B, S, H, 2, d).transpose(3, 0, 2, 1, 4)
    v = v.reshape(B, S, H, DA_V_DIM).transpose(0, 2, 1, 3)
    lam = lam.astype(jnp.float32)
    lam_full = jnp.exp(jnp.sum(lam[0] * lam[1])) - jnp.exp(jnp.sum(lam[2] * lam[3])) + lambda_init
    scale = d ** -0.5
    k_pos = jnp.arange(S)

    def block(i):
        q0 = i * Q_BLOCK
        qb = lax.dynamic_slice_in_dim(q, q0, Q_BLOCK, axis=3)
        s = jnp.einsum('cbhqd,cbhkd->cbhqk', qb, k) * scale
        mask = k_pos[None, :] <= (q0 + jnp.arange(Q_BLOCK))[:, None]
        p = _masked_softmax(s, mask)
        a = p[0] - lam_full * p[1]
        return jnp.einsum('bhqk,bhkv->bhqv', a.astype(v.dtype), v)

    o = lax.map(block, jnp.arange(S // Q_BLOCK))
    o = o.transpose(1, 0, 3, 2, 4).reshape(B, S, H, DA_V_DIM)
    o = _rmsnorm(o, subln_g) * (1.0 - lambda_init)
    return o.reshape(B, S, D) @ w_out

def _nsa_compress(t, pos_emb, w1, b1, w2):
    B, G, S, d = t.shape
    ch = t.reshape(B, G, S // NSA_CMP_STRIDE, NSA_CMP_STRIDE, d)
    blk = jnp.concatenate([ch[:, :, :-1], ch[:, :, 1:]], axis=3) + pos_emb
    blk = blk.reshape(B, G, blk.shape[2], NSA_CMP_BLOCK * d)
    return jax.nn.gelu(blk @ w1 + b1) @ w2

def nsa_attention(h, cos, sin, w_in, w_out, cmp_pos, cmp_w1, cmp_b1, cmp_w2):
    B, S, D = h.shape
    H, G, Hg, d = NSA_HEADS, NSA_KV_GROUPS, NSA_HEADS_PER_GROUP, NSA_HEAD_DIM
    kvw = G * d
    proj = h @ w_in
    bounds = [H * d + j * kvw for j in range(7)]
    q, k_c, v_c, k_s, v_s, k_w, v_w, g_raw = jnp.split(proj, bounds, axis=-1)
    q = _rotary(q.reshape(B, S, H, d), cos, sin).reshape(B, S, G, Hg, d).transpose(0, 2, 3, 1, 4)

    def kv(t, rope):
        t = t.reshape(B, S, G, d)
        if rope:
            t = _rotary(t, cos, sin)
        return t.transpose(0, 2, 1, 3)

    k_c, v_c = kv(k_c, False), kv(v_c, False)
    k_s, v_s = kv(k_s, True), kv(v_s, True)
    k_w, v_w = kv(k_w, True), kv(v_w, True)
    gates = jax.nn.sigmoid(g_raw.astype(jnp.float32)).reshape(B, S, G, Hg, 3).transpose(0, 2, 3, 1, 4)

    k_cmp = _nsa_compress(k_c, cmp_pos[0], cmp_w1[0], cmp_b1[0], cmp_w2[0])
    v_cmp = _nsa_compress(v_c, cmp_pos[1], cmp_w1[1], cmp_b1[1], cmp_w2[1])
    n_cmp = k_cmp.shape[2]
    n_sel = S // NSA_SEL_BLOCK
    n_top = min(NSA_TOP_N, n_sel)
    cmp_start = jnp.arange(n_cmp) * NSA_CMP_STRIDE
    cmp_end = cmp_start + NSA_CMP_BLOCK - 1
    sel_start = jnp.arange(n_sel) * NSA_SEL_BLOCK
    cmp_to_sel = ((cmp_start[:, None] < sel_start[None, :] + NSA_SEL_BLOCK)
                  & (cmp_start[:, None] + NSA_CMP_BLOCK > sel_start[None, :])).astype(jnp.float32)
    k_blocks = k_s.reshape(B, G, n_sel, NSA_SEL_BLOCK, d)
    v_blocks = v_s.reshape(B, G, n_sel, NSA_SEL_BLOCK, d)
    pad = ((0, 0), (0, 0), (NSA_WINDOW, 0), (0, 0))
    k_w_pad, v_w_pad = jnp.pad(k_w, pad), jnp.pad(v_w, pad)
    b_ix = jnp.arange(B)[:, None, None, None]
    g_ix = jnp.arange(G)[None, :, None, None]
    blk_off = jnp.arange(NSA_SEL_BLOCK)
    sel_ids = jnp.arange(n_sel)
    scale = d ** -0.5

    def block(i):
        q0 = i * Q_BLOCK
        tq = q0 + jnp.arange(Q_BLOCK)
        qb = lax.dynamic_slice_in_dim(q, q0, Q_BLOCK, axis=3)
        s_c = jnp.einsum('bghqd,bgnd->bghqn', qb, k_cmp) * scale
        p_c = _masked_softmax(s_c, cmp_end[None, :] <= tq[:, None])
        o_c = jnp.einsum('bghqn,bgnd->bghqd', p_c.astype(v_cmp.dtype), v_cmp)
        imp = jnp.einsum('bgqn,ns->bgqs', p_c.sum(axis=2), cmp_to_sel)
        q_blk = tq // NSA_SEL_BLOCK
        forced = ((sel_ids[None, :] == 0) | (sel_ids[None, :] == q_blk[:, None])
                  | (sel_ids[None, :] == q_blk[:, None] - 1))
        causal = sel_ids[None, :] <= q_blk[:, None]
        imp = jnp.where(forced, NSA_FORCE, jnp.where(causal, imp, -NSA_FORCE))
        _, sel = lax.top_k(imp, n_top)
        k_sel = k_blocks[b_ix, g_ix, sel].reshape(B, G, Q_BLOCK, n_top * NSA_SEL_BLOCK, d)
        v_sel = v_blocks[b_ix, g_ix, sel].reshape(B, G, Q_BLOCK, n_top * NSA_SEL_BLOCK, d)
        tok = (sel[..., None] * NSA_SEL_BLOCK + blk_off).reshape(B, G, Q_BLOCK, n_top * NSA_SEL_BLOCK)
        s_s = jnp.einsum('bghqd,bgqkd->bghqk', qb, k_sel) * scale
        p_s = _masked_softmax(s_s, tok[:, :, None] <= tq[:, None])
        o_s = jnp.einsum('bghqk,bgqkd->bghqd', p_s.astype(v_sel.dtype), v_sel)
        k_win = lax.dynamic_slice_in_dim(k_w_pad, q0, Q_BLOCK + NSA_WINDOW, axis=2)
        v_win = lax.dynamic_slice_in_dim(v_w_pad, q0, Q_BLOCK + NSA_WINDOW, axis=2)
        tk = q0 - NSA_WINDOW + jnp.arange(Q_BLOCK + NSA_WINDOW)
        dist = tq[:, None] - tk[None, :]
        mask_w = (tk[None, :] >= 0) & (dist >= 0) & (dist < NSA_WINDOW)
        s_w = jnp.einsum('bghqd,bgkd->bghqk', qb, k_win) * scale
        p_w = _masked_softmax(s_w, mask_w)
        o_w = jnp.einsum('bghqk,bgkd->bghqd', p_w.astype(v_win.dtype), v_win)
        gb = lax.dynamic_slice_in_dim(gates, q0, Q_BLOCK, axis=3)
        o = gb[..., 0:1] * o_c + gb[..., 1:2] * o_s + gb[..., 2:3] * o_w
        return o.astype(h.dtype)

    o = lax.map(block, jnp.arange(S // Q_BLOCK))
    o = o.transpose(1, 0, 4, 2, 3, 5).reshape(B, S, D)
    return o @ w_out

def hier_moe(h, w_grp, b_grp, w_exp, b_exp, w_gate, w_up, w_down):
    B, S, D = h.shape
    t = h.reshape(B * S, D)
    T = t.shape[0]
    pg = jax.nn.softmax((t @ w_grp).astype(jnp.float32) + b_grp, axis=-1)
    p_top, grp = lax.top_k(pg, 1)
    le = jnp.einsum('td,gde->tge', t, w_exp).astype(jnp.float32) + b_exp
    le_sel = le[jnp.arange(T), grp[:, 0]]
    val, idx = lax.top_k(le_sel, MOE_TOP_K)
    wts = jax.nn.softmax(val, axis=-1) * p_top
    eid = grp * MOE_EXPERTS_PER_GROUP + idx
    combine = jnp.sum(jax.nn.one_hot(eid, MOE_EXPERTS, dtype=jnp.float32) * wts[..., None], axis=1)
    y = jnp.zeros_like(t)
    for gi in range(MOE_GROUPS):
        sl = slice(gi * MOE_EXPERTS_PER_GROUP, (gi + 1) * MOE_EXPERTS_PER_GROUP)
        a = jax.nn.silu(jnp.einsum('td,edh->teh', t, w_gate[sl])) * jnp.einsum('td,edh->teh', t, w_up[sl])
        a = a * combine[:, sl, None].astype(a.dtype)
        y = y + jnp.einsum('teh,ehd->td', a, w_down[sl]).astype(t.dtype)
    return y.reshape(B, S, D)

def first_inputs(seed: int = 0) -> dict:
    key = jax.random.key(seed)
    ks = iter(jax.random.split(key, 32))
    D = D_MODEL
    n_a = (DEPTH + N_MIXERS - 1) // N_MIXERS
    n_b = DEPTH // N_MIXERS

    def nrm(shape, scale):
        return jax.random.normal(next(ks), shape, jnp.float32) * scale

    return {
        'x': nrm((BATCH, SEQ, D), 1.0),
        'c': nrm((BATCH, D), 1.0),
        'positions': (jax.random.randint(next(ks), (BATCH, 1), 0, 4096) + jnp.arange(SEQ)[None, :]).astype(jnp.int32),
        'ada_w': nrm((DEPTH, D, 6 * D), 0.5 * D ** -0.5),
        'ada_b': nrm((DEPTH, 6 * D), 0.02),
        'norm_g': 1.0 + nrm((DEPTH, 2, D), 0.02),
        'final_g': 1.0 + nrm((D,), 0.02),
        'diff_w_in': nrm((n_a, D, 3 * D), D ** -0.5),
        'diff_w_out': nrm((n_a, D, D), D ** -0.5),
        'diff_lambda': nrm((n_a, 4, DA_HEAD_DIM), 0.1),
        'diff_subln_g': 1.0 + nrm((n_a, DA_V_DIM), 0.02),
        'nsa_w_in': nrm((n_b, D, NSA_IN_DIM), D ** -0.5),
        'nsa_w_out': nrm((n_b, D, D), D ** -0.5),
        'nsa_cmp_pos': nrm((n_b, 2, NSA_CMP_BLOCK, NSA_HEAD_DIM), 0.02),
        'nsa_cmp_w1': nrm((n_b, 2, NSA_CMP_BLOCK * NSA_HEAD_DIM, NSA_CMP_HIDDEN), (NSA_CMP_BLOCK * NSA_HEAD_DIM) ** -0.5),
        'nsa_cmp_b1': nrm((n_b, 2, NSA_CMP_HIDDEN), 0.02),
        'nsa_cmp_w2': nrm((n_b, 2, NSA_CMP_HIDDEN, NSA_HEAD_DIM), NSA_CMP_HIDDEN ** -0.5),
        'moe_w_group': nrm((DEPTH, D, MOE_GROUPS), D ** -0.5),
        'moe_b_group': nrm((DEPTH, MOE_GROUPS), 0.01),
        'moe_w_expert': nrm((DEPTH, MOE_GROUPS, D, MOE_EXPERTS_PER_GROUP), D ** -0.5),
        'moe_b_expert': nrm((DEPTH, MOE_GROUPS, MOE_EXPERTS_PER_GROUP), 0.01),
        'moe_w_gate': nrm((DEPTH, MOE_EXPERTS, D, MOE_HIDDEN), D ** -0.5),
        'moe_w_up': nrm((DEPTH, MOE_EXPERTS, D, MOE_HIDDEN), D ** -0.5),
        'moe_w_down': nrm((DEPTH, MOE_EXPERTS, MOE_HIDDEN, D), MOE_HIDDEN ** -0.5),
    }

def first_block(x, c, positions, ada_w, ada_b, norm_g, final_g,
              diff_w_in, diff_w_out, diff_lambda, diff_subln_g,
              nsa_w_in, nsa_w_out, nsa_cmp_pos, nsa_cmp_w1, nsa_cmp_b1, nsa_cmp_w2,
              moe_w_group, moe_b_group, moe_w_expert, moe_b_expert,
              moe_w_gate, moe_w_up, moe_w_down):
    cos, sin = _rope_tables(positions)
    c_act = jax.nn.silu(c)
    for i in range(DEPTH):
        mod = c_act @ ada_w[i] + ada_b[i]
        sh1, sc1, g1, sh2, sc2, g2 = jnp.split(mod[:, None, :], 6, axis=-1)
        h = _rmsnorm(x, norm_g[i, 0]) * (1.0 + sc1) + sh1
        j = i // N_MIXERS
        if i % N_MIXERS == 0:
            lambda_init = 0.8 - 0.6 * math.exp(-0.3 * i)
            mix = diff_attention(h, cos, sin, diff_w_in[j], diff_w_out[j], diff_lambda[j],
                                 diff_subln_g[j], lambda_init)
        else:
            mix = nsa_attention(h, cos, sin, nsa_w_in[j], nsa_w_out[j], nsa_cmp_pos[j],
                                nsa_cmp_w1[j], nsa_cmp_b1[j], nsa_cmp_w2[j])
        x = x + g1 * mix
        h = _rmsnorm(x, norm_g[i, 1]) * (1.0 + sc2) + sh2
        x = x + g2 * hier_moe(h, moe_w_group[i], moe_b_group[i], moe_w_expert[i], moe_b_expert[i],
                              moe_w_gate[i], moe_w_up[i], moe_w_down[i])
    return _rmsnorm(x, final_g)


HEAD_DIM = 64
D_MIX = D_MODEL
GROUP_W = D_MIX // 4
N_HEADS_A = GROUP_W // HEAD_DIM
N_HEADS_B = GROUP_W // HEAD_DIM
N_GROUPS_C = 4
N_GROUPS_D = 4
MOBA_BLOCK = 256
MOBA_TOPK = 3
QBLOCK = 128
ROPE_DIM = HEAD_DIM // 4
SGU_CHUNK = 128
POOL_WINDOWS = (2, 4, 8, 16)
D_FF = 2816
CONV_WIDTH = 3
DN_ALPHA = (2 * DEPTH) ** 0.25
DN_BETA = (8 * DEPTH) ** -0.25
LN_EPS = 1e-5
IN_SIZES = (GROUP_W, GROUP_W, GROUP_W, GROUP_W, GROUP_W, GROUP_W, N_HEADS_B, GROUP_W, GROUP_W, GROUP_W)
IN_SPLITS = tuple(int(s) for s in np.cumsum(IN_SIZES)[:-1])
N_IN = int(sum(IN_SIZES))


def layer_norm(x, g, b):
    xf = x.astype(jnp.float32)
    mu = jnp.mean(xf, axis=-1, keepdims=True)
    var = jnp.mean(jnp.square(xf - mu), axis=-1, keepdims=True)
    return ((xf - mu) * lax.rsqrt(var + LN_EPS) * g.astype(jnp.float32) + b.astype(jnp.float32)).astype(x.dtype)

def to_heads(t, n_heads):
    b, s, _ = t.shape
    return t.reshape(b, s, n_heads, -1).transpose(0, 2, 1, 3)

def from_heads(t):
    b, h, s, d = t.shape
    return t.transpose(0, 2, 1, 3).reshape(b, s, h * d)

def rotary_tables(seq_len):
    pos = jnp.arange(seq_len, dtype=jnp.float32)
    inv_freq = ROPE_THETA ** (-jnp.arange(0, ROPE_DIM, 2, dtype=jnp.float32) / ROPE_DIM)
    ang = pos[:, None] * inv_freq[None, :]
    return jnp.cos(ang), jnp.sin(ang)

def partial_rotary(x, cos, sin):
    half = ROPE_DIM // 2
    cos = cos.astype(x.dtype)
    sin = sin.astype(x.dtype)
    x1 = x[..., :half]
    x2 = x[..., half:ROPE_DIM]
    return jnp.concatenate([x1 * cos - x2 * sin, x1 * sin + x2 * cos, x[..., ROPE_DIM:]], axis=-1)

def moba_attention(q, k, v):
    bsz, h, s, hd = q.shape
    s_pad = -(-s // MOBA_BLOCK) * MOBA_BLOCK
    pad = ((0, 0), (0, 0), (0, s_pad - s), (0, 0))
    q, k, v = jnp.pad(q, pad), jnp.pad(k, pad), jnp.pad(v, pad)
    nb = s_pad // MOBA_BLOCK
    n_sel = min(MOBA_TOPK, nb)
    scale = hd ** -0.5
    kb = k.reshape(bsz, h, nb, MOBA_BLOCK, hd)
    vb = v.reshape(bsz, h, nb, MOBA_BLOCK, hd)
    kbar = jnp.mean(kb.astype(jnp.float32), axis=3)
    gate = jnp.einsum('bhsd,bhnd->bhsn', q.astype(jnp.float32), kbar)
    q_blk = jnp.arange(s_pad) // MOBA_BLOCK
    fully_past = jnp.arange(nb)[None, :] < q_blk[:, None]
    gate = jnp.where(fully_past, gate, -jnp.inf)
    _, sel = lax.top_k(gate, n_sel)
    bi = jnp.arange(bsz)[:, None, None, None]
    hi = jnp.arange(h)[None, :, None, None]

    def one_chunk(n):
        start = n * QBLOCK
        blk = start // MOBA_BLOCK
        qc = lax.dynamic_slice_in_dim(q, start, QBLOCK, axis=2)
        selc = lax.dynamic_slice_in_dim(sel, start, QBLOCK, axis=2)
        valid = selc < blk
        ks = kb[bi, hi, selc]
        vs = vb[bi, hi, selc]
        s_sel = jnp.einsum('bhqd,bhqnjd->bhqnj', qc, ks).astype(jnp.float32) * scale
        s_sel = jnp.where(valid[..., None], s_sel, -jnp.inf).reshape(bsz, h, QBLOCK, n_sel * MOBA_BLOCK)
        k_own = lax.dynamic_slice_in_dim(k, blk * MOBA_BLOCK, MOBA_BLOCK, axis=2)
        v_own = lax.dynamic_slice_in_dim(v, blk * MOBA_BLOCK, MOBA_BLOCK, axis=2)
        s_own = jnp.einsum('bhqd,bhjd->bhqj', qc, k_own).astype(jnp.float32) * scale
        qpos = start + jnp.arange(QBLOCK)
        kpos = blk * MOBA_BLOCK + jnp.arange(MOBA_BLOCK)
        s_own = jnp.where(kpos[None, :] <= qpos[:, None], s_own, -jnp.inf)
        p = jax.nn.softmax(jnp.concatenate([s_sel, s_own], axis=-1), axis=-1)
        p_sel = p[..., :n_sel * MOBA_BLOCK].reshape(bsz, h, QBLOCK, n_sel, MOBA_BLOCK).astype(v.dtype)
        p_own = p[..., n_sel * MOBA_BLOCK:].astype(v.dtype)
        return (jnp.einsum('bhqnj,bhqnjd->bhqd', p_sel, vs)
                + jnp.einsum('bhqj,bhjd->bhqd', p_own, v_own))

    outs = lax.map(one_chunk, jnp.arange(s_pad // QBLOCK))
    out = outs.transpose(1, 2, 0, 3, 4).reshape(bsz, h, s_pad, hd)
    return out[:, :, :s]

def forgetting_attention(q, k, v, log_f):
    bsz, h, s, hd = q.shape
    scale = hd ** -0.5
    c = jnp.cumsum(log_f, axis=-1)
    kpos = jnp.arange(s)

    def one_block(n):
        start = n * QBLOCK
        qc = lax.dynamic_slice_in_dim(q, start, QBLOCK, axis=2)
        cq = lax.dynamic_slice_in_dim(c, start, QBLOCK, axis=2)
        logits = (jnp.einsum('bhqd,bhkd->bhqk', qc, k).astype(jnp.float32) * scale
                  + cq[..., :, None] - c[..., None, :])
        qpos = start + jnp.arange(QBLOCK)
        logits = jnp.where(kpos[None, :] <= qpos[:, None], logits, -jnp.inf)
        p = jax.nn.softmax(logits, axis=-1).astype(v.dtype)
        return jnp.einsum('bhqk,bhkd->bhqd', p, v)

    outs = lax.map(one_block, jnp.arange(s // QBLOCK))
    return outs.transpose(1, 2, 0, 3, 4).reshape(bsz, h, s, hd)

def causal_spatial_gating(u, v, ln_g, ln_b, w_s, b_s):
    bsz, s, width = v.shape
    g = N_GROUPS_C
    c = width // g
    vn = layer_norm(v.reshape(bsz, s, g, c), ln_g.reshape(g, c), ln_b.reshape(g, c))
    vc = vn.reshape(bsz, s // SGU_CHUNK, SGU_CHUNK, g, c)
    causal = jnp.tril(jnp.ones((SGU_CHUNK, SGU_CHUNK), dtype=bool))
    w = jnp.where(causal[None], w_s, jnp.zeros_like(w_s))
    mixed = jnp.einsum('gts,bnsgc->bntgc', w, vc) + b_s.T[None, None, :, :, None]
    return u * mixed.reshape(bsz, s, width)

def multiscale_pool(p, w_g, scale):
    bsz, s, width = p.shape
    g = len(POOL_WINDOWS)
    c = width // g
    pg = p.reshape(bsz, s, g, c).astype(jnp.float32)
    cs = jnp.concatenate([jnp.zeros((bsz, 1, g, c), jnp.float32), jnp.cumsum(pg, axis=1)], axis=1)
    t = jnp.arange(s)
    outs = []
    for gi, win in enumerate(POOL_WINDOWS):
        cs_g = cs[:, :, gi]
        lo = jnp.maximum(t + 1 - win, 0)
        window_sum = cs_g[:, 1:] - cs_g[:, lo]
        count = jnp.minimum(t + 1, win).astype(jnp.float32)
        outs.append(window_sum / count[None, :, None] - pg[:, :, gi])
    pooled = jnp.stack(outs, axis=2).astype(p.dtype)
    mixed = jnp.einsum('bsgc,gcd->bsgd', pooled, w_g)
    return mixed.reshape(bsz, s, width) * scale

def hybrid_mixer(x, w_in, b_forget, sgu_ln_g, sgu_ln_b, sgu_w, sgu_b, pool_w, pool_scale, w_o, cos, sin):
    z = x @ w_in
    aq, ak, av, bq, bk, bv, bf, cu, cv, dp = jnp.split(z, IN_SPLITS, axis=-1)
    ya = moba_attention(partial_rotary(to_heads(aq, N_HEADS_A), cos, sin),
                        partial_rotary(to_heads(ak, N_HEADS_A), cos, sin),
                        to_heads(av, N_HEADS_A))
    log_f = jax.nn.log_sigmoid((bf + b_forget).astype(jnp.float32)).transpose(0, 2, 1)
    yb = forgetting_attention(to_heads(bq, N_HEADS_B), to_heads(bk, N_HEADS_B),
                              to_heads(bv, N_HEADS_B), log_f)
    yc = causal_spatial_gating(jax.nn.gelu(cu, approximate=False), jax.nn.gelu(cv, approximate=False),
                               sgu_ln_g, sgu_ln_b, sgu_w, sgu_b)
    yd = multiscale_pool(dp, pool_w, pool_scale)
    y = jnp.concatenate([from_heads(ya), from_heads(yb), yc, yd], axis=-1)
    return y @ w_o

def conv_gated_ffn(x, w_up, conv_w, conv_b, w_down):
    h = x @ w_up
    h = lax.conv_general_dilated(h, conv_w[:, None, :], window_strides=(1,),
                                 padding=[(CONV_WIDTH - 1, 0)],
                                 dimension_numbers=('NWC', 'WIO', 'NWC'),
                                 feature_group_count=h.shape[-1]) + conv_b
    gate, val = jnp.split(h, 2, axis=-1)
    return (jax.nn.silu(gate) * val) @ w_down

def second_inputs(seed: int = 0) -> dict:
    key = jax.random.key(seed)
    ks = jax.random.split(key, 20)
    L = DEPTH
    nrm = jax.random.normal
    f32 = jnp.float32
    ch = GROUP_W // N_GROUPS_D
    return {
        'x': nrm(ks[0], (BATCH, SEQ, D_MODEL), f32),
        'w_in': nrm(ks[1], (L, D_MODEL, N_IN), f32) * D_MODEL ** -0.5,
        'b_forget': 3.0 + 0.1 * nrm(ks[2], (L, N_HEADS_B), f32),
        'sgu_ln_g': 1.0 + 0.05 * nrm(ks[3], (L, GROUP_W), f32),
        'sgu_ln_b': 0.02 * nrm(ks[4], (L, GROUP_W), f32),
        'sgu_w': nrm(ks[5], (L, N_GROUPS_C, SGU_CHUNK, SGU_CHUNK), f32) * SGU_CHUNK ** -0.5,
        'sgu_b': 1.0 + 0.1 * nrm(ks[6], (L, N_GROUPS_C, SGU_CHUNK), f32),
        'pool_w': nrm(ks[7], (L, N_GROUPS_D, ch, ch), f32) * ch ** -0.5,
        'pool_scale': 1.0 + 0.1 * nrm(ks[8], (L, GROUP_W), f32),
        'w_o': nrm(ks[9], (L, D_MIX, D_MODEL), f32) * D_MIX ** -0.5 * DN_BETA,
        'ln1_g': 1.0 + 0.05 * nrm(ks[10], (L, D_MODEL), f32),
        'ln1_b': 0.02 * nrm(ks[11], (L, D_MODEL), f32),
        'w_up': nrm(ks[12], (L, D_MODEL, 2 * D_FF), f32) * D_MODEL ** -0.5,
        'conv_w': nrm(ks[13], (L, CONV_WIDTH, 2 * D_FF), f32) * CONV_WIDTH ** -0.5,
        'conv_b': 0.02 * nrm(ks[14], (L, 2 * D_FF), f32),
        'w_down': nrm(ks[15], (L, D_FF, D_MODEL), f32) * D_FF ** -0.5 * DN_BETA,
        'ln2_g': 1.0 + 0.05 * nrm(ks[16], (L, D_MODEL), f32),
        'ln2_b': 0.02 * nrm(ks[17], (L, D_MODEL), f32),
    }

def second_block(x, w_in, b_forget, sgu_ln_g, sgu_ln_b, sgu_w, sgu_b, pool_w, pool_scale, w_o,
              ln1_g, ln1_b, w_up, conv_w, conv_b, w_down, ln2_g, ln2_b):
    cos, sin = rotary_tables(x.shape[1])
    for l in range(DEPTH):
        y = hybrid_mixer(x, w_in[l], b_forget[l], sgu_ln_g[l], sgu_ln_b[l], sgu_w[l], sgu_b[l],
                         pool_w[l], pool_scale[l], w_o[l], cos, sin)
        x = layer_norm(DN_ALPHA * x + y, ln1_g[l], ln1_b[l])
        y = conv_gated_ffn(x, w_up[l], conv_w[l], conv_b[l], w_down[l])
        x = layer_norm(DN_ALPHA * x + y, ln2_g[l], ln2_b[l])
    return x


def setup_inputs(seed=0):
    out = dict(first_inputs(seed))
    for name, value in second_inputs(seed + 1).items():
        if name != "x":
            out[name + "_2"] = value
    return out


def reference(
    x, c, positions, ada_w, ada_b, norm_g, final_g, diff_w_in, diff_w_out, diff_lambda,
    diff_subln_g, nsa_w_in, nsa_w_out, nsa_cmp_pos, nsa_cmp_w1, nsa_cmp_b1, nsa_cmp_w2,
    moe_w_group, moe_b_group, moe_w_expert, moe_b_expert, moe_w_gate, moe_w_up, moe_w_down,
    w_in_2, b_forget_2, sgu_ln_g_2, sgu_ln_b_2, sgu_w_2, sgu_b_2, pool_w_2, pool_scale_2, w_o_2,
    ln1_g_2, ln1_b_2, w_up_2, conv_w_2, conv_b_2, w_down_2, ln2_g_2, ln2_b_2,
):
    x = first_block(
        x, c, positions, ada_w, ada_b, norm_g, final_g, diff_w_in, diff_w_out, diff_lambda,
        diff_subln_g, nsa_w_in, nsa_w_out, nsa_cmp_pos, nsa_cmp_w1, nsa_cmp_b1, nsa_cmp_w2,
        moe_w_group, moe_b_group, moe_w_expert, moe_b_expert, moe_w_gate, moe_w_up, moe_w_down,
    )
    return second_block(
        x, w_in_2, b_forget_2, sgu_ln_g_2, sgu_ln_b_2, sgu_w_2, sgu_b_2, pool_w_2, pool_scale_2,
        w_o_2, ln1_g_2, ln1_b_2, w_up_2, conv_w_2, conv_b_2, w_down_2, ln2_g_2, ln2_b_2,
    )


_drawn_inputs = setup_inputs


def setup_inputs(seed=0):
    import zlib

    import numpy as np

    out = dict(_drawn_inputs(seed))
    spreads = {}
    factors = {'diff_lambda': 7.032,
     'diff_subln_g': 4.088,
     'nsa_cmp_pos': 27.484,
     'nsa_cmp_b1': 31.457,
     'moe_b_group': 22.791,
     'moe_b_expert': 22.981,
     'b_forget_2': 64.0,
     'sgu_ln_g_2': 8.0,
     'sgu_ln_b_2': 31.315,
     'sgu_b_2': 3.593,
     'conv_b_2': 6.704,
     'pool_scale_2': 3.676}
    for name, (base, spread) in spreads.items():
        noise = np.random.default_rng([zlib.crc32(name.encode()), seed]).standard_normal(out[name].shape)
        drawn = base * np.exp(spread * noise) if base else spread * noise
        out[name] = __import__('jax').numpy.asarray(drawn.astype(out[name].dtype))
    for name, factor in factors.items():
        out[name] = (out[name] * factor).astype(out[name].dtype)
    return out
```

```python
from contextlib import ExitStack

import numpy as np
import concourse.bass as bass
from concourse import mybir

SEQ, D, P = 256, 1024, 128
NT, NC = SEQ // P, D // P
ROT = 8
EXPERTS, GROUPS, PER_GROUP, HID = 32, 4, 8, 256
FF = 2816
FF_GROUPS = FF // HID
NSA_IN, IN2 = 1840, 2308
CMP_N = 15
ROT_EPS, LN_EPS = 1e-6, 1e-5
ALPHA = 4.0 ** 0.25
LAMBDA_INIT = 0.2
NEG = -1e30
SLOTS, UNIT = 6, 2048

C_ID, C_TRI, C_ONE, C_MASK, C_EVEN = 0, 128, 256, 384, 512
C_CB, C_C01, C_R4, C_R32, C_INV = 640, 670, 700, 704, 736
C_COS, C_SIN, C_REP, C_BLK, C_BAND, C_END = 744, 760, 776, 904, 912, 2960
R_ADAB, R_NG, R_C, R_SUB, R_B1, R_PS, R_SB, R_END = 0, 48, 80, 88, 89, 93, 97, 105
N_ADA = 0
N_IN = {"a0": 24, "a1": 24 + 16 + 96}
N_OUT = {"a0": 36, "a1": N_IN["a1"] + 12}
N_CMP = N_IN["a1"] + 4
N_EXP = {"m0": 40, "m1": N_OUT["a1"] + 4}
N_IN["s0"] = N_EXP["m1"] + 96
N_OUT["s0"] = N_IN["s0"] + 10
N_EXP["f0"] = N_OUT["s0"] + 4
N_IN["s1"] = N_EXP["f0"] + 3 * FF_GROUPS
N_OUT["s1"] = N_IN["s1"] + 10
N_EXP["f1"] = N_OUT["s1"] + 4
COUNT = {"m0": EXPERTS, "m1": EXPERTS, "f0": FF_GROUPS, "f1": FF_GROUPS}
COLS = {
    "a0": [(c, 256) for c in range(0, 3072, 256)],
    "a1": [(1024, 256), (1280, 256), (1536, 256), (1792, 48)] + [(c, 256) for c in range(0, 1024, 256)],
    "s0": [(c, 256) for c in range(0, 2304, 256)] + [(2304, 4)],
}
COLS["s1"] = COLS["s0"]
ATT = ("a0", "a1", "s0", "s1")


def recurring():
    att = {"a0": 16, "a1": 32, "s0": 8, "s1": 8}
    units = {"a0": 8, "a1": 32, "s0": 8, "s1": 8}
    subs = ("a0", "m0", "a1", "m1", "s0", "f0", "s1", "f1")
    lns = ("first", "ln1_0", "ln2_0", "ln1_1", "ln2_1")
    r = {}
    for kind in ("in_done", "z"):
        r[kind] = {t: len(COLS[t]) for t in ATT}
    r["out_done"] = {t: 4 for t in ATT}
    for kind in ("qkT", "qk"):
        r[kind] = {"a0": 8, "a1": 6, "s0": 4, "s1": 4}
    for kind in ("scores", "max", "exp"):
        r[kind] = att
    for kind in ("norm", "turned", "probT", "pv"):
        r[kind] = units
    r["o"] = {"a0": 8, "a1": 8, "s0": 4, "s1": 4}
    r["roped"] = {"a0": 1, "a1": 2, "s0": 1, "s1": 1}
    for kind in ("xT", "hT_act", "hT_dve"):
        r[kind] = {t: 4 for t in subs}
    for kind in ("up_done", "down_done", "aT", "silu"):
        r[kind] = COUNT
    r["upc"] = {"m0": EXPERTS, "m1": EXPERTS}
    for kind in ("taps", "taps_gate", "conv", "conv_value"):
        r[kind] = {"f0": FF_GROUPS, "f1": FF_GROUPS}
    for kind in ("tap1", "tap2"):
        r[kind] = {"f0": 4 * FF_GROUPS, "f1": 4 * FF_GROUPS}
    r["xn"] = {t: NT for t in subs[:4]}
    r["x_done"] = {t: 1 for t in subs[:4]}
    r["ssq"] = {t: 1 for t in subs[:4] + lns[:1]}
    for kind in ("var", "rstd"):
        r[kind] = {t: 1 for t in subs[:4] + lns}
    r["tile"] = {t: NT for t in lns}
    r["done"] = {t: 1 for t in lns}
    return r


RECUR = recurring()


def split(name):
    parts = name.split("_")
    for n in range(1, len(parts)):
        tag, kind = "_".join(parts[:n]), "_".join(parts[n:])
        if kind in RECUR and tag in RECUR[kind]:
            return tag, kind
    return None, name


def constants():
    c = np.zeros((P, C_END), np.float32)
    i = np.arange(P)
    c[:, C_ID:C_ID + P] = np.eye(P)
    c[:, C_TRI:C_TRI + P] = i[:, None] <= i[None, :]
    c[:, C_ONE:C_ONE + P] = 1.0
    c[:, C_MASK:C_MASK + P] = np.where(i[None, :] <= i[:, None], 0.0, NEG)
    m = np.arange(64)
    for tp in range(2):
        c[:, C_EVEN + 64 * tp:C_EVEN + 64 * tp + 64] = i[:, None] == 2 * m[None, :] + tp
    n = np.arange(CMP_N)
    for t in range(NT):
        seen = 16 * n[None, :] + 31 <= (t * P + i)[:, None]
        c[:, C_CB + t * CMP_N:C_CB + (t + 1) * CMP_N] = np.where(seen, 0.0, NEG)
        c[:, C_C01 + t * CMP_N:C_C01 + (t + 1) * CMP_N] = seen
    c[:, C_R4:C_R4 + 4] = 4 - np.arange(4)
    c[:, C_R32:C_R32 + 32] = 32 - np.arange(32)
    inv = 500000.0 ** (-np.arange(0, 16, 2) / 16.0)
    c[:, C_INV:C_INV + 8] = inv
    inv = inv.astype(np.float32)
    for t in range(NT):
        ang = (t * P + i).astype(np.float32)[:, None] * inv[None, :]
        c[:, C_COS + 8 * t:C_COS + 8 * t + 8] = np.cos(ang)
        c[:, C_SIN + 8 * t:C_SIN + 8 * t + 8] = np.sin(ang)
    for h in range(8):
        for k in range(CMP_N):
            c[k, C_REP + 16 * h + k] = 1.0
        c[16 * h:16 * h + 16, C_BLK + h] = 1.0
    s, t = np.arange(SEQ), np.arange(SEQ)
    for g, win in enumerate((2, 4, 8, 16)):
        inside = (s[:, None] <= t[None, :]) & (s[:, None] > t[None, :] - win)
        band = inside / np.minimum(t + 1, win)[None, :] - (s[:, None] == t[None, :])
        for a in range(NT):
            at = C_BAND + (a * 4 + g) * SEQ
            c[:, at:at + SEQ] = band[a * P:(a + 1) * P]
    return c


def build(nc, A, out):
    f32, i32 = mybir.dt.float32, mybir.dt.int32
    ACT, ALU = mybir.ActivationFunctionType, mybir.AluOpType
    X = mybir.AxisListType.X
    ds = bass.ds

    with ExitStack() as ctx:
        sems = {}

        def S(name):
            name = split(name)[1]
            if name not in sems:
                sems[name] = ctx.enter_context(nc.semaphore(name))
            return sems[name]

        def nth(name, n):
            tag, kind = split(name)
            if tag is None:
                return S(name), n
            order = list(RECUR[kind])
            return S(name), n + sum(RECUR[kind][t] for t in order[:order.index(tag)])

        def sb(name, shape, dt=f32):
            return ctx.enter_context(nc.sbuf_tensor(name, shape, dt))

        ring = sb("ring", [P, SLOTS, UNIT])
        cst = sb("cst", [P, C_END])
        x = sb("x", [P, NT, D])
        xn = sb("xn", [P, NT, D])
        hT = sb("hT", [P, NC, SEQ])
        oT = sb("oT", [P, NC, SEQ])
        work = sb("work", [P, 10240])
        z = work[:, 0:6144].rearrange("p (t n) -> p t n", t=NT)
        qkT = work[:, 6144:10240].rearrange("p (c n) -> p c n", c=16)
        cmb = work[:, 0:8192].rearrange("p (e n) -> p e n", e=EXPERTS)
        acc = sb("acc", [P, 6 * D])
        gbc = sb("gbc", [P, 2, D])
        mixed = sb("mixed", [P, 3072])
        prob = mixed[:, 0:1536].rearrange("p (j n) -> p j n", j=4)
        probT = mixed[:, 1536:2304].rearrange("p (j n) -> p j n", j=2)
        sil = sb("sil", [P, 2, 512])
        upc = sb("upc", [P, 2, 512])
        aT = sb("aT", [P, 2, 512])
        adaw = mixed[:, :].rearrange("p (u k n) -> p u k n", u=2, k=4)
        adat = sb("adat", [P, 384])
        rows = sb("rows", [P, 3, P])
        colA = sb("colA", [P, R_END])
        colB = sb("colB", [P, 80])
        csil = sb("csil", [P, NC])
        modc = sb("modc", [P, 48])
        ng = sb("ng", [P, 2, NC])
        rw = sb("rw", [P, NC, 36])
        rb = sb("rb", [P, 36])
        lamt = sb("lamt", [P, 4, 64])
        sm = sb("sm", [P, 64])
        posi = sb("posi", [P, NT], i32)
        rope = sb("rope", [P, 6, 16])
        rt = sb("rt", [P, 4, 256])
        nmax = sb("nmax", [P, 4, 2])
        psum_ = sb("psum_", [P, 4, 2])
        rsum = sb("rsum", [P, 4, 2])
        lg = sb("lg", [P, NT, 36])
        rs = sb("rs", [P, 10, 64])
        cbT = sb("cbT", [32, SEQ])
        gate = sb("gate", [P, NT, 48])
        stat = sb("stat", [P, NT, 2, 6])
        mv = sb("mv", [P, NT, 2])
        fox = sb("fox", [P, 4, 8])
        cum = sb("cum", [4, 2, SEQ])
        bfor = sb("bfor", [P, 4])
        pw = sb("pw", [P, 2, 64])
        kd = acc[:, 0:1024].rearrange("p (t a n) -> p t a n", t=NT, a=4)
        kdT = acc[:, 1024:2048].rearrange("p (a n) -> p a n", a=4)
        blk = acc[:, 2048:3008].rearrange("p (v j n) -> p v j n", v=2, j=16)
        vblk = acc[:, 3008:4032].rearrange("p (g h d) -> p g h d", g=2, h=8)
        pc = acc[:, 4032:4544].rearrange("p (t h n) -> p t h n", t=NT, h=16)
        pcT = acc[:, 4544:5056].rearrange("p (g n) -> p g n", g=2)
        hid = acc[:, 5056:5176].rearrange("p (v c n) -> p v c n", v=2, c=2)
        kcT = acc[:, 5176:5206]
        vc = acc[:, 5206:5334].rearrange("p (g d) -> p g d", g=2)
        cw2 = acc[:, 5334:5718].rearrange("p (c n) -> p c n", c=2)
        cms = acc[:, 5718:5846].rearrange("p (a n) -> p a n", a=4)
        sgw = acc[:, 0:512].rearrange("p (g n) -> p g n", g=4)
        sgwT = acc[:, 512:1024].rearrange("p (g n) -> p g n", g=4)
        sgl = acc[:, 1024:1536].rearrange("p (a n) -> p a n", a=2)
        sgt = acc[:, 1536:2048].rearrange("p (t n) -> p t n", t=NT)
        pool = acc[:, 2048:2560].rearrange("p (c n) -> p c n", c=2)
        cvt = acc[:, 2560:4608].rearrange("p (b c n) -> p b c n", b=2, c=4)
        cvrow = acc[:, 4608:5120].rearrange("p (w n) -> p w n", w=4)
        cvc = acc[:, 5120:5296].rearrange("p (w n) -> p w n", w=4)
        cvcur = acc[:, 5296:5328].rearrange("p (b w n) -> p b w n", b=2, w=4)

        bank = [ctx.enter_context(nc.psum_tensor(f"bank{i}", [P, 512], f32)) for i in range(8)]
        scratch = nc.dram_tensor("combine_rows", (2, EXPERTS * SEQ), f32, kind="Internal").ap()

        ident, ones = cst[:, C_ID:C_ID + P], cst[:, C_ONE:C_ONE + P]
        tri, maskb = cst[:, C_TRI:C_TRI + P], cst[:, C_MASK:C_MASK + P]

        def pair(b):
            return bank[b][:, :].rearrange("p (c n) -> p c n", c=2)

        def slot(n):
            return ring[:, n % SLOTS, :]

        def landed(eng, n, more=0):
            eng.wait_ge(*nth(f"weights_landed{n % SLOTS}", 16 * (n // SLOTS + 1) + 16 * more))

        class Chain:
            def __init__(self, eng, name):
                self.eng, self.sem, self.n = eng, S(name), 0

            def __call__(self, ins):
                self.n += 1
                ins.then_inc(self.sem, 1)

            def sync(self):
                self.eng.wait_ge(self.sem, self.n)

        def attention(tag):
            jobs, units = [], []
            if tag == "a0":
                for j in range(16):
                    jobs.append(dict(par=j % 2, q=qkT[:, j // 2, :], k=qkT[:, 8 + j // 2, :], fox=None))
                for u in range(8):
                    units.append(dict(jobs=(2 * u, 2 * u + 1), v=2048 + 128 * u, M=128, off=0,
                                      group=u, first=True, last=True))
            elif tag == "a1":
                for j in range(32):
                    h, w = j // 2, j % 2
                    jobs.append(dict(par=h % 2, q=qkT[:, h // 2, :], k=kdT[:, 2 * w + h // 8, :], fox=None))
                    units.append(dict(jobs=(j,), v=(1664 if w else 1408) + 64 * (h // 8), M=64,
                                      off=64 * (h % 2), group=h // 2, first=w == 0,
                                      last=h % 2 == 1 and w == 1, h=h, w=w))
            else:
                for j in range(8):
                    b, h = j // 4, j % 4
                    jobs.append(dict(par=h % 2, q=qkT[:, 4 * b + h // 2, :],
                                     k=qkT[:, 4 * b + 2 + h // 2, :], fox=h if b else None))
                    units.append(dict(jobs=(j,), v=(1280 if b else 512) + 64 * h, M=64,
                                      off=64 * (h % 2), group=j // 2, first=True, last=h % 2 == 1))
            ends = {u["jobs"][-1]: n for n, u in enumerate(units)}
            return jobs, units, ends

        def w_in(tag, c, w):
            src = A["diff_w_in"][0] if tag == "a0" else A["nsa_w_in"][0] if tag == "a1" else A["w_in_2"][int(tag[1])]
            return src[:, c:c + w].rearrange("(k p) n -> p k n", p=P)

        def w_out(tag, j):
            src = A["diff_w_out"][0] if tag == "a0" else A["nsa_w_out"][0] if tag == "a1" else A["w_o_2"][int(tag[1])]
            return src[:, 256 * j:256 * j + 256].rearrange("(k p) n -> p k n", p=P)

        block = ctx.enter_context(nc.Block())

        @block.sync
        def _(sp):
            def load(n, src, width=256, more=0):
                dst = slot(n)[:, 0:src_free(src)]
                if len(src.shape) == 3:
                    dst = dst.rearrange("p (k n) -> p k n", k=src.shape[1])
                sp.dma_start(dst, src).then_inc(S(f"weights_landed{n % SLOTS}"), 16)

            def src_free(src):
                r = 1
                for s in src.shape[1:]:
                    r *= s
                return r

            def last_reader(n):
                m = n - SLOTS
                for tag, first in N_EXP.items():
                    if first <= m < first + 3 * COUNT[tag]:
                        e, part = divmod(m - first, 3)
                        return nth(f"{tag}_up_done" if part < 2 else f"{tag}_down_done", e + 1)
                for tag in ATT:
                    if N_IN[tag] <= m < N_OUT[tag]:
                        j = m - N_IN[tag]
                        if tag == "a1" and 4 <= j < 8:
                            return nth("a1_hidden_done", (j - 4) // 2 + 1)
                        if tag == "a1" and j >= 8:
                            j -= 4
                        return nth(f"{tag}_in_done", j + 1)
                    if N_OUT[tag] <= m < N_OUT[tag] + 4:
                        return nth(f"{tag}_out_done", m - N_OUT[tag] + 1)
                return nth("ada0_done", m + 1)

            def stream(n, src):
                if n >= SLOTS:
                    sp.wait_ge(*last_reader(n))
                load(n, src)

            def projection(tag):
                n = N_IN[tag]
                for j, (c, w) in enumerate(COLS[tag]):
                    if tag == "a1" and j == 4:
                        for m in range(4):
                            src = A["nsa_cmp_w1"][0, m // 2, (m % 2) * 1024:(m % 2) * 1024 + 1024, :]
                            stream(n, src.rearrange("(k p) n -> p k n", p=P))
                            n += 1
                    stream(n, w_in(tag, c, w))
                    n += 1
                for j in range(4):
                    stream(N_OUT[tag] + j, w_out(tag, j))

            def expert(tag, e, i=None):
                if tag[0] == "m":
                    layer = int(tag[1])
                    up = [A[w][layer, ds(e, 1)].rearrange("o (k p) n -> p (o k) n", p=P)
                          for w in ("moe_w_gate", "moe_w_up")]
                    return up + [A["moe_w_down"][layer, ds(e, 1)].rearrange("o (k p) n -> p (o k) n", p=P)]
                layer = int(tag[1])
                up = [A["w_up_2"][layer][:, ds(e * HID + half * FF, HID)].rearrange("(k p) n -> p k n", p=P)
                      for half in range(2)]
                return up + [A["w_down_2"][layer][ds(e * HID, HID), :].rearrange("(k p) n -> p k n", p=P)]

            def experts(tag):
                first, count = N_EXP[tag], COUNT[tag]
                layer1 = A["ada_w"][1].rearrange("(k p) n -> p k n", p=P)

                def ada1(i, u):
                    sp.dma_start(adaw[:, u], layer1[:, 4 * u:4 * u + 4, ds(i * 384, 384)])\
                      .then_inc(S(f"ada1_landed{u}"), 16)

                for e in (0, 1):
                    for part, src in enumerate(expert(tag, e)):
                        stream(first + 3 * e + part, src)
                    if tag == "m0":
                        ada1(0, e)
                with sp.Fori(1, count // 2) as i:
                    for u in (0, 1):
                        for part, src in enumerate(expert(tag, i * 2 + u)):
                            done = f"{tag}_up_done" if part < 2 else f"{tag}_down_done"
                            sp.wait_ge(*nth(done, i * 2 + (u - 1)))
                            load(first + 3 * u + part, src)
                        if tag == "m0":
                            sp.wait_ge(*nth(f"ada1_used{u}", i))
                            ada1(i, u)
                if count % 2:
                    for part, src in enumerate(expert(tag, count - 1)):
                        stream(first + 3 * (count - 1) + part, src)

            for n in range(24):
                k, third = divmod(n, 3)
                stream(n, A["ada_w"][0, k * P:(k + 1) * P, third * 2048:(third + 1) * 2048])
            projection("a0")
            experts("m0")
            projection("a1")
            experts("m1")
            for l in "01":
                projection("s" + l)
                experts("f" + l)

        @block.gpsimd
        def _(pool_eng):
            g = pool_eng

            def aux(name, dst, src):
                g.dma_start(dst, src).then_inc(S(name), 16)

            def row(src):
                return src.rearrange("(o n) -> o n", o=1)

            def everywhere(src):
                return row(src).broadcast_to([P, src.shape[0]])

            g.memset(rows[:, :, :], 0.0).then_inc(S("rows_clear"), 1)
            g.wait_ge(*nth("rows_clear", 1))
            aux("rowc_landed", rows[0:NC, 2, :], A["c"][0].rearrange("(c p) -> c p", p=P))
            aux("const_landed", cst[:, :], A["consts"])
            ra = rows[:, 0, :]
            aux("rows_landed", ra[0:48, :], A["ada_b"][0].rearrange("(c p) -> c p", p=P))
            aux("rows_landed", ra[R_NG:R_NG + 32, :], A["norm_g"].rearrange("l s (c p) -> (l s c) p", p=P))
            aux("rows_landed", ra[R_SUB:R_SUB + 1, :], A["diff_subln_g"])
            aux("rows_landed", ra[R_B1:R_B1 + 4, :], A["nsa_cmp_b1"][0].rearrange("v (c p) -> (v c) p", p=P))
            aux("rows_landed", ra[R_PS:R_PS + 4, :], A["pool_scale_2"].rearrange("l (c p) -> (l c) p", p=P))
            aux("rows_landed", ra[R_SB:R_SB + 8, :], A["sgu_b_2"].rearrange("l g t -> (l g) t"))
            aux("rows_landed", rows[0:48, 1, :], A["ada_b"][1].rearrange("(c p) -> c p", p=P))
            aux("rows_landed", rows[48:80, 1, :],
                A["nsa_cmp_pos"][0].rearrange("v (j t) d -> (v j) (t d)", t=2))
            aux("x_landed", x[:, :, :], A["x"][0].rearrange("(t p) n -> p t n", p=P))
            for t in range(NT):
                aux("pos_landed", posi[:, t:t + 1], A["positions"][0, t * P:(t + 1) * P].rearrange("(p o) -> p o", o=1))
            aux("lam_landed", lamt[:, :, :].rearrange("p a b -> p (a b)"),
                everywhere(A["diff_lambda"][0].rearrange("a b -> (a b)")))

            def gates(l):
                for n, v in enumerate((2, 5)):
                    aux("gbc_landed", gbc[:, n, :], everywhere(A["ada_b"][l, v * D:(v + 1) * D]))

            def router(l):
                aux("router_landed", rw[:, :, 0:4], A["moe_w_group"][l].rearrange("(k p) n -> p k n", p=P))
                for q in range(GROUPS):
                    aux("router_landed", rw[:, :, 4 + 8 * q:12 + 8 * q],
                        A["moe_w_expert"][l, q].rearrange("(k p) n -> p k n", p=P))
                aux("router_landed", rb[:, 0:4], everywhere(A["moe_b_group"][l]))
                aux("router_landed", rb[:, 4:36], everywhere(A["moe_b_expert"][l].rearrange("a b -> (a b)")))

            def combine(l):
                g.wait_ge(*nth("combine_rows_ready", l + 1))
                aux("combine_stored", scratch[l].rearrange("(e t) -> e t", e=EXPERTS), cbT[:, :])
                g.wait_ge(*nth("combine_stored", 16 * (l + 1)))
                aux("combine_landed", work[:, 0:8192], everywhere(scratch[l]))

            gates(0)
            router(0)
            combine(0)
            router(1)
            g.wait_ge(*nth("m0_x_done", 1))
            gates(1)
            g.wait_ge(*nth("mod_done", 2))
            aux("cmpw_landed", cw2[:, :, 0:64], A["nsa_cmp_w2"][0, 0].rearrange("(c p) n -> p c n", p=P))
            aux("cmpw_landed", cw2[:, :, 64:128], A["nsa_cmp_w2"][0, 0].rearrange("(c p) n -> p c n", p=P))
            aux("cmpw_landed", cw2[:, :, 128:192], A["nsa_cmp_w2"][0, 1].rearrange("(c p) n -> p c n", p=P))
            combine(1)
            aux("final_landed", gbc[:, 0, :], everywhere(A["final_g"]))

            def ln(name, l):
                for n, v in enumerate(("g", "b")):
                    aux(f"{name}{l}_landed", gbc[:, n, :], everywhere(A[f"{name}_{v}_2"][l]))

            for l in range(2):
                if l == 0:
                    g.wait_ge(*nth("first_done", 1))
                else:
                    g.wait_ge(*nth("ln2_0_done", 1))
                ln("ln1", l)
                aux("mix_landed", sgw[:, :, :], A["sgu_w_2"][l].rearrange("g t s -> t g s"))
                aux("mix_landed", sgl[:, 0, :], everywhere(A["sgu_ln_g_2"][l]))
                aux("mix_landed", sgl[:, 1, :], everywhere(A["sgu_ln_b_2"][l]))
                aux("mix_landed", bfor[:, :], everywhere(A["b_forget_2"][l]))
                aux("mix_landed", pw[:, :, :], A["pool_w_2"][l].rearrange("(b a) c d -> (a c) b d", a=2))
                for w in range(3):
                    aux("conv_landed", cvrow[0:44, w, :], A["conv_w_2"][l, w].rearrange("(c p) -> c p", p=P))
                aux("conv_landed", cvrow[0:44, 3, :], A["conv_b_2"][l].rearrange("(c p) -> c p", p=P))
                g.wait_ge(*nth(f"ln1_{l}_done", 1))
                ln("ln2", l)
            for t in range(NT):
                g.wait_ge(*nth("ln2_1_tile", t + 1))
                g.dma_start(out[0, t * P:(t + 1) * P, :], x[:, t, :]).then_inc(S("out_stored"), 16)
            g.wait_ge(*nth("out_stored", 32))

        @block.tensor
        def _(pe):
            def mm(o, l, r, start=True, stop=True):
                return pe.matmul(o, l, r, start=start, stop=stop, skip_group_check=True)

            def columns(first, n, tag):
                for i in range(first, first + n):
                    last = pe.transpose(bank[7][:, i * P:i * P + P], rows[:, i, :], ident)
                last.then_inc(S(tag), 1)

            def modulation(l):
                pe.wait_ge(*nth("ada0_done" if l == 0 else "ada1_done", 24 if l == 0 else 16))
                for v in (0, 1, 3, 4):
                    for c in range(NC):
                        at = v * D + c * P
                        last = mm(bank[7][:, v * 8 + c:v * 8 + c + 1], acc[:, at:at + P], ones[:, 0:1])
                last.then_inc(S("modc_ready"), 1)
                for n, v in enumerate((2, 5)):
                    for h in range(2):
                        last = mm(bank[2 * n + h][:, :], ones, acc[:, v * D + h * 512:v * D + h * 512 + 512])
                last.then_inc(S("modg_ready"), 1)

            def transposes(tag, src, ready):
                for b in range(4):
                    for c in (2 * b, 2 * b + 1):
                        for t in range(NT):
                            if c == 0:
                                pe.wait_ge(*nth(ready, t + 1))
                            if c == 6 and t == 0 and tag in ("a0", "a1"):
                                pe.wait_ge(*nth("modc_read", int(tag[1]) + 1))
                            last = pe.transpose(bank[4 + b][:, (c % 2) * 256 + t * P:(c % 2) * 256 + t * P + P],
                                                src[:, t, c * P:(c + 1) * P], ident)
                    last.then_inc(S(f"{tag}_xT"), 1)

            def hT_ready(tag):
                pe.wait_ge(*nth(f"{tag}_hT_act", 4))
                pe.wait_ge(*nth(f"{tag}_hT_dve", 4))

            def project(tag, j, n):
                c, w = COLS[tag][j]
                landed(pe, n)
                if j >= 4:
                    pe.wait_ge(*nth(f"{tag}_z", j - 3))
                W = slot(n)[:, 0:8 * w].rearrange("p (k n) -> p k n", k=NC)
                for t in range(NT):
                    for k in range(NC):
                        last = mm(pair(4 + j % 4)[:, t, 0:w], hT[:, k, t * P:(t + 1) * P], W[:, k, :],
                                  start=k == 0, stop=k == NC - 1)
                last.then_inc(S(f"{tag}_in_done"), 1)

            def project_out(tag):
                for j in range(4):
                    n = N_OUT[tag] + j
                    landed(pe, n)
                    W = slot(n).rearrange("p (k n) -> p k n", k=NC)
                    for t in range(NT):
                        for k in range(NC):
                            last = mm(pair(4 + j)[:, t, :], oT[:, k, t * P:(t + 1) * P], W[:, k, :],
                                      start=k == 0, stop=k == NC - 1)
                    last.then_inc(S(f"{tag}_out_done"), 1)

            def head_transposes(tag, sources):
                for i, (view, c) in enumerate(sources):
                    b = (i // 2) % 4
                    if i % 2 == 0 and i >= 8:
                        pe.wait_ge(*nth(f"{tag}_qk", i // 2 - 3))
                    for t in range(NT):
                        last = pe.transpose(bank[b][:, (i % 2) * 256 + t * P:(i % 2) * 256 + t * P + P],
                                            view[:, t, c:c + P], ident)
                    if i % 2:
                        last.then_inc(S(f"{tag}_qkT"), 1)

            def attend(tag, after=None):
                jobs, units, ends = attention(tag)
                J = len(jobs)

                def scores(j):
                    job = jobs[j]
                    if j >= 4:
                        pe.wait_ge(*nth(f"{tag}_exp", j - 3))
                    rows_ = slice(64 * job["par"], 64 * job["par"] + 64)
                    for t, (at, kl) in enumerate(((0, P), (P, SEQ))):
                        o = bank[j % 4][:, at:at + kl]
                        mm(o, job["q"][rows_, t * P:(t + 1) * P], job["k"][rows_, 0:kl], stop=False)
                        if job["fox"] is not None:
                            h = job["fox"]
                            mm(o, ident[0:4, h:h + 1].broadcast_to([4, P]), cum[:, 1, 0:kl], False, False)
                            mm(o, cum[:, 0, t * P:(t + 1) * P], ident[0:4, h:h + 1].broadcast_to([4, kl]),
                               False, False)
                        last = mm(bank[j % 4][:, at + kl - P:at + kl], ident, maskb, start=False)
                    last.then_inc(S(f"{tag}_scores"), 1)

                def turn(u):
                    pe.wait_ge(*nth(f"{tag}_norm", u + 1))
                    if u >= 2:
                        pe.wait_ge(*nth(f"{tag}_probT", u - 1))
                    j = units[u]["jobs"][0]
                    for b in range(3):
                        last = pe.transpose(bank[4 + u % 2][:, b * P:(b + 1) * P],
                                            prob[:, j % 4, b * P:(b + 1) * P], ident)
                    last.then_inc(S(f"{tag}_turned"), 1)

                def values(u):
                    U = units[u]
                    pe.wait_ge(*nth(f"{tag}_probT", u + 1))
                    if U["first"] and U["group"] >= 2 and U["off"] == 0:
                        pe.wait_ge(*nth(f"{tag}_o", U["group"] - 1))
                    o = bank[6 + U["group"] % 2][U["off"]:U["off"] + U["M"], :]
                    mm(o[:, 0:SEQ], z[:, 0, U["v"]:U["v"] + U["M"]], probT[:, u % 2, 0:SEQ],
                       start=U["first"], stop=False)
                    last = mm(o[:, P:SEQ], z[:, 1, U["v"]:U["v"] + U["M"]], probT[:, u % 2, SEQ:384],
                              start=False, stop=tag != "a1")
                    if tag == "a1" and U["w"] == 1:
                        g_ = U["h"] // 8
                        if u == 1:
                            pe.wait_ge(*nth("cmp_ready", 2))
                        last = mm(o[:, 0:SEQ], vblk[:, g_, U["h"] % 8, :], pcT[:, g_, :], start=False)
                    last.then_inc(S(f"{tag}_pv"), 1)

                for j in range(J + 4):
                    if j < J:
                        scores(j)
                    if j - 2 in ends:
                        turn(ends[j - 2])
                    if j - 3 in ends:
                        values(ends[j - 3])

            def experts(tag):
                first, count = N_EXP[tag], COUNT[tag]

                def up(e, i=0):
                    for part in range(2):
                        n = first + 3 * e + part
                        landed(pe, n, i)
                        W = slot(n).rearrange("p (k n) -> p k n", k=NC)
                        for c in range(2):
                            for k in range(NC):
                                last = mm(pair(4 + 2 * (e % 2) + part)[:, c, :], W[:, k, c * P:(c + 1) * P],
                                          hT[:, k, :], start=k == 0, stop=k == NC - 1)
                    last.then_inc(S(f"{tag}_up_done"), 1)

                def down(e, i=0, start=False):
                    n = first + 3 * e + 2
                    landed(pe, n, i)
                    pe.wait_ge(*nth(f"{tag}_aT", i * 2 + e + 1))
                    W = slot(n).rearrange("p (k n) -> p k n", k=2)
                    a = aT[:, e % 2, :].rearrange("p (c n) -> p c n", c=2)
                    for t in range(NT):
                        for h in range(2):
                            for c in range(2):
                                last = mm(bank[2 * t + h][:, :], a[:, c, t * P:(t + 1) * P],
                                          W[:, c, h * 512:(h + 1) * 512], start=start and c == 0, stop=True)
                    last.then_inc(S(f"{tag}_down_done"), 1)

                if tag[0] == "m":
                    l = int(tag[1])
                    pe.wait_ge(*nth("router_landed", 7 * 16 * (l + 1)))
                    for t in range(NT):
                        for k in range(NC):
                            last = mm(bank[6][:, t * 64:t * 64 + 36], hT[:, k, t * P:(t + 1) * P], rw[:, k, :],
                                      start=k == 0, stop=k == NC - 1)
                    last.then_inc(S("logits_done"), 1)
                up(0)
                if tag[0] == "m":
                    pe.wait_ge(*nth("logits_read", l + 1))
                up(1)
                if tag[0] == "m":
                    pe.wait_ge(*nth("combine_ready", l + 1))
                    for t in range(NT):
                        last = pe.transpose(bank[0][0:32, t * P:(t + 1) * P], rs[:, 0, t * 32:(t + 1) * 32], ident)
                    last.then_inc(S("combine_turned"), 1)
                    pe.wait_ge(*nth("combine_rows_ready", l + 1))
                down(0, start=True)
                up(2)
                down(1)
                up(3)
                with pe.Fori(1, count // 2 - 1) as i:
                    down(0, i)
                    up(2, i)
                    down(1, i)
                    up(3, i)
                down(count - count % 2 - 2)
                if count % 2:
                    up(count - 1)
                down(count - count % 2 - 1)
                if count % 2:
                    down(count - 1)

            pe.wait_ge(*nth("rowc_landed", 16))
            pe.wait_ge(*nth("const_landed", 16))
            pe.transpose(bank[6][:, 0:NC], rows[0:NC, 2, :], ident[0:NC, 0:NC]).then_inc(S("c_turned"), 1)
            pe.wait_ge(*nth("rows_landed", 8 * 16))
            columns(0, 2, "cols_turned")
            modulation(0)
            transposes("a0", xn, "a0_xn")
            hT_ready("a0")
            for j in range(12):
                project("a0", j, N_IN["a0"] + j)
            pe.wait_ge(*nth("a0_roped", 1))
            head_transposes("a0", [(z, P * i) for i in range(16)])
            pe.wait_ge(*nth("a0_qk", 8))
            attend("a0")
            pe.wait_ge(*nth("sub_sq", 1))
            for b in range(4):
                last = mm(bank[b][:, :], ones, xn[:, b // 2, (b % 2) * 512:(b % 2) * 512 + 512])
            last.then_inc(S("sub_sum"), 1)
            pe.wait_ge(*nth("a0_oT", 1))
            project_out("a0")
            transposes("m0", xn, "m0_xn")
            hT_ready("m0")
            experts("m0")
            pe.wait_ge(*nth("m0_x_done", 1))
            modulation(1)
            transposes("a1", xn, "a1_xn")
            hT_ready("a1")
            for j in range(4):
                project("a1", j, N_IN["a1"] + j)
            project("a1", 4, N_IN["a1"] + 8)
            pe.wait_ge(*nth("a1_z", 4))
            for v in range(2):
                for g_ in range(2):
                    for tp in range(2):
                        for t in range(NT):
                            c = 1024 + v * 128 + g_ * 64
                            at = (v * 2 + g_) * 128 + t * 64
                            last = mm(bank[0][64 * tp:64 * tp + 64, at:at + 64], z[:, t, c:c + 64],
                                      cst[:, C_EVEN + 64 * tp:C_EVEN + 64 * tp + 64])
            last.then_inc(S("cmp_split"), 1)
            project("a1", 5, N_IN["a1"] + 9)
            for v in range(2):
                pe.wait_ge(*nth("blk_ready", v + 1))
                for half in range(2):
                    landed(pe, N_CMP + 2 * v + half)
                for c in range(2):
                    for j in range(16):
                        W = slot(N_CMP + 2 * v + j // 8).rearrange("p (k n) -> p k n", k=8)
                        last = mm(bank[1 + 2 * v][:, c * 32:c * 32 + 30],
                                  W[:, j % 8, c * P:(c + 1) * P], blk[:, v, j, :],
                                  start=j == 0, stop=j == 15)
                last.then_inc(S("a1_hidden_done"), 1)
            project("a1", 6, N_IN["a1"] + 10)
            pe.wait_ge(*nth("hid_ready", 1))
            pe.wait_ge(*nth("cmpw_landed", 48))
            for c in range(2):
                mm(bank[2][:, 0:30], cw2[:, c, 0:128], hid[:, 0, c, :], start=c == 0, stop=c == 1)
            for g_ in range(2):
                for c in range(2):
                    last = mm(bank[2][0:15, 64 + 64 * g_:128 + 64 * g_], hid[:, 1, c, 15 * g_:15 * g_ + 15],
                              cw2[:, c, 128:192], start=c == 0, stop=c == 1)
            last.then_inc(S("cmp_kv"), 1)
            project("a1", 7, N_IN["a1"] + 11)
            pe.wait_ge(*nth("cmp_kv_read", 1))
            for g_ in range(2):
                last = mm(bank[3][:, g_ * 64:g_ * 64 + 64], cst[0:15, C_REP:C_REP + P], vc[0:15, g_, :])
            last.then_inc(S("vc_spread"), 1)
            pe.wait_ge(*nth("a1_roped", 2))
            pe.wait_ge(*nth("vblk_ready", 1))
            kd_ = kd.rearrange("p t a n -> p t (a n)")
            head_transposes("a1", [(z, P * i) for i in range(8)] + [(kd_, P * i) for i in range(4)])
            pe.wait_ge(*nth("a1_qk", 6))
            pe.wait_ge(*nth("a1_z", 8))
            for t in range(NT):
                for h in range(16):
                    r = slice(64 * (h % 2), 64 * (h % 2) + 64)
                    at = (t * 8 + h // 2) * 16
                    last = mm(bank[4 + h % 2][:, at:at + CMP_N], qkT[r, h // 2, t * P:(t + 1) * P],
                              kcT[r, 15 * (h // 8):15 * (h // 8) + 15])
            last.then_inc(S("cmp_scores"), 1)
            pe.wait_ge(*nth("pc_ready", 1))
            for g_ in range(2):
                for t in range(NT):
                    last = pe.transpose(bank[5][:, g_ * 256 + t * P:g_ * 256 + t * P + P],
                                        pc[:, t, 8 * g_:8 * g_ + 8, :].rearrange("p h n -> p (h n)"), ident)
            last.then_inc(S("pc_turned"), 1)
            pe.wait_ge(*nth("cmp_ready", 1))
            attend("a1")
            pe.wait_ge(*nth("a1_o", 8))
            project_out("a1")
            transposes("m1", xn, "m1_xn")
            hT_ready("m1")
            experts("m1")
            for l in range(2):
                tag, ffn = f"s{l}", f"f{l}"
                transposes(tag, x, "first_tile" if l == 0 else "ln2_0_tile")
                hT_ready(tag)
                for j in range(10):
                    project(tag, j, N_IN[tag] + j)
                pe.wait_ge(*nth("mix_landed", 5 * 16 * (l + 1)))
                for g_ in range(4):
                    last = pe.transpose(bank[3][:, g_ * P:(g_ + 1) * P], sgw[:, g_, :], ident)
                last.then_inc(S("sgw_turned"), 1)
                pe.wait_ge(*nth("conv_landed", 4 * 16 * (l + 1)))
                for w in range(4):
                    last = pe.transpose(bank[2][:, w * 44:w * 44 + 44], cvrow[0:44, w, :], ident[0:44, 0:44])
                last.then_inc(S("conv_turned"), 1)
                pe.wait_ge(*nth("logf_ready", l + 1))
                mm(bank[1][0:4, 0:SEQ], fox[:, 3, 0:4], cst[:, C_TRI:C_TRI + SEQ], stop=False)
                mm(bank[1][0:4, P:SEQ], fox[:, 3, 4:8], tri, start=False).then_inc(S("cum_done"), 1)
                pe.wait_ge(*nth(f"{tag}_z", 10))
                for g_ in range(4):
                    o = bank[0][64 * (g_ % 2):64 * (g_ % 2) + 64, (g_ // 2) * SEQ:(g_ // 2 + 1) * SEQ]
                    for t in range(NT):
                        at = C_BAND + (t * 4 + g_) * SEQ
                        last = mm(o[:, t * P:SEQ], z[:, t, 2052 + 64 * g_:2116 + 64 * g_],
                                  cst[:, at + t * P:at + SEQ], start=t == 0, stop=t == 1)
                last.then_inc(S("pooled"), 1)
                pe.wait_ge(*nth("pool_ready", l + 1))
                for g_ in range(4):
                    r = slice(64 * (g_ % 2), 64 * (g_ % 2) + 64)
                    last = mm(bank[0][r, (g_ // 2) * SEQ:(g_ // 2 + 1) * SEQ], pw[r, g_ // 2, :],
                              pool[r, g_ // 2, :])
                last.then_inc(S("pool_mixed"), 1)
                pe.wait_ge(*nth("sgv_ready", l + 1))
                for t in range(NT):
                    for g_ in range(4):
                        at = t * SEQ + g_ * 64
                        last = mm(bank[4][:, at:at + 64], sgwT[:, g_, :], z[:, t, 1796 + 64 * g_:1860 + 64 * g_])
                last.then_inc(S("sg_mixed"), 1)
                pe.wait_ge(*nth("sgy_ready", l + 1))
                for c in range(2):
                    for t in range(NT):
                        last = pe.transpose(bank[5][:, c * SEQ + t * P:c * SEQ + t * P + P],
                                            sgt[:, t, c * P:(c + 1) * P], ident)
                last.then_inc(S("sg_turned"), 1)
                pe.wait_ge(*nth(f"{tag}_roped", 1))
                pe.wait_ge(*nth("mix_read", l + 1))
                head_transposes(tag, [(z, c) for c in (0, 128, 256, 384, 768, 896, 1024, 1152)])
                pe.wait_ge(*nth(f"{tag}_qk", 4))
                attend(tag)
                pe.wait_ge(*nth(f"{tag}_o", 4))
                project_out(tag)
                transposes(ffn, x, f"ln1_{l}_tile")
                hT_ready(ffn)
                experts(ffn)

        @block.scalar
        def _(act):
            ch = Chain(act, "act_chain")

            def norm(tag):
                for t in range(NT):
                    ch(act.activation(xn[:, t, :], x[:, t, :], ACT.Square, accum_out=sm[:, t:t + 1]))
                ch.sync()
                act.activation(sm[:, 6:8], sm[:, 0:2], ACT.Copy).then_inc(S(f"{tag}_ssq"), 1)
                root(tag)

            def root(tag, at=2, n=2):
                act.wait_ge(*nth(f"{tag}_var", 1))
                act.activation(sm[:, at + n:at + 2 * n], sm[:, at:at + n], ACT.Sqrt).then_inc(S(f"{tag}_rstd"), 1)

            def hT_copy(tag, scale=None, bias=None):
                for c in (0, 1, 4, 5):
                    act.wait_ge(*nth(f"{tag}_xT", c // 2 + 1))
                    kw = {} if scale is None else dict(scale=scale[:, c:c + 1], bias=bias[:, c:c + 1])
                    f = ACT.Copy if scale is None else ACT.Identity
                    act.activation(hT[:, c, :], pair(4 + c // 2)[:, c % 2, :], f, **kw)\
                       .then_inc(S(f"{tag}_hT_act"), 1)

            def z_copy(tag, j):
                c, w = COLS[tag][j]
                act.wait_ge(*nth(f"{tag}_in_done", j + 1))
                act.activation(z[:, :, c:c + w], pair(4 + j % 4)[:, :, 0:w], ACT.Copy).then_inc(S(f"{tag}_z"), 1)

            def qk_copy(tag, n, queries):
                for i in range(n):
                    act.wait_ge(*nth(f"{tag}_qkT", i + 1))
                    q = queries[i]
                    dst = (qkT[:, 2 * i:2 * i + 2, :] if tag != "a1" or i < 4
                           else kdT[:, 2 * i - 8:2 * i - 6, :])
                    act.activation(dst, pair(i % 4)[:, :, :], ACT.Copy, scale=0.125 if q else 1.0)\
                       .then_inc(S(f"{tag}_qk"), 1)

            def attend(tag):
                jobs, units, ends = attention(tag)
                unit_of = {j: n for n, u in enumerate(units) for j in u["jobs"]}
                for j in range(len(jobs) + 3):
                    if j < len(jobs):
                        act.wait_ge(*nth(f"{tag}_max", j + 1))
                        if j >= 4:
                            act.wait_ge(*nth(f"{tag}_turned", unit_of[j - 4] + 1))
                        ch(act.activation(prob[:, j % 4, 0:P], bank[j % 4][:, 0:P], ACT.Exp,
                                          bias=nmax[:, j % 4, 0:1], accum_out=psum_[:, j % 4, 0:1]))
                        act.activation(prob[:, j % 4, P:384], bank[j % 4][:, P:384], ACT.Exp,
                                       bias=nmax[:, j % 4, 1:2], accum_out=psum_[:, j % 4, 1:2])\
                           .then_inc(S(f"{tag}_exp"), 1)
                    if j - 2 in ends:
                        u = ends[j - 2]
                        act.wait_ge(*nth(f"{tag}_turned", u + 1))
                        if u >= 2:
                            act.wait_ge(*nth(f"{tag}_pv", u - 1))
                        act.activation(probT[:, u % 2, :], bank[4 + u % 2][:, 0:384], ACT.Copy)\
                           .then_inc(S(f"{tag}_probT"), 1)

            def experts_m(tag):
                count = COUNT[tag]

                def silu(e, i=0, wait=True):
                    act.wait_ge(*nth(f"{tag}_up_done", i * 2 + e + 1))
                    if wait:
                        act.wait_ge(*nth(f"{tag}_aT", i * 2 + e - 1))
                    act.activation(sil[:, e % 2, :], bank[4 + 2 * (e % 2)][:, :], ACT.Silu)\
                       .then_inc(S(f"{tag}_silu"), 1)

                silu(0, wait=False)
                silu(1, wait=False)
                with act.Fori(1, count // 2) as i:
                    silu(0, i)
                    silu(1, i)

            def experts_f(tag):
                count = COUNT[tag]

                def conv(e, i=0, wait=True):
                    act.wait_ge(*nth(f"{tag}_up_done", i * 2 + e + 1))
                    act.wait_ge(*nth(f"{tag}_taps", i * 2 + e + 1))
                    if wait:
                        act.wait_ge(*nth(f"{tag}_aT", i * 2 + e - 1))
                    for c in range(4):
                        act.activation(cvt[:, e % 2, c, :], pair(4 + 2 * (e % 2) + c // 2)[:, c % 2, :], ACT.Identity,
                                       scale=cvcur[:, e % 2, 2, c:c + 1], bias=cvcur[:, e % 2, 3, c:c + 1])\
                           .then_inc(S(f"{tag}_tap2"), 1)
                    act.wait_ge(*nth(f"{tag}_conv", i * 2 + e + 1))
                    act.activation(sil[:, e % 2, :], cvt[:, e % 2, 0:2, :].rearrange("p c n -> p (c n)"), ACT.Silu)\
                       .then_inc(S(f"{tag}_silu"), 1)

                conv(0, wait=False)
                conv(1, wait=False)
                with act.Fori(1, count // 2) as i:
                    conv(0, i)
                    conv(1, i)
                conv(count - 1)

            act.wait_ge(*nth("c_turned", 1))
            act.activation(csil[:, :], bank[6][:, 0:NC], ACT.Silu).then_inc(S("csil_ready"), 1)
            act.wait_ge(*nth("lam_dots", 1))
            act.activation(sm[:, 12:14], sm[:, 10:12], ACT.Exp).then_inc(S("lam_exp"), 1)
            act.wait_ge(*nth("angles", 1))
            act.activation(rope[:, 0:2, :], rope[:, 2:4, :], ACT.Sin).then_inc(S("rope_ready"), 1)
            act.wait_ge(*nth("x_landed", 16))
            norm("a0")
            act.wait_ge(*nth("mod_done", 1))
            hT_copy("a0", ng[:, 0, :], modc[:, 0:8])
            for j in range(12):
                z_copy("a0", j)
            qk_copy("a0", 8, [True] * 4 + [False] * 4)
            attend("a0")
            act.wait_ge(*nth("sub_var", 1))
            act.activation(xn[:, :, :], xn[:, :, :], ACT.Sqrt).then_inc(S("sub_rstd"), 1)
            act.wait_ge(*nth("a0_x_done", 1))
            norm("m0")
            hT_copy("m0", ng[:, 1, :], modc[:, 24:32])

            def route(l):
                act.wait_ge(*nth("route_diff", l + 1))
                act.activation(rs[:, 6, 0:8], rs[:, 5, 0:8], ACT.Exp).then_inc(S("route_exp"), 1)
                act.activation(rs[:, 6, 8:10], rs[:, 5, 8:10], ACT.Exp).then_inc(S("route_exp"), 1)

            route(0)
            experts_m("m0")
            act.wait_ge(*nth("m0_x_done", 1))
            norm("a1")
            act.wait_ge(*nth("mod_done", 2))
            hT_copy("a1", ng[:, 0, :], modc[:, 0:8])
            for j in range(4):
                z_copy("a1", j)
            act.wait_ge(*nth("a1_z", 4))
            act.activation(gate[:, :, :], z[:, :, 1792:1840], ACT.Exp, scale=-1.0).then_inc(S("gate_exp"), 1)
            z_copy("a1", 4)
            z_copy("a1", 5)
            for v in range(2):
                act.wait_ge(*nth("a1_hidden_done", v + 1))
                for c in range(2):
                    at = R_B1 + 2 * v + c
                    last = act.activation(hid[:, v, c, :], bank[1 + 2 * v][:, c * 32:c * 32 + 30],
                                          ACT.Gelu_apprx_tanh, bias=colA[:, at:at + 1])
                    if (v, c) != (1, 1):
                        ch(last)
            last.then_inc(S("hid_ready"), 1)
            z_copy("a1", 6)
            z_copy("a1", 7)
            qk_copy("a1", 6, [True] * 4 + [False] * 2)
            act.wait_ge(*nth("pc_diff", 1))
            act.activation(pc[:, :, :, 0:CMP_N], pc[:, :, :, 0:CMP_N], ACT.Exp).then_inc(S("pc_exp"), 1)
            act.wait_ge(*nth("pc_turned", 1))
            act.activation(pcT[:, :, :], pair(5)[:, :, :], ACT.Copy).then_inc(S("cmp_ready"), 1)
            act.wait_ge(*nth("cmp_ready", 1))
            act.activation(sm[:, 20:21], sm[:, 0:1], ACT.Copy).then_inc(S("cmp_ready"), 1)
            attend("a1")
            act.wait_ge(*nth("a1_x_done", 1))
            norm("m1")
            hT_copy("m1", ng[:, 1, :], modc[:, 24:32])
            route(1)
            experts_m("m1")
            act.wait_ge(*nth("m1_x_done", 1))
            norm("first")
            for l in range(2):
                tag, ffn = f"s{l}", f"f{l}"
                hT_copy(tag)
                for j in range(10):
                    z_copy(tag, j)
                act.wait_ge(*nth("absf", l + 1))
                ch(act.activation(fox[:, 1, :], fox[:, 1, :], ACT.Exp, scale=-1.0))
                ch.sync()
                act.activation(fox[:, 2, :], fox[:, 1, :], ACT.Ln, bias=1.0).then_inc(S("ln1p"), 1)
                act.wait_ge(*nth(f"{tag}_z", 10))
                act.activation(z[:, :, 1796:2052], z[:, :, 1796:2052], ACT.Gelu).then_inc(S("gelu"), 1)
                act.activation(z[:, :, 1540:1796], z[:, :, 1540:1796], ACT.Gelu).then_inc(S("gelu"), 1)
                act.wait_ge(*nth("sg_var", l + 1))
                act.activation(sm[:, 40:48], sm[:, 32:40], ACT.Sqrt).then_inc(S("sg_rstd"), 1)
                qk_copy(tag, 4, [True, False, True, False])
                attend(tag)
                root(f"ln1_{l}")
                hT_copy(ffn)
                experts_f(ffn)
                root(f"ln2_{l}")

        @block.vector
        def _(dve):
            ch = Chain(dve, "dve_chain")
            TT, TS, STT = dve.tensor_tensor, dve.tensor_scalar, dve.scalar_tensor_tensor

            def ts(o, a, s1, op0, s2=None, op1=None):
                if op1 is None:
                    return TS(out=o, in0=a, scalar1=s1, scalar2=None, op0=op0)
                return TS(out=o, in0=a, scalar1=s1, scalar2=s2, op0=op0, op1=op1)

            def stt(o, a, s, b, op0, op1):
                return STT(out=o, in0=a, scalar=s, in1=b, op0=op0, op1=op1)

            def norm(tag):
                dve.wait_ge(*nth(f"{tag}_ssq", 1))
                ch(ts(sm[:, 2:4], sm[:, 6:8], 1.0 / D, ALU.mult, ROT_EPS, ALU.add))
                ch.sync()
                dve.reciprocal(sm[:, 2:4], sm[:, 2:4]).then_inc(S(f"{tag}_var"), 1)
                dve.wait_ge(*nth(f"{tag}_rstd", 1))

            def norm_x(tag):
                norm(tag)
                for t in range(NT):
                    ts(xn[:, t, :], x[:, t, :], sm[:, 4 + t:5 + t], ALU.mult).then_inc(S(f"{tag}_xn"), 1)

            def hT_copy(tag, scale=None, bias=None):
                for c in (2, 3, 6, 7):
                    dve.wait_ge(*nth(f"{tag}_xT", c // 2 + 1))
                    src = pair(4 + c // 2)[:, c % 2, :]
                    if scale is None:
                        ins = dve.tensor_copy(hT[:, c, :], src)
                    else:
                        ins = ts(hT[:, c, :], src, scale[:, c:c + 1], ALU.mult,
                                 bias[:, c:c + 1], ALU.add)
                    ins.then_inc(S(f"{tag}_hT_dve"), 1)

            def modulation(l):
                bias = colA[:, 0:48] if l == 0 else colB[:, 0:48]
                dve.wait_ge(*nth("modc_ready", l + 1))
                ch(TT(modc[:, 0:16], bank[7][:, 0:16], bias[:, 0:16], ALU.add))
                TT(modc[:, 24:40], bank[7][:, 24:40], bias[:, 24:40], ALU.add).then_inc(S("modc_read"), 1)
                ch.sync()
                dve.wait_ge(*nth("modc_read", l + 1))
                for s_ in range(2):
                    at = R_NG + (2 * l + s_) * NC
                    ch(stt(ng[:, s_, :], modc[:, 24 * s_ + 8:24 * s_ + 16], 1.0, colA[:, at:at + NC],
                           ALU.add, ALU.mult))
                dve.wait_ge(*nth("modg_ready", l + 1))
                dve.wait_ge(*nth("gbc_landed", 32 * (l + 1)))
                for n in range(2):
                    for h in range(2):
                        v = gbc[:, n, h * 512:(h + 1) * 512]
                        ins = TT(v, v, bank[2 * n + h][:, :], ALU.add)
                        if n * h == 0:
                            ch(ins)
                ins.then_inc(S("mod_done"), 1)

            def rotate(tag, spans, tables):
                for c, nh in spans:
                    for t in range(NT):
                        hv = z[:, t, c:c + 64 * nh].rearrange("p (h d) -> p h d", d=64)
                        x1, x2 = hv[:, :, 0:ROT], hv[:, :, ROT:2 * ROT]
                        co, si = (v[:, t, :].unsqueeze(1).broadcast_to([P, nh, ROT]) for v in tables)
                        tmp = [rt[:, k, 0:8 * nh].rearrange("p (h d) -> p h d", d=ROT) for k in range(4)]
                        ch.sync()
                        ch(TT(tmp[0], x1, co, ALU.mult))
                        ch(TT(tmp[1], x2, si, ALU.mult))
                        ch(TT(tmp[2], x2, co, ALU.mult))
                        ch(TT(tmp[3], x1, si, ALU.mult))
                        ch.sync()
                        ch(TT(x1, tmp[0], tmp[1], ALU.subtract))
                        ch(TT(x2, tmp[2], tmp[3], ALU.add))
                ch.sync()
                dve.tensor_copy(sm[:, 62:63], sm[:, 4:5]).then_inc(S(f"{tag}_roped"), 1)

            def attend(tag):
                jobs, units, ends = attention(tag)
                J = len(jobs)
                for j in range(J + 5):
                    if j < J:
                        dve.wait_ge(*nth(f"{tag}_scores", j + 1))
                        ch(dve.tensor_reduce(out=nmax[:, j % 4, 0:1], in_=bank[j % 4][:, 0:P], axis=X,
                                             op=ALU.max, negate=True))
                        dve.tensor_reduce(out=nmax[:, j % 4, 1:2], in_=bank[j % 4][:, P:384], axis=X,
                                          op=ALU.max, negate=True).then_inc(S(f"{tag}_max"), 1)
                    if j - 1 in ends:
                        U = units[ends[j - 1]]
                        dve.wait_ge(*nth(f"{tag}_exp", j))
                        for jj in U["jobs"]:
                            ch(dve.reciprocal(rsum[:, jj % 4, :], psum_[:, jj % 4, :]))
                        ch.sync()
                        b0 = U["jobs"][0] % 4
                        if tag == "a0":
                            b1 = U["jobs"][1] % 4
                            ch(ts(rsum[:, b1, :], rsum[:, b1, :], sm[:, 14:15], ALU.mult))
                        if tag == "a1":
                            gv = gate[:, :, 3 * U["h"] + 1 + U["w"]:3 * U["h"] + 2 + U["w"]]
                            ch(TT(rsum[:, b0, :], rsum[:, b0, :], gv.rearrange("p t o -> p (t o)"), ALU.mult))
                            ch.sync()
                        for t, (a, b) in enumerate(((0, P), (P, 384))):
                            ins = ts(prob[:, b0, a:b], prob[:, b0, a:b], rsum[:, b0, t:t + 1], ALU.mult)
                            if tag == "a0" or t == 0:
                                ch(ins)
                        if tag == "a0":
                            ch.sync()
                            for t, (a, b) in enumerate(((0, P), (P, 384))):
                                ins = stt(prob[:, b0, a:b], prob[:, b1, a:b], rsum[:, b1, t:t + 1],
                                          prob[:, b0, a:b], ALU.mult, ALU.add)
                                if t == 0:
                                    ch(ins)
                        ins.then_inc(S(f"{tag}_norm"), 1)
                    if j - 4 in ends and units[ends[j - 4]]["last"]:
                        u = ends[j - 4]
                        G = units[u]["group"]
                        dve.wait_ge(*nth(f"{tag}_pv", u + 1))
                        dve.tensor_copy(oT[:, G, :], bank[6 + G % 2][:, 0:SEQ]).then_inc(S(f"{tag}_o"), 1)

            def gated_residual(tag, n):
                for j in range(4):
                    dve.wait_ge(*nth(f"{tag}_out_done", j + 1))
                    gv = gbc[:, n, 256 * j:256 * j + 256].unsqueeze(1).broadcast_to([P, NT, 256])
                    ch(TT(xn[:, :, 256 * j:256 * j + 256], pair(4 + j)[:, :, :], gv, ALU.mult))
                    ch.sync()
                    ins = TT(x[:, :, 256 * j:256 * j + 256], x[:, :, 256 * j:256 * j + 256],
                             xn[:, :, 256 * j:256 * j + 256], ALU.add)
                    if j < 3:
                        ch(ins)
                ins.then_inc(S(f"{tag}_x_done"), 1)
                dve.wait_ge(*nth(f"{tag}_x_done", 1))

            def route(l):
                dve.wait_ge(*nth("logits_done", l + 1))
                dve.wait_ge(*nth("router_landed", 7 * 16 * (l + 1)))
                lv = bank[6][:, 0:128].rearrange("p (t n) -> p t n", t=NT)[:, :, 0:36]
                TT(lg[:, :, :], lv, rb[:, :].unsqueeze(1).broadcast_to([P, NT, 36]), ALU.add)\
                    .then_inc(S("logits_read"), 1)
                dve.wait_ge(*nth("logits_read", l + 1))

                def R(k, n):
                    return rs[:, k, 0:NT * n].rearrange("p (t n) -> p t n", t=NT)

                def col(k, at=0):
                    return rs[:, k, at:at + NT].rearrange("p (t o) -> p t o", o=1)

                def step(ins):
                    ch(ins)
                    ch.sync()

                def first_max(o, v, n, rev, sc, m, r):
                    step(dve.tensor_reduce(out=m, in_=v, axis=X, op=ALU.max))
                    step(TT(sc, v, m.broadcast_to([P, NT, n]), ALU.is_ge))
                    step(TT(sc, sc, cst[:, rev:rev + n].unsqueeze(1).broadcast_to([P, NT, n]), ALU.mult))
                    step(dve.tensor_reduce(out=r, in_=sc, axis=X, op=ALU.max))
                    step(TT(o, sc, r.broadcast_to([P, NT, n]), ALU.is_equal))

                lgrp, lexp = lg[:, :, 0:4], lg[:, :, 4:36]
                first_max(R(1, 4), lgrp, 4, C_R4, R(2, 4), col(9, 0), col(9, 2))
                step(TT(R(5, 4), lgrp, col(9, 0).broadcast_to([P, NT, 4]), ALU.subtract))
                oh = rs[:, 1, 0:8].rearrange("p (t g o) -> p t g o", t=NT, o=1).broadcast_to([P, NT, 4, 8])
                ohx = rs[:, 2, 0:64].rearrange("p (t g o) -> p t g o", t=NT, g=4)
                step(dve.tensor_copy(ohx, oh))
                step(TT(R(3, 32), lexp, R(2, 32), ALU.mult))
                step(ts(R(2, 32), R(2, 32), 1.0, ALU.subtract, -NEG, ALU.mult))
                step(TT(R(3, 32), R(3, 32), R(2, 32), ALU.add))
                first_max(R(4, 32), R(3, 32), 32, C_R32, R(7, 32), col(9, 4), col(9, 6))
                step(stt(R(3, 32), R(4, 32), 3.0 * NEG, R(3, 32), ALU.mult, ALU.add))
                first_max(R(8, 32), R(3, 32), 32, C_R32, R(7, 32), col(9, 8), col(9, 10))
                TT(rs[:, 5, 8:10], rs[:, 9, 8:10], rs[:, 9, 4:6], ALU.subtract).then_inc(S("route_diff"), 1)
                dve.wait_ge(*nth("route_exp", 2 * (l + 1)))
                step(dve.tensor_reduce(out=col(9, 12), in_=rs[:, 6, 0:8].rearrange("p (t n) -> p t n", t=NT),
                                       axis=X, op=ALU.add))
                step(stt(rs[:, 9, 14:16], rs[:, 6, 8:10], 1.0, rs[:, 9, 12:14], ALU.add, ALU.mult))
                step(dve.reciprocal(rs[:, 9, 16:18], rs[:, 9, 14:16]))
                step(TT(rs[:, 9, 18:20], rs[:, 9, 16:18], rs[:, 6, 8:10], ALU.mult))
                step(TT(R(4, 32), R(4, 32), col(9, 16).broadcast_to([P, NT, 32]), ALU.mult))
                step(TT(R(8, 32), R(8, 32), col(9, 18).broadcast_to([P, NT, 32]), ALU.mult))
                TT(R(0, 32), R(4, 32), R(8, 32), ALU.add).then_inc(S("combine_ready"), 1)
                dve.wait_ge(*nth("combine_turned", l + 1))
                if l:
                    dve.wait_ge(*nth("combine_stored", 16 * l))
                dve.tensor_copy(cbT[:, :], bank[0][0:32, 0:SEQ]).then_inc(S("combine_rows_ready"), 1)

            def experts_m(tag):
                l, count = int(tag[1]), COUNT[tag]

                def expert(e, i=0, wait=True):
                    dve.wait_ge(*nth(f"{tag}_up_done", i * 2 + e + 1))
                    row = cmb[:, ds(i * 2 + e, 1), :].broadcast_to([P, 2, SEQ])
                    TT(upc[:, e % 2, :].rearrange("p (c n) -> p c n", c=2), pair(5 + 2 * (e % 2))[:, :, :], row,
                       ALU.mult).then_inc(S(f"{tag}_upc"), 1)
                    dve.wait_ge(*nth(f"{tag}_upc", i * 2 + e + 1))
                    dve.wait_ge(*nth(f"{tag}_silu", i * 2 + e + 1))
                    if wait:
                        dve.wait_ge(*nth(f"{tag}_down_done", i * 2 + e - 1))
                    TT(aT[:, e % 2, :], sil[:, e % 2, :], upc[:, e % 2, :], ALU.mult).then_inc(S(f"{tag}_aT"), 1)

                def ada1(i, u, wait=True):
                    dve.wait_ge(*nth(f"ada1_landed{u}", i * 16 + 16))
                    for k in range(4):
                        c = csil[:, 4 * u + k:4 * u + k + 1]
                        if k or u:
                            dve.wait_ge(*nth("ada1_step", i * 7 + (4 * u + k)))
                        if u == 1 and k == 3:
                            o, sem = acc[:, ds(i * 384, 384)], "ada1_done"
                        else:
                            o, sem = adat[:, :], "ada1_step"
                        if k == 0 and u == 0:
                            ins = ts(o, adaw[:, u, k, :], c, ALU.mult)
                        else:
                            ins = stt(o, adaw[:, u, k, :], c, adat[:, :], ALU.mult, ALU.add)
                        ins.then_inc(S(sem), 1)
                    dve.tensor_copy(sm[:, 50 + u:51 + u], adaw[:, u, 3, 0:1]).then_inc(S(f"ada1_used{u}"), 1)

                dve.wait_ge(*nth("combine_landed", 16 * (l + 1)))
                for e in range(2):
                    expert(e, wait=False)
                    if l == 0:
                        ada1(0, e)
                with dve.Fori(1, count // 2) as i:
                    for e in range(2):
                        expert(e, i)
                        if l == 0:
                            ada1(i, e)
                for t in range(NT):
                    for h in range(2):
                        if t + h == 0:
                            dve.wait_ge(*nth(f"{tag}_down_done", count))
                        v = xn[:, t, h * 512:(h + 1) * 512]
                        ch(TT(v, bank[2 * t + h][:, :], gbc[:, 1, h * 512:(h + 1) * 512], ALU.mult))
                ch.sync()
                TT(x[:, :, :], x[:, :, :], xn[:, :, :], ALU.add).then_inc(S(f"{tag}_x_done"), 1)
                dve.wait_ge(*nth(f"{tag}_x_done", 1))

            def experts_f(tag):
                count = COUNT[tag]

                def taps(e, i=0):
                    for half in range(2):
                        src = cvc[:, :, ds(i * 4 + (2 * e + 22 * half), 2)]
                        ins = dve.tensor_copy(cvcur[:, e % 2, :, 2 * half:2 * half + 2], src)
                        ins.then_inc(S(f"{tag}_taps" if half else f"{tag}_taps_gate"), 1)

                def expert(e, i=0, wait=True):
                    taps(e, i)
                    dve.wait_ge(*nth(f"{tag}_taps", i * 2 + e + 1))
                    for tap, sh in ((1, 1), (0, 2)):
                        for c in range(4):
                            src = pair(4 + 2 * (e % 2) + c // 2)[:, c % 2, 0:SEQ - sh]
                            o = cvt[:, e % 2, c, sh:SEQ]
                            if tap == 1:
                                dve.wait_ge(*nth(f"{tag}_tap2", i * 8 + (4 * e + 2 * (c // 2) + 2)))
                            else:
                                dve.wait_ge(*nth(f"{tag}_tap1", i * 8 + (4 * e + c + 1)))
                            ins = stt(o, src, cvcur[:, e % 2, tap, c:c + 1], o, ALU.mult, ALU.add)
                            if tap == 1:
                                ins.then_inc(S(f"{tag}_tap1"), 1)
                            elif c in (1, 3):
                                ins.then_inc(S(f"{tag}_conv" if c == 1 else f"{tag}_conv_value"), 1)
                    dve.wait_ge(*nth(f"{tag}_conv_value", i * 2 + e + 1))
                    dve.wait_ge(*nth(f"{tag}_silu", i * 2 + e + 1))
                    if wait:
                        dve.wait_ge(*nth(f"{tag}_down_done", i * 2 + e - 1))
                    TT(aT[:, e % 2, :], sil[:, e % 2, :], cvt[:, e % 2, 2:4, :].rearrange("p c n -> p (c n)"),
                       ALU.mult).then_inc(S(f"{tag}_aT"), 1)

                expert(0, wait=False)
                expert(1, wait=False)
                with dve.Fori(1, count // 2) as i:
                    expert(0, i)
                    expert(1, i)
                expert(count - 1)
                dve.wait_ge(*nth(f"{tag}_down_done", count))
                for t in range(NT):
                    for h in range(2):
                        v = x[:, t, h * 512:(h + 1) * 512]
                        ch(stt(v, v, ALPHA, bank[2 * t + h][:, :], ALU.mult, ALU.add))
                ch.sync()

            def layer_norm(tag, l):
                name = f"{tag}_{l}"
                for t in range(NT):
                    for h in range(2):
                        ch(dve.bn_stats(out=stat[:, t, h, :], in_=x[:, t, h * 512:(h + 1) * 512]))
                ch.sync()
                for t in range(NT):
                    ch(dve.bn_aggr(out=mv[:, t, :], in_=stat[:, t, :, :]))
                ch.sync()
                ch(ts(sm[:, 2:4], mv[:, :, 1], LN_EPS, ALU.add))
                ch.sync()
                dve.reciprocal(sm[:, 2:4], sm[:, 2:4]).then_inc(S(f"{name}_var"), 1)
                dve.wait_ge(*nth(f"{name}_rstd", 1))
                dve.wait_ge(*nth(f"{tag}{l}_landed", 32))
                for t in range(NT):
                    v = x[:, t, :]
                    ch(ts(v, v, mv[:, t, 0:1], ALU.subtract, sm[:, 4 + t:5 + t], ALU.mult))
                    ch.sync()
                    ch(TT(v, v, gbc[:, 0, :], ALU.mult))
                    ch.sync()
                    TT(v, v, gbc[:, 1, :], ALU.add).then_inc(S(f"{name}_tile"), 1)
                dve.wait_ge(*nth(f"{name}_tile", 2))
                dve.tensor_copy(sm[:, 60:61], sm[:, 4:5]).then_inc(S(f"{name}_done"), 1)

            dve.wait_ge(*nth("lam_landed", 16))
            for n in range(2):
                ch(TT(rt[:, n, 0:64], lamt[:, 2 * n, :], lamt[:, 2 * n + 1, :], ALU.mult))
            ch.sync()
            dve.tensor_reduce(out=sm[:, 10:12], in_=rt[:, 0:2, 0:64], axis=X, op=ALU.add)\
                .then_inc(S("lam_dots"), 1)
            dve.wait_ge(*nth("pos_landed", 32))
            dve.wait_ge(*nth("const_landed", 16))
            ch(dve.tensor_copy(sm[:, 8:10], posi[:, :]))
            ch.sync()

            def step(ins):
                ch(ins)
                ch.sync()

            ang, k_, r_, rc = rope[:, 4, :], rope[:, 5, :], rope[:, 3, :], rope[:, 2, :]
            for t in range(NT):
                step(ts(ang[:, 8 * t:8 * t + 8], cst[:, C_INV:C_INV + 8], sm[:, 8 + t:9 + t], ALU.mult))
            step(ts(k_, ang, 1.0 / (2 * np.pi), ALU.mult, 12582912.0, ALU.add))
            step(ts(k_, k_, 12582912.0, ALU.subtract))
            c1 = 6.28125
            c2 = float(np.floor((2 * np.pi - c1) * 2 ** 21) / 2 ** 21)
            c3 = float(np.float32(2 * np.pi - c1 - c2))
            step(stt(r_, k_, -c1, ang, ALU.mult, ALU.add))
            step(stt(r_, k_, -c2, r_, ALU.mult, ALU.add))
            step(stt(r_, k_, -c3, r_, ALU.mult, ALU.add))
            lim = 3.1415925
            step(ts(rc, r_, float(np.pi / 2), ALU.add))
            step(ts(k_, rc, float(np.pi), ALU.is_gt))
            step(stt(rc, k_, float(-2 * np.pi), rc, ALU.mult, ALU.add))
            ts(rope[:, 2:4, :], rope[:, 2:4, :], lim, ALU.min, -lim, ALU.max).then_inc(S("angles"), 1)
            dve.wait_ge(*nth("lam_exp", 1))
            step(TT(sm[:, 14:15], sm[:, 13:14], sm[:, 12:13], ALU.subtract))
            step(ts(sm[:, 14:15], sm[:, 14:15], LAMBDA_INIT, ALU.subtract))
            dve.wait_ge(*nth("cols_turned", 1))
            ch(dve.tensor_copy(colA[:, :], bank[7][:, 0:R_END]))
            ch(dve.tensor_copy(colB[:, :], bank[7][:, P:P + 80]))
            ch.sync()
            step(ts(colA[:, R_SUB:R_SUB + 1], colA[:, R_SUB:R_SUB + 1], 1.0 - LAMBDA_INIT, ALU.mult))
            dve.wait_ge(*nth("csil_ready", 1))
            for n in range(24):
                k, third = divmod(n, 3)
                landed(dve, n)
                o = acc[:, third * UNIT:(third + 1) * UNIT]
                if k == 0:
                    ins = ts(o, slot(n), csil[:, 0:1], ALU.mult)
                else:
                    dve.wait_ge(*nth("ada0_done", n - 2))
                    ins = stt(o, slot(n), csil[:, k:k + 1], o, ALU.mult, ALU.add)
                ins.then_inc(S("ada0_done"), 1)
            norm_x("a0")
            modulation(0)
            dve.wait_ge(*nth("mod_done", 1))
            hT_copy("a0", ng[:, 0, :], modc[:, 0:8])
            dve.wait_ge(*nth("rope_ready", 1))
            dve.wait_ge(*nth("a0_z", 8))
            tables = [rope[:, n, :].rearrange("p (t d) -> p t d", t=NT) for n in range(2)]
            rotate("a0", [(0, 32)], tables)
            dve.wait_ge(*nth("a0_z", 12))
            attend("a0")
            dve.wait_ge(*nth("a0_o", 8))
            oF = oT[:, :, :].rearrange("p c n -> p (c n)")
            xF = xn[:, :, :].rearrange("p t n -> p (t n)")
            TT(xF, oF, oF, ALU.mult).then_inc(S("sub_sq"), 1)
            dve.wait_ge(*nth("sub_sum", 1))
            for b in range(4):
                ch(ts(xF[:, b * 512:(b + 1) * 512], bank[b][:, :], 1.0 / P, ALU.mult, ROT_EPS, ALU.add))
            ch.sync()
            dve.reciprocal(xF, xF).then_inc(S("sub_var"), 1)
            dve.wait_ge(*nth("sub_rstd", 1))
            stt(oF, oF, colA[:, R_SUB:R_SUB + 1], xF, ALU.mult, ALU.mult).then_inc(S("a0_oT"), 1)
            gated_residual("a0", 0)
            norm_x("m0")
            hT_copy("m0", ng[:, 1, :], modc[:, 24:32])
            route(0)
            experts_m("m0")
            norm_x("a1")
            dve.wait_ge(*nth("ada1_done", 16))
            modulation(1)
            dve.wait_ge(*nth("mod_done", 2))
            hT_copy("a1", ng[:, 0, :], modc[:, 0:8])
            dve.wait_ge(*nth("a1_z", 4))
            rotate("a1", [(1280, 8)], tables)
            for w in range(2):
                for g_ in range(2):
                    src = z[:, :, 1280 + 256 * w + 64 * g_:1344 + 256 * w + 64 * g_]
                    for dup in range(2):
                        ch(dve.tensor_copy(kd[:, :, 2 * w + g_, 64 * dup:64 * dup + 64], src))
            dve.wait_ge(*nth("gate_exp", 1))
            step(ts(gate[:, :, :], gate[:, :, :], 1.0, ALU.add))
            step(dve.reciprocal(gate[:, :, :], gate[:, :, :]))
            dve.wait_ge(*nth("cmp_split", 1))
            for v in range(2):
                for g_ in range(2):
                    xv = bank[0][:, (v * 2 + g_) * 128:(v * 2 + g_) * 128 + 128].rearrange("p (n j) -> p j n", j=8)
                    for jh in range(2):
                        pv = colB[:, 48 + v * 16 + 8 * jh:56 + v * 16 + 8 * jh].unsqueeze(2).broadcast_to([P, 8, 15])
                        ins = TT(blk[:, v, 8 * jh:8 * jh + 8, 15 * g_:15 * g_ + 15], xv[:, :, jh:jh + 15], pv, ALU.add)
                        if (g_, jh) != (1, 1):
                            ch(ins)
                ins.then_inc(S("blk_ready"), 1)
            dve.wait_ge(*nth("cmp_kv", 1))
            ch(dve.tensor_copy(kcT, bank[2][:, 0:30]))
            dve.tensor_copy(vc[0:15, :, :], bank[2][0:15, 64:192].rearrange("p (g d) -> p g d", g=2))\
                .then_inc(S("cmp_kv_read"), 1)
            dve.wait_ge(*nth("vc_spread", 1))
            for g_ in range(2):
                src = bank[3][:, g_ * 64:g_ * 64 + 64].unsqueeze(1).broadcast_to([P, 8, 64])
                msk = cst[:, C_BLK:C_BLK + 8].unsqueeze(2).broadcast_to([P, 8, 64])
                ins = TT(vblk[:, g_, :, :], src, msk, ALU.mult)
                if g_ == 0:
                    ch(ins)
            ins.then_inc(S("vblk_ready"), 1)
            dve.wait_ge(*nth("a1_z", 8))
            rotate("a1", [(0, 16)], tables)
            ch(dve.memset(pc[:, :, :, CMP_N:16], 0.0))
            dve.wait_ge(*nth("cmp_scores", 1))
            pch = pc.rearrange("p t (h a) n -> p t h a n", a=2)
            for par in range(2):
                src = bank[4 + par][:, 0:256].rearrange("p (t h n) -> p t h n", t=NT, h=8)
                for t in range(NT):
                    mk = cst[:, C_CB + CMP_N * t:C_CB + CMP_N * (t + 1)].unsqueeze(1).broadcast_to([P, 8, CMP_N])
                    ch(TT(pch[:, t, :, par, 0:CMP_N], src[:, t, :, 0:CMP_N], mk, ALU.add))
            ch.sync()
            pcm = pc.rearrange("p t h n -> p (t h) n")[:, :, 0:CMP_N]
            step(dve.tensor_reduce(out=cms[:, 0, :], in_=pcm, axis=X, op=ALU.max))
            TT(pcm, pcm, cms[:, 0, :].unsqueeze(2).broadcast_to([P, 32, CMP_N]), ALU.subtract)\
                .then_inc(S("pc_diff"), 1)
            dve.wait_ge(*nth("pc_exp", 1))
            for t in range(NT):
                mk = cst[:, C_C01 + CMP_N * t:C_C01 + CMP_N * (t + 1)].unsqueeze(1).broadcast_to([P, 16, CMP_N])
                ch(TT(pc[:, t, :, 0:CMP_N], pc[:, t, :, 0:CMP_N], mk, ALU.mult))
            ch.sync()
            step(dve.tensor_reduce(out=cms[:, 1, :], in_=pcm, axis=X, op=ALU.add))
            step(ts(cms[:, 1, :], cms[:, 1, :], 1e-30, ALU.max))
            step(dve.reciprocal(cms[:, 2, :], cms[:, 1, :]))
            for t in range(NT):
                gv = gate[:, t, :].rearrange("p (h a) -> p h a", a=3)[:, :, 0]
                ch(TT(cms[:, 3, 16 * t:16 * t + 16], cms[:, 2, 16 * t:16 * t + 16], gv, ALU.mult))
            ch.sync()
            TT(pcm, pcm, cms[:, 3, :].unsqueeze(2).broadcast_to([P, 32, CMP_N]), ALU.mult)\
                .then_inc(S("pc_ready"), 1)
            attend("a1")
            gated_residual("a1", 0)
            norm_x("m1")
            hT_copy("m1", ng[:, 1, :], modc[:, 24:32])
            route(1)
            experts_m("m1")
            norm("first")
            dve.wait_ge(*nth("final_landed", 16))
            for t in range(NT):
                stt(x[:, t, :], x[:, t, :], sm[:, 4 + t:5 + t], gbc[:, 0, :], ALU.mult, ALU.mult)\
                    .then_inc(S("first_tile"), 1)
            dve.wait_ge(*nth("first_tile", 2))
            dve.tensor_copy(sm[:, 61:62], sm[:, 4:5]).then_inc(S("first_done"), 1)
            tables2 = [cst[:, c:c + 16].rearrange("p (t d) -> p t d", t=NT) for c in (C_COS, C_SIN)]
            for l in range(2):
                tag, ffn = f"s{l}", f"f{l}"
                hT_copy(tag)
                dve.wait_ge(*nth(f"{tag}_z", 10))
                dve.wait_ge(*nth("mix_landed", 5 * 16 * (l + 1)))
                step(TT(fox[:, 0, :].rearrange("p (t h) -> p t h", t=NT), z[:, :, 1536:1540],
                        bfor[:, :].unsqueeze(1).broadcast_to([P, NT, 4]), ALU.add))
                stt(fox[:, 1, :], fox[:, 0, :], -1.0, fox[:, 0, :], ALU.mult, ALU.max).then_inc(S("absf"), 1)
                dve.wait_ge(*nth("ln1p", l + 1))
                step(ts(fox[:, 0, :], fox[:, 0, :], 0.0, ALU.min))
                TT(fox[:, 3, :], fox[:, 0, :], fox[:, 2, :], ALU.subtract).then_inc(S("logf_ready"), 1)
                dve.wait_ge(*nth("sgw_turned", l + 1))
                step(TT(sgwT, bank[3][:, :].rearrange("p (g n) -> p g n", g=4),
                        tri.unsqueeze(1).broadcast_to([P, 4, P]), ALU.mult))
                dve.wait_ge(*nth("conv_turned", l + 1))
                step(dve.tensor_copy(cvc, bank[2][:, 0:176].rearrange("p (w n) -> p w n", w=4)))
                dve.wait_ge(*nth("cum_done", l + 1))
                ch(dve.tensor_copy(cum[:, 0, :], bank[1][0:4, 0:SEQ]))
                ch(ts(cum[:, 1, :], bank[1][0:4, 0:SEQ], -1.0, ALU.mult))
                dve.wait_ge(*nth("pooled", l + 1))
                dve.tensor_copy(pool, pair(0)[:, :, :]).then_inc(S("pool_ready"), 1)
                dve.wait_ge(*nth("gelu", 2 * l + 1))
                vv = z[:, :, 1796:2052].rearrange("p t (g c) -> p t g c", g=4)
                sq = sgt.rearrange("p t (g c) -> p t g c", g=4)

                def per(at, n=64):
                    return sm[:, at:at + 8].rearrange("p (t g o) -> p t g o", t=NT, o=1)\
                        .broadcast_to([P, NT, 4, n])

                step(dve.tensor_reduce(out=sm[:, 16:24], in_=vv, axis=X, op=ALU.add))
                step(ts(sm[:, 16:24], sm[:, 16:24], 1.0 / 64, ALU.mult))
                step(TT(vv, vv, per(16), ALU.subtract))
                step(TT(sq, vv, vv, ALU.mult))
                step(dve.tensor_reduce(out=sm[:, 24:32], in_=sq, axis=X, op=ALU.add))
                step(ts(sm[:, 24:32], sm[:, 24:32], 1.0 / 64, ALU.mult, LN_EPS, ALU.add))
                dve.reciprocal(sm[:, 32:40], sm[:, 24:32]).then_inc(S("sg_var"), 1)
                dve.wait_ge(*nth("sg_rstd", l + 1))
                step(TT(vv, vv, per(40), ALU.mult))
                vt = z[:, :, 1796:2052]
                step(TT(vt, vt, sgl[:, 0, :].unsqueeze(1).broadcast_to([P, NT, 256]), ALU.mult))
                TT(vt, vt, sgl[:, 1, :].unsqueeze(1).broadcast_to([P, NT, 256]), ALU.add)\
                    .then_inc(S("sgv_ready"), 1)
                rotate(tag, [(0, 8)], tables2)
                dve.wait_ge(*nth("gelu", 2 * l + 2))
                dve.wait_ge(*nth("sg_mixed", l + 1))
                for g_ in range(4):
                    at = R_SB + 4 * l + g_
                    c = slice(64 * g_, 64 * g_ + 64)
                    ins = stt(sgt[:, :, c], pair(4)[:, :, c], colA[:, at:at + 1],
                              z[:, :, 1540 + 64 * g_:1604 + 64 * g_], ALU.add, ALU.mult)
                    if g_ < 3:
                        ch(ins)
                ins.then_inc(S("sgy_ready"), 1)
                dve.wait_ge(*nth("pool_mixed", l + 1))
                for c in range(2):
                    at = R_PS + 2 * l + c
                    ch(ts(oT[:, 6 + c, :], pair(0)[:, c, :], colA[:, at:at + 1], ALU.mult))
                dve.wait_ge(*nth("sg_turned", l + 1))
                dve.tensor_copy(oT[:, 4:6, :], pair(5)[:, :, :]).then_inc(S("mix_read"), 1)
                attend(tag)
                for j in range(4):
                    dve.wait_ge(*nth(f"{tag}_out_done", j + 1))
                    v = x[:, :, 256 * j:256 * j + 256]
                    ch(stt(v, v, ALPHA, pair(4 + j)[:, :, :], ALU.mult, ALU.add))
                ch.sync()
                layer_norm("ln1", l)
                hT_copy(ffn)
                experts_f(ffn)
                layer_norm("ln2", l)


_UNUSED = ()


def kernel(**inputs):
    import concourse.bacc as _bacc
    from concourse.bass_utils import run_bass_kernel_spmd as _run

    nc = _bacc.Bacc("TRN2", target_bir_lowering=False, num_devices=1)
    arrays, aps = {}, {}
    inputs = dict(inputs)
    for name, a in inputs.items():
        a = np.ascontiguousarray(a)
        arrays[f"in_{name}"] = a
        aps[name] = nc.dram_tensor(f"in_{name}", a.shape, mybir.dt.from_np(a.dtype), kind="ExternalInput").ap()
    c = constants()
    arrays["in_consts"] = c
    aps["consts"] = nc.dram_tensor("in_consts", c.shape, mybir.dt.float32, kind="ExternalInput").ap()
    out = nc.dram_tensor("out_x", (1, SEQ, D), mybir.dt.float32, kind="ExternalOutput").ap()
    build(nc, aps, out)
    r = _run(nc, [arrays], core_ids=[0])
    return r.results[0]["out_x"]
```

```python
from contextlib import ExitStack

import numpy as np
import concourse.bass as bass
from concourse import mybir

SEQ, D, P = 256, 1024, 128
NT, NC = SEQ // P, D // P
ROT = 8
EXPERTS, GROUPS, PER_GROUP, HID = 32, 4, 8, 256
FF = 2816
FF_GROUPS = FF // HID
NSA_IN, IN2 = 1840, 2308
CMP_N = 15
ROT_EPS, LN_EPS = 1e-6, 1e-5
ALPHA = 4.0 ** 0.25
LAMBDA_INIT = 0.2
NEG = -1e30
SLOTS, UNIT = 3, 2048
HALF = UNIT // 2

C_ID, C_TRI, C_ONE, C_MASK, C_EVEN = 0, 128, 256, 384, 512
C_CB, C_C01, C_R4, C_R32, C_INV = 640, 670, 700, 704, 736
C_COS, C_SIN, C_REP, C_BLK, C_BAND, C_END = 744, 760, 776, 904, 912, 2960
R_ADAB, R_NG, R_C, R_SUB, R_B1, R_PS, R_SB, R_END = 0, 48, 80, 88, 89, 93, 97, 105
N_ADA = 0
FIRST = 8
N_IN = {"a0": FIRST, "a1": FIRST + 16 + 96}
N_OUT = {"a0": FIRST + 12, "a1": N_IN["a1"] + 12}
N_CMP = N_IN["a1"] + 6
N_EXP = {"m0": FIRST + 16, "m1": N_OUT["a1"] + 4}
N_IN["s0"] = N_EXP["m1"] + 96
N_OUT["s0"] = N_IN["s0"] + 10
N_EXP["f0"] = N_OUT["s0"] + 4
N_IN["s1"] = N_EXP["f0"] + 3 * FF_GROUPS
N_OUT["s1"] = N_IN["s1"] + 10
N_EXP["f1"] = N_OUT["s1"] + 4
N_END = N_EXP["f1"] + 3 * FF_GROUPS
COUNT = {"m0": EXPERTS, "m1": EXPERTS, "f0": FF_GROUPS, "f1": FF_GROUPS}
COLS = {
    "a0": [(c, 256) for c in range(0, 3072, 256)],
    "a1": [(1024, 256), (1280, 256), (1536, 256), (1792, 48)] + [(c, 256) for c in range(0, 1024, 256)],
    "s0": [(c, 256) for c in range(0, 2304, 256)] + [(2304, 4)],
}
COLS["s1"] = COLS["s0"]
ATT = ("a0", "a1", "s0", "s1")


def unit_in(tag, j):
    return N_IN[tag] + j + (4 if tag == "a1" and j >= 6 else 0)


def unit_up(tag, e, part, later=False):
    return N_EXP[tag] + (3 * e + part - 1 if e >= 1 or later else part)


def unit_down(tag, e):
    return N_EXP[tag] + 4 + 3 * e - (2 if e == COUNT[tag] - 1 else 0)


def halves(n):
    return 2 * (n - FIRST) + 2


def recurring():
    att = {"a0": 16, "a1": 32, "s0": 8, "s1": 8}
    units = {"a0": 8, "a1": 32, "s0": 8, "s1": 8}
    subs = ("a0", "m0", "a1", "m1", "s0", "f0", "s1", "f1")
    lns = ("first", "ln1_0", "ln2_0", "ln1_1", "ln2_1")
    r = {}
    r["z"] = {t: len(COLS[t]) for t in ATT}
    for kind in ("qkT", "qk"):
        r[kind] = {"a0": 8, "a1": 6, "s0": 4, "s1": 4}
    for kind in ("scores", "max", "exp"):
        r[kind] = att
    for kind in ("norm", "turned", "probT", "pv"):
        r[kind] = units
    r["o"] = {"a0": 8, "a1": 8, "s0": 4, "s1": 4}
    r["roped"] = {"a0": 1, "a1": 2, "s0": 1, "s1": 1}
    for kind in ("xT", "hT_act", "hT_dve"):
        r[kind] = {t: 4 for t in subs}
    for kind in ("aT", "silu", "prod"):
        r[kind] = COUNT
    r["upc"] = {"m0": EXPERTS, "m1": EXPERTS}
    for kind in ("taps", "taps_gate", "conv", "conv_value"):
        r[kind] = {"f0": FF_GROUPS, "f1": FF_GROUPS}
    for kind in ("tap1", "tap2"):
        r[kind] = {"f0": 4 * FF_GROUPS, "f1": 4 * FF_GROUPS}
    for kind in ("hi", "lo"):
        r[kind] = {t: 4 for t in ("a0", "oa0", "m0", "a1", "oa1", "m1", "s0", "os0", "f0", "s1", "os1", "f1")}
    r["xn"] = {t: NT for t in subs[:4]}
    r["x_done"] = {t: 1 for t in subs[:4]}
    r["ssq"] = {t: 1 for t in subs[:4] + lns[:1]}
    for kind in ("var", "rstd"):
        r[kind] = {t: 1 for t in subs[:4] + lns}
    r["tile"] = {t: NT for t in lns}
    r["done"] = {t: 1 for t in lns}
    return r


RECUR = recurring()


def split(name):
    parts = name.split("_")
    for n in range(1, len(parts)):
        tag, kind = "_".join(parts[:n]), "_".join(parts[n:])
        if kind in RECUR and tag in RECUR[kind]:
            return tag, kind
    return None, name


def constants():
    c = np.zeros((P, C_END), np.float32)
    i = np.arange(P)
    c[:, C_ID:C_ID + P] = np.eye(P)
    c[:, C_TRI:C_TRI + P] = i[:, None] <= i[None, :]
    c[:, C_ONE:C_ONE + P] = 1.0
    c[:, C_MASK:C_MASK + P] = np.where(i[None, :] <= i[:, None], 0.0, NEG)
    m = np.arange(64)
    for tp in range(2):
        c[:, C_EVEN + 64 * tp:C_EVEN + 64 * tp + 64] = i[:, None] == 2 * m[None, :] + tp
    n = np.arange(CMP_N)
    for t in range(NT):
        seen = 16 * n[None, :] + 31 <= (t * P + i)[:, None]
        c[:, C_CB + t * CMP_N:C_CB + (t + 1) * CMP_N] = np.where(seen, 0.0, NEG)
        c[:, C_C01 + t * CMP_N:C_C01 + (t + 1) * CMP_N] = seen
    c[:, C_R4:C_R4 + 4] = 4 - np.arange(4)
    c[:, C_R32:C_R32 + 32] = 32 - np.arange(32)
    inv = 500000.0 ** (-np.arange(0, 16, 2) / 16.0)
    c[:, C_INV:C_INV + 8] = inv
    inv = inv.astype(np.float32)
    for t in range(NT):
        ang = (t * P + i).astype(np.float32)[:, None] * inv[None, :]
        c[:, C_COS + 8 * t:C_COS + 8 * t + 8] = np.cos(ang)
        c[:, C_SIN + 8 * t:C_SIN + 8 * t + 8] = np.sin(ang)
    for h in range(8):
        for k in range(CMP_N):
            c[k, C_REP + 16 * h + k] = 1.0
        c[16 * h:16 * h + 16, C_BLK + h] = 1.0
    s, t = np.arange(SEQ), np.arange(SEQ)
    for g, win in enumerate((2, 4, 8, 16)):
        inside = (s[:, None] <= t[None, :]) & (s[:, None] > t[None, :] - win)
        band = inside / np.minimum(t + 1, win)[None, :] - (s[:, None] == t[None, :])
        for a in range(NT):
            at = C_BAND + (a * 4 + g) * SEQ
            c[:, at:at + SEQ] = band[a * P:(a + 1) * P]
    return c


def build(nc, A, out):
    f32, i32 = mybir.dt.float32, mybir.dt.int32
    ACT, ALU = mybir.ActivationFunctionType, mybir.AluOpType
    X = mybir.AxisListType.X
    ds = bass.ds

    with ExitStack() as ctx:
        sems = {}

        def S(name):
            name = split(name)[1]
            if name not in sems:
                sems[name] = ctx.enter_context(nc.semaphore(name))
            return sems[name]

        def nth(name, n):
            tag, kind = split(name)
            if kind == "a1_hidden_done":
                return S("halves_used"), halves(N_CMP + 2 * n - 1)
            if kind.endswith("_in_done"):
                return S("halves_used"), halves(unit_in(kind[:2], n - 1))
            if kind.endswith("_out_done"):
                return S("halves_used"), halves(N_OUT[kind[:2]] + n - 1)
            if tag is None:
                return S(name), n
            order = list(RECUR[kind])
            return S(name), n + sum(RECUR[kind][t] for t in order[:order.index(tag)])

        def sb(name, shape, dt=f32):
            return ctx.enter_context(nc.sbuf_tensor(name, shape, dt))

        ring = sb("ring", [P, SLOTS, UNIT])
        cst = sb("cst", [P, C_BAND])
        x = sb("x", [P, NT, D])
        xn = sb("xn", [P, NT, D])
        fr = mybir.dt.float32r
        whi, wlo = sb("whi", [P, 4, HALF], fr), sb("wlo", [P, 4, HALF], fr)
        hhi, hlo = sb("hhi", [P, NC, SEQ], fr), sb("hlo", [P, NC, SEQ], fr)
        hT = sb("hT", [P, NC, SEQ])
        oT = hT
        work = sb("work", [P, 10240])
        z = work[:, 0:6144].rearrange("p (t n) -> p t n", t=NT)
        qkT = work[:, 6144:10240].rearrange("p (c n) -> p c n", c=16)
        cmb = work[:, 0:8192].rearrange("p (e n) -> p e n", e=EXPERTS)
        acc = sb("acc", [P, 6 * D])
        gbc = sb("gbc", [P, 2, D])
        mixed = sb("mixed", [P, 2304])
        prob = mixed[:, 0:1536].rearrange("p (j n) -> p j n", j=4)
        probT = mixed[:, 1536:2304].rearrange("p (j n) -> p j n", j=2)
        hF = hT[:, :, :].rearrange("p c n -> p (c n)")
        sil = hF[:, 0:1024].rearrange("p (b n) -> p b n", b=2)
        upc = hF[:, 1024:2048].rearrange("p (b n) -> p b n", b=2)
        ahi, alo = sb("ahi", [P, 2, 512], fr), sb("alo", [P, 2, 512], fr)
        adaw = mixed[:, 0:1536].rearrange("p (b k n) -> p b k n", b=2, k=2)
        ada_rest = xn[:, :, :].rearrange("p b n -> p (b n)").rearrange("p (b n) -> p b n", b=2)
        idb, maskh = sb("idb", [P, P], mybir.dt.bfloat16), sb("maskh", [P, P], mybir.dt.bfloat16)
        adat = sb("adat", [P, 384])
        rows = sb("rows", [P, 3, P])
        colA = sb("colA", [P, R_END])
        colB = sb("colB", [P, 80])
        csil = sb("csil", [P, NC])
        modc = sb("modc", [P, 48])
        ng = sb("ng", [P, 2, NC])
        rw = sb("rw", [P, NC, 36])
        rb = sb("rb", [P, 36])
        lamt = sb("lamt", [P, 4, 64])
        sm = sb("sm", [P, 64])
        posi = sb("posi", [P, NT], i32)
        rope = sb("rope", [P, 6, 16])
        rt = hF[:, 0:1024].rearrange("p (k n) -> p k n", k=4)
        nmax = sb("nmax", [P, 4, 2])
        psum_ = sb("psum_", [P, 4, 2])
        rsum = sb("rsum", [P, 4, 2])
        lg = sb("lg", [P, NT, 36])
        rs = sb("rs", [P, 10, 64])
        cbT = sb("cbT", [32, SEQ])
        gate = sb("gate", [P, NT, 48])
        stat = sb("stat", [P, NT, 2, 6])
        mv = sb("mv", [P, NT, 2])
        fox = sb("fox", [P, 4, 8])
        cum = sb("cum", [4, 2, SEQ])
        bfor = sb("bfor", [P, 4])
        pw = sb("pw", [P, 2, 64])
        kd = acc[:, 0:1024].rearrange("p (t a n) -> p t a n", t=NT, a=4)
        kdT = acc[:, 1024:2048].rearrange("p (a n) -> p a n", a=4)
        blk = acc[:, 2048:3008].rearrange("p (v j n) -> p v j n", v=2, j=16)
        vblk = acc[:, 3008:4032].rearrange("p (g h d) -> p g h d", g=2, h=8)
        pc = acc[:, 4032:4544].rearrange("p (t h n) -> p t h n", t=NT, h=16)
        pcT = acc[:, 4544:5056].rearrange("p (g n) -> p g n", g=2)
        hid = acc[:, 5056:5176].rearrange("p (v c n) -> p v c n", v=2, c=2)
        kcT = acc[:, 5176:5206]
        vc = acc[:, 5206:5334].rearrange("p (g d) -> p g d", g=2)
        cw2 = acc[:, 5334:5718].rearrange("p (c n) -> p c n", c=2)
        cms = acc[:, 5718:5846].rearrange("p (a n) -> p a n", a=4)
        sgw = acc[:, 0:512].rearrange("p (g n) -> p g n", g=4)
        sgwT = acc[:, 512:1024].rearrange("p (g n) -> p g n", g=4)
        sgl = acc[:, 1024:1536].rearrange("p (a n) -> p a n", a=2)
        sgt = acc[:, 1536:2048].rearrange("p (t n) -> p t n", t=NT)
        pool = acc[:, 2048:2560].rearrange("p (c n) -> p c n", c=2)
        cvt = acc[:, 2560:4608].rearrange("p (b c n) -> p b c n", b=2, c=4)
        bands = acc[:, 2560:4608]
        cvrow = acc[:, 4608:5120].rearrange("p (w n) -> p w n", w=4)
        cvc = acc[:, 5120:5296].rearrange("p (w n) -> p w n", w=4)
        cvcur = acc[:, 5296:5328].rearrange("p (b w n) -> p b w n", b=2, w=4)

        bank = [ctx.enter_context(nc.psum_tensor(f"bank{i}", [P, 512], f32)) for i in range(8)]
        scratch = nc.dram_tensor("combine_rows", (2, EXPERTS * SEQ), f32, kind="Internal").ap()

        ident, ones = cst[:, C_ID:C_ID + P], cst[:, C_ONE:C_ONE + P]
        tri, maskb = cst[:, C_TRI:C_TRI + P], cst[:, C_MASK:C_MASK + P]

        def pair(b):
            return bank[b][:, :].rearrange("p (c n) -> p c n", c=2)

        def slot(n):
            return ring[:, n % SLOTS, :]

        def half(n, h):
            b = (2 * n + h) % 4
            return whi[:, b, :], wlo[:, b, :]

        def landed(eng, n, more=0):
            eng.wait_ge(*nth(f"weights_landed{n % SLOTS}", 16 * (n // SLOTS + 1) + 32 * more))

        def used(eng, n, more=0):
            eng.wait_ge(S("halves_used"), halves(n) + 12 * more)

        class Chain:
            def __init__(self, eng, name):
                self.eng, self.sem, self.n = eng, S(name), 0

            def __call__(self, ins):
                self.n += 1
                ins.then_inc(self.sem, 1)

            def sync(self):
                self.eng.wait_ge(self.sem, self.n)

        def attention(tag):
            jobs, units = [], []
            if tag == "a0":
                for j in range(16):
                    jobs.append(dict(par=j % 2, q=qkT[:, j // 2, :], k=qkT[:, 8 + j // 2, :], fox=None))
                for u in range(8):
                    units.append(dict(jobs=(2 * u, 2 * u + 1), v=2048 + 128 * u, M=128, off=0,
                                      group=u, first=True, last=True))
            elif tag == "a1":
                for j in range(32):
                    h, w = j // 2, j % 2
                    jobs.append(dict(par=h % 2, q=qkT[:, h // 2, :], k=kdT[:, 2 * w + h // 8, :], fox=None))
                    units.append(dict(jobs=(j,), v=(1664 if w else 1408) + 64 * (h // 8), M=64,
                                      off=64 * (h % 2), group=h // 2, first=w == 0,
                                      last=h % 2 == 1 and w == 1, h=h, w=w))
            else:
                for j in range(8):
                    b, h = j // 4, j % 4
                    jobs.append(dict(par=h % 2, q=qkT[:, 4 * b + h // 2, :],
                                     k=qkT[:, 4 * b + 2 + h // 2, :], fox=h if b else None))
                    units.append(dict(jobs=(j,), v=(1280 if b else 512) + 64 * h, M=64,
                                      off=64 * (h % 2), group=j // 2, first=True, last=h % 2 == 1))
            ends = {u["jobs"][-1]: n for n, u in enumerate(units)}
            return jobs, units, ends

        def w_in(tag, c, w):
            src = A["diff_w_in"][0] if tag == "a0" else A["nsa_w_in"][0] if tag == "a1" else A["w_in_2"][int(tag[1])]
            return src[:, c:c + w].rearrange("(k p) n -> p k n", p=P)

        def w_out(tag, j):
            src = A["diff_w_out"][0] if tag == "a0" else A["nsa_w_out"][0] if tag == "a1" else A["w_o_2"][int(tag[1])]
            return src[:, 256 * j:256 * j + 256].rearrange("(k p) n -> p k n", p=P)

        block = ctx.enter_context(nc.Block())

        @block.sync
        def _(sp):
            def load(n, src, width=256, more=0):
                dst = slot(n)[:, 0:src_free(src)]
                if len(src.shape) == 3:
                    dst = dst.rearrange("p (k n) -> p k n", k=src.shape[1])
                sp.dma_start(dst, src).then_inc(S(f"weights_landed{n % SLOTS}"), 16)

            def src_free(src):
                r = 1
                for s in src.shape[1:]:
                    r *= s
                return r

            def stream(n, src, more=0):
                m = n - SLOTS
                if m >= FIRST:
                    sp.wait_ge(S("halves_split"), halves(m) + 12 * more)
                elif m >= 0:
                    sp.wait_ge(S("ada0_done"), m + 1)
                load(n, src)

            def projection(tag):
                for j, (c, w) in enumerate(COLS[tag]):
                    if tag == "a1" and j == 6:
                        for m in range(4):
                            src = A["nsa_cmp_w1"][0, m // 2, (m % 2) * 1024:(m % 2) * 1024 + 1024, :]
                            stream(N_CMP + m, src.rearrange("(k p) n -> p k n", p=P))
                    stream(unit_in(tag, j), w_in(tag, c, w))
                for j in range(4):
                    stream(N_OUT[tag] + j, w_out(tag, j))

            def up_source(tag, e, part):
                l = int(tag[1])
                if tag[0] == "m":
                    w = A[("moe_w_gate", "moe_w_up")[part]][l, ds(e, 1)]
                    return w.rearrange("o (k p) n -> p (o k) n", p=P)
                return A["w_up_2"][l][:, ds(e * HID + part * FF, HID)].rearrange("(k p) n -> p k n", p=P)

            def down_source(tag, e):
                l = int(tag[1])
                if tag[0] == "m":
                    return A["moe_w_down"][l, ds(e, 1)].rearrange("o (k p) n -> p (o k) n", p=P)
                return A["w_down_2"][l][ds(e * HID, HID), :].rearrange("(k p) n -> p k n", p=P)

            def experts(tag):
                count = COUNT[tag]

                def step(e, i=0):
                    stream(N_EXP[tag] + 4 + 3 * e, down_source(tag, i * 2 + e), i)
                    for part in range(2):
                        stream(unit_up(tag, e + 2, part), up_source(tag, i * 2 + (e + 2), part), i)

                for e in range(2):
                    for part in range(2):
                        stream(unit_up(tag, e, part), up_source(tag, e, part))
                step(0)
                step(1)
                with sp.Fori(1, (count - 2) // 2) as i:
                    step(0, i)
                    step(1, i)
                if count % 2:
                    step(count - 3)
                for e in (count - 2, count - 1):
                    stream(unit_down(tag, e), down_source(tag, e))

            for k in range(NC):
                stream(k, A["ada_w"][0, k * P:(k + 1) * P, 0:UNIT])
            projection("a0")
            experts("m0")
            projection("a1")
            experts("m1")
            for l in "01":
                projection("s" + l)
                experts("f" + l)

        @block.gpsimd
        def _(pool_eng):
            g = pool_eng

            def aux(name, dst, src):
                g.dma_start(dst, src).then_inc(S(name), 16)

            def row(src):
                return src.rearrange("(o n) -> o n", o=1)

            def everywhere(src):
                return row(src).broadcast_to([P, src.shape[0]])

            g.memset(rows[:, :, :], 0.0).then_inc(S("rows_clear"), 1)
            g.wait_ge(*nth("rows_clear", 1))
            aux("rowc_landed", rows[0:NC, 2, :], A["c"][0].rearrange("(c p) -> c p", p=P))
            aux("const_landed", cst[:, :], A["consts"][:, 0:C_BAND])
            ra = rows[:, 0, :]
            aux("rows_landed", ra[0:48, :], A["ada_b"][0].rearrange("(c p) -> c p", p=P))
            aux("rows_landed", ra[R_NG:R_NG + 32, :], A["norm_g"].rearrange("l s (c p) -> (l s c) p", p=P))
            aux("rows_landed", ra[R_SUB:R_SUB + 1, :], A["diff_subln_g"])
            aux("rows_landed", ra[R_B1:R_B1 + 4, :], A["nsa_cmp_b1"][0].rearrange("v (c p) -> (v c) p", p=P))
            aux("rows_landed", ra[R_PS:R_PS + 4, :], A["pool_scale_2"].rearrange("l (c p) -> (l c) p", p=P))
            aux("rows_landed", ra[R_SB:R_SB + 8, :], A["sgu_b_2"].rearrange("l g t -> (l g) t"))
            aux("rows_landed", rows[0:48, 1, :], A["ada_b"][1].rearrange("(c p) -> c p", p=P))
            aux("rows_landed", rows[48:80, 1, :],
                A["nsa_cmp_pos"][0].rearrange("v (j t) d -> (v j) (t d)", t=2))
            aux("x_landed", x[:, :, :], A["x"][0].rearrange("(t p) n -> p t n", p=P))
            for t in range(NT):
                aux("pos_landed", posi[:, t:t + 1], A["positions"][0, t * P:(t + 1) * P].rearrange("(p o) -> p o", o=1))
            aux("lam_landed", lamt[:, :, :].rearrange("p a b -> p (a b)"),
                everywhere(A["diff_lambda"][0].rearrange("a b -> (a b)")))

            def gates(l):
                for n, v in enumerate((2, 5)):
                    aux("gbc_landed", gbc[:, n, :], everywhere(A["ada_b"][l, v * D:(v + 1) * D]))

            def router(l):
                aux("router_landed", rw[:, :, 0:4], A["moe_w_group"][l].rearrange("(k p) n -> p k n", p=P))
                for q in range(GROUPS):
                    aux("router_landed", rw[:, :, 4 + 8 * q:12 + 8 * q],
                        A["moe_w_expert"][l, q].rearrange("(k p) n -> p k n", p=P))
                aux("router_landed", rb[:, 0:4], everywhere(A["moe_b_group"][l]))
                aux("router_landed", rb[:, 4:36], everywhere(A["moe_b_expert"][l].rearrange("a b -> (a b)")))

            def combine(l):
                g.wait_ge(*nth("combine_rows_ready", l + 1))
                aux("combine_stored", scratch[l].rearrange("(e t) -> e t", e=EXPERTS), cbT[:, :])
                g.wait_ge(*nth("combine_stored", 16 * (l + 1)))
                aux("combine_landed", work[:, 0:8192], everywhere(scratch[l]))

            gates(0)
            router(0)
            for q in range(32):
                if q < 2:
                    g.wait_ge(*nth("a0_xT", 4))
                else:
                    g.wait_ge(S("ada0_rest"), q - 1)
                k, part = divmod(q, 4)
                at = UNIT + part * HALF
                aux(f"ada_rest_landed{q % 2}", ada_rest[:, q % 2, :], A["ada_w"][0, k * P:(k + 1) * P, at:at + HALF])
            combine(0)
            layer1 = A["ada_w"][1].rearrange("(k p) n -> p k n", p=P)

            for q in range(4):
                if q > 1:
                    g.wait_ge(S("ada1_used"), q - 1)
                aux(f"ada1_landed{q % 2}", adaw[:, q % 2], layer1[:, 2 * q:2 * q + 2, 15 * 384:16 * 384])
            with g.Fori(0, 15) as i:
                for q in range(4):
                    g.wait_ge(S("ada1_used"), i * 4 + (q + 3))
                    aux(f"ada1_landed{q % 2}", adaw[:, q % 2], layer1[:, 2 * q:2 * q + 2, ds(i * 384, 384)])
            router(1)
            g.wait_ge(*nth("m0_x_done", 1))
            gates(1)
            g.wait_ge(*nth("mod_done", 2))
            aux("cmpw_landed", cw2[:, :, 0:64], A["nsa_cmp_w2"][0, 0].rearrange("(c p) n -> p c n", p=P))
            aux("cmpw_landed", cw2[:, :, 64:128], A["nsa_cmp_w2"][0, 0].rearrange("(c p) n -> p c n", p=P))
            aux("cmpw_landed", cw2[:, :, 128:192], A["nsa_cmp_w2"][0, 1].rearrange("(c p) n -> p c n", p=P))
            combine(1)
            aux("final_landed", gbc[:, 0, :], everywhere(A["final_g"]))

            def ln(name, l):
                for n, v in enumerate(("g", "b")):
                    aux(f"{name}{l}_landed", gbc[:, n, :], everywhere(A[f"{name}_{v}_2"][l]))

            for l in range(2):
                if l == 0:
                    g.wait_ge(*nth("first_done", 1))
                else:
                    g.wait_ge(*nth("ln2_0_done", 1))
                ln("ln1", l)
                aux("mix_landed", sgw[:, :, :], A["sgu_w_2"][l].rearrange("g t s -> t g s"))
                aux("mix_landed", sgl[:, 0, :], everywhere(A["sgu_ln_g_2"][l]))
                aux("mix_landed", sgl[:, 1, :], everywhere(A["sgu_ln_b_2"][l]))
                aux("mix_landed", bfor[:, :], everywhere(A["b_forget_2"][l]))
                aux("mix_landed", pw[:, :, :], A["pool_w_2"][l].rearrange("(b a) c d -> (a c) b d", a=2))
                aux("mix_landed", bands, A["consts"][:, C_BAND:C_END])
                for w in range(3):
                    aux("conv_landed", cvrow[0:44, w, :], A["conv_w_2"][l, w].rearrange("(c p) -> c p", p=P))
                aux("conv_landed", cvrow[0:44, 3, :], A["conv_b_2"][l].rearrange("(c p) -> c p", p=P))
                g.wait_ge(*nth(f"ln1_{l}_done", 1))
                ln("ln2", l)
            for t in range(NT):
                g.wait_ge(*nth("ln2_1_tile", t + 1))
                g.dma_start(out[0, t * P:(t + 1) * P, :], x[:, t, :]).then_inc(S("out_stored"), 16)
            g.wait_ge(*nth("out_stored", 32))

        @block.tensor
        def _(pe):
            def mm(o, l, r, start=True, stop=True):
                return pe.matmul(o, l, r, start=start, stop=stop, skip_group_check=True)

            def columns(first, n, tag):
                for i in range(first, first + n):
                    last = pe.transpose(bank[7][:, i * P:i * P + P], rows[:, i, :], ident)
                last.then_inc(S(tag), 1)

            def mod_columns(vectors, b):
                for v in vectors:
                    for c in range(NC):
                        at = v * D + c * P
                        last = mm(bank[b][:, v * 8 + c:v * 8 + c + 1], acc[:, at:at + P], ones[:, 0:1])
                last.then_inc(S("modc_ready"), 1)

            def mod_gates(b):
                for n, v in enumerate((2, 5)):
                    for h in range(2):
                        last = mm(bank[b + 2 * n + h][:, :], ones, acc[:, v * D + h * 512:v * D + h * 512 + 512])
                last.then_inc(S("modg_ready"), 1)

            def transposes(tag, src, ready):
                for b in range(4):
                    for c in (2 * b, 2 * b + 1):
                        for t in range(NT):
                            if c == 0:
                                pe.wait_ge(*nth(ready, t + 1))
                            if c == 6 and t == 0 and tag == "a0":
                                pe.wait_ge(*nth("ng_ready", 1))
                            last = pe.transpose(bank[4 + b][:, (c % 2) * 256 + t * P:(c % 2) * 256 + t * P + P],
                                                src[:, t, c * P:(c + 1) * P], ident)
                    last.then_inc(S(f"{tag}_xT"), 1)

            def hT_ready(tag):
                pe.wait_ge(*nth(f"{tag}_lo", 4))

            def split_ready(n, h, more=0):
                pe.wait_ge(S("halves_split"), halves(n) - 1 + h + 12 * more)

            def project(tag, j, n=None, out_of=None):
                if out_of is None:
                    w, n, b = COLS[tag][j][1], unit_in(tag, j), 4 + j % 4
                    if j >= 4:
                        pe.wait_ge(*nth(f"{tag}_z", j - 3))
                else:
                    w, n, b = 256, N_OUT[tag] + j, 4 + j
                ks = 4 if w == 256 else 8
                for h in range(2 if w == 256 else 1):
                    split_ready(n, h if w == 256 else 1)
                    Wh, Wl = (v[:, 0:ks * w].rearrange("p (k n) -> p k n", k=ks) for v in half(n, h))
                    for t in range(NT):
                        for k in range(ks):
                            first = h == 0 and t == 0 and k == 0
                            c = 4 * h + k
                            xh, xl = hhi[:, c, t * P:(t + 1) * P], hlo[:, c, t * P:(t + 1) * P]
                            o = pair(b)[:, t, 0:w]
                            mm(o, xh, Wh[:, k, :], start=first)
                            mm(o, xh, Wl[:, k, :], start=False)
                            last = mm(o, xl, Wh[:, k, :], start=False)
                    last.then_inc(S("halves_used"), 1 if w == 256 else 2)

            def project_out(tag):
                pe.wait_ge(*nth(f"o{tag}_lo", 4))
                for j in range(4):
                    project(tag, j, out_of=True)

            def head_transposes(tag, sources):
                for i, (view, c) in enumerate(sources):
                    b = (i // 2) % 4
                    if i % 2 == 0 and i >= 8:
                        pe.wait_ge(*nth(f"{tag}_qk", i // 2 - 3))
                    for t in range(NT):
                        last = pe.transpose(bank[b][:, (i % 2) * 256 + t * P:(i % 2) * 256 + t * P + P],
                                            view[:, t, c:c + P], ident)
                    if i % 2:
                        last.then_inc(S(f"{tag}_qkT"), 1)

            def attend(tag, after=None):
                jobs, units, ends = attention(tag)
                J = len(jobs)

                def scores(j):
                    job = jobs[j]
                    if j >= 4:
                        pe.wait_ge(*nth(f"{tag}_exp", j - 3))
                    rows_ = slice(64 * job["par"], 64 * job["par"] + 64)
                    for t, (at, kl) in enumerate(((0, P), (P, SEQ))):
                        o = bank[j % 4][:, at:at + kl]
                        mm(o, job["q"][rows_, t * P:(t + 1) * P], job["k"][rows_, 0:kl], stop=False)
                        if job["fox"] is not None:
                            h = job["fox"]
                            mm(o, ident[0:4, h:h + 1].broadcast_to([4, P]), cum[:, 1, 0:kl], False, False)
                            mm(o, cum[:, 0, t * P:(t + 1) * P], ident[0:4, h:h + 1].broadcast_to([4, kl]),
                               False, False)
                        last = mm(bank[j % 4][:, at + kl - P:at + kl], idb[:, :], maskh[:, :], start=False)
                    last.then_inc(S(f"{tag}_scores"), 1)

                def turn(u):
                    pe.wait_ge(*nth(f"{tag}_norm", u + 1))
                    if u >= 2:
                        pe.wait_ge(*nth(f"{tag}_probT", u - 1))
                    j = units[u]["jobs"][0]
                    for b in range(3):
                        last = pe.transpose(bank[4 + u % 2][:, b * P:(b + 1) * P],
                                            prob[:, j % 4, b * P:(b + 1) * P], ident)
                    last.then_inc(S(f"{tag}_turned"), 1)

                def values(u):
                    U = units[u]
                    pe.wait_ge(*nth(f"{tag}_probT", u + 1))
                    if U["first"] and U["group"] >= 2 and U["off"] == 0:
                        pe.wait_ge(*nth(f"{tag}_o", U["group"] - 1))
                    o = bank[6 + U["group"] % 2][U["off"]:U["off"] + U["M"], :]
                    mm(o[:, 0:SEQ], z[:, 0, U["v"]:U["v"] + U["M"]], probT[:, u % 2, 0:SEQ],
                       start=U["first"], stop=False)
                    last = mm(o[:, P:SEQ], z[:, 1, U["v"]:U["v"] + U["M"]], probT[:, u % 2, SEQ:384],
                              start=False, stop=tag != "a1")
                    if tag == "a1" and U["w"] == 1:
                        g_ = U["h"] // 8
                        if u == 1:
                            pe.wait_ge(*nth("cmp_ready", 2))
                        last = mm(o[:, 0:SEQ], vblk[:, g_, U["h"] % 8, :], pcT[:, g_, :], start=False)
                    last.then_inc(S(f"{tag}_pv"), 1)

                for j in range(J + 4):
                    if j < J:
                        scores(j)
                    if j - 2 in ends:
                        turn(ends[j - 2])
                    if j - 3 in ends:
                        values(ends[j - 3])

            def experts(tag):
                count = COUNT[tag]

                def up(e, i=0):
                    for part in range(2):
                        n = unit_up(tag, e, part)
                        b = 4 + 2 * (e % 2) + part
                        for h in range(2):
                            split_ready(n, h, i)
                            Wh, Wl = (v.rearrange("p (k n) -> p k n", k=4) for v in half(n, h))
                            for c in range(2):
                                for k in range(4):
                                    xh, xl = hhi[:, 4 * h + k, :], hlo[:, 4 * h + k, :]
                                    o = pair(b)[:, c, :]
                                    mm(o, Wh[:, k, c * P:(c + 1) * P], xh, start=h + c + k == 0)
                                    mm(o, Wh[:, k, c * P:(c + 1) * P], xl, start=False)
                                    last = mm(o, Wl[:, k, c * P:(c + 1) * P], xh, start=False)
                            last.then_inc(S("halves_used"), 1)

                def down(e, i=0, start=False):
                    n = unit_down(tag, e)
                    pe.wait_ge(*nth(f"{tag}_aT", i * 2 + e + 1))
                    for c in range(2):
                        split_ready(n, c, i)
                        Wh, Wl = half(n, c)
                        for t in range(NT):
                            a = slice(c * SEQ + t * P, c * SEQ + t * P + P)
                            for j in range(2):
                                o, w = bank[2 * t + j][:, :], slice(j * 512, (j + 1) * 512)
                                mm(o, ahi[:, e % 2, a], Wh[:, w], start=start and c == 0)
                                mm(o, ahi[:, e % 2, a], Wl[:, w], start=False)
                                last = mm(o, alo[:, e % 2, a], Wh[:, w], start=False)
                        last.then_inc(S("halves_used"), 1)

                if tag[0] == "m":
                    l = int(tag[1])
                    pe.wait_ge(*nth("router_landed", 7 * 16 * (l + 1)))
                    for t in range(NT):
                        for k in range(NC):
                            last = mm(bank[6][:, t * 64:t * 64 + 36], hT[:, k, t * P:(t + 1) * P], rw[:, k, :],
                                      start=k == 0, stop=k == NC - 1)
                    last.then_inc(S("logits_done"), 1)
                up(0)
                if tag[0] == "m":
                    pe.wait_ge(*nth("logits_read", l + 1))
                    pe.wait_ge(*nth("combine_ready", l + 1))
                    for t in range(NT):
                        last = pe.transpose(bank[0][0:32, t * P:(t + 1) * P], rs[:, 0, t * 32:(t + 1) * 32], ident)
                    last.then_inc(S("combine_turned"), 1)
                up(1)
                if tag[0] == "m":
                    pe.wait_ge(*nth("combine_rows_ready", l + 1))
                down(0, start=True)
                up(2)
                down(1)
                up(3)
                with pe.Fori(1, (count - 2) // 2) as i:
                    down(0, i)
                    up(2, i)
                    down(1, i)
                    up(3, i)
                if count % 2:
                    down(count - 3)
                    up(count - 1)
                down(count - 2)
                if tag == "m0":
                    pe.wait_ge(*nth("ada1_done", 16))
                    mod_columns((0, 1, 3, 4), 4)
                down(count - 1)

            pe.wait_ge(*nth("rowc_landed", 16))
            pe.wait_ge(*nth("const_landed", 16))
            pe.transpose(bank[6][:, 0:NC], rows[0:NC, 2, :], ident[0:NC, 0:NC]).then_inc(S("c_turned"), 1)
            pe.wait_ge(*nth("rows_landed", 8 * 16))
            columns(0, 2, "cols_turned")
            pe.wait_ge(*nth("mask_ready", 1))
            pe.wait_ge(*nth("ada0_done", NC))
            mod_columns((0, 1), 7)
            transposes("a0", xn, "a0_xn")
            hT_ready("a0")
            for j in range(12):
                project("a0", j)
            pe.wait_ge(*nth("a0_roped", 1))
            head_transposes("a0", [(z, P * i) for i in range(16)])
            pe.wait_ge(*nth("a0_qk", 8))
            attend("a0")
            pe.wait_ge(*nth("ada0_rest", 32))
            mod_columns((3, 4), 0)
            pe.wait_ge(*nth("a0_o", 8))
            mod_gates(4)
            pe.wait_ge(*nth("sub_sq", 1))
            for b in range(4):
                last = mm(bank[b][:, :], ones, xn[:, b // 2, (b % 2) * 512:(b % 2) * 512 + 512])
            last.then_inc(S("sub_sum"), 1)
            project_out("a0")
            transposes("m0", xn, "m0_xn")
            hT_ready("m0")
            experts("m0")
            transposes("a1", xn, "a1_xn")
            mod_gates(0)
            hT_ready("a1")
            for j in range(4):
                project("a1", j)
            project("a1", 4)
            pe.wait_ge(*nth("a1_z", 4))
            for v in range(2):
                for g_ in range(2):
                    for tp in range(2):
                        for t in range(NT):
                            c = 1024 + v * 128 + g_ * 64
                            at = (v * 2 + g_) * 128 + t * 64
                            last = mm(bank[0][64 * tp:64 * tp + 64, at:at + 64], z[:, t, c:c + 64],
                                      cst[:, C_EVEN + 64 * tp:C_EVEN + 64 * tp + 64])
            last.then_inc(S("cmp_split"), 1)
            project("a1", 5)
            for v in range(2):
                pe.wait_ge(*nth("blk_ready", v + 1))
                first = True
                for m in range(4):
                    n, h = N_CMP + 2 * v + m // 2, m % 2
                    split_ready(n, h)
                    for c in range(2):
                        for j in range(4):
                            for part in half(n, h):
                                W = part.bitcast(f32).rearrange("p (k n) -> p k n", k=4)
                                last = mm(bank[1 + 2 * v][:, c * 32:c * 32 + 30],
                                          W[:, j, c * P:(c + 1) * P], blk[:, v, 4 * m + j, :],
                                          start=first)
                                first = False
                    last.then_inc(S("halves_used"), 1)
            project("a1", 6)
            pe.wait_ge(*nth("hid_ready", 1))
            pe.wait_ge(*nth("cmpw_landed", 48))
            for c in range(2):
                mm(bank[2][:, 0:30], cw2[:, c, 0:128], hid[:, 0, c, :], start=c == 0, stop=c == 1)
            for g_ in range(2):
                for c in range(2):
                    last = mm(bank[2][0:15, 64 + 64 * g_:128 + 64 * g_], hid[:, 1, c, 15 * g_:15 * g_ + 15],
                              cw2[:, c, 128:192], start=c == 0, stop=c == 1)
            last.then_inc(S("cmp_kv"), 1)
            project("a1", 7)
            pe.wait_ge(*nth("cmp_kv_read", 1))
            for g_ in range(2):
                last = mm(bank[3][:, g_ * 64:g_ * 64 + 64], cst[0:15, C_REP:C_REP + P], vc[0:15, g_, :])
            last.then_inc(S("vc_spread"), 1)
            pe.wait_ge(*nth("a1_roped", 2))
            pe.wait_ge(*nth("vblk_ready", 1))
            kd_ = kd.rearrange("p t a n -> p t (a n)")
            head_transposes("a1", [(z, P * i) for i in range(8)] + [(kd_, P * i) for i in range(4)])
            pe.wait_ge(*nth("a1_qk", 6))
            pe.wait_ge(*nth("a1_z", 8))
            for t in range(NT):
                for h in range(16):
                    r = slice(64 * (h % 2), 64 * (h % 2) + 64)
                    at = (t * 8 + h // 2) * 16
                    last = mm(bank[4 + h % 2][:, at:at + CMP_N], qkT[r, h // 2, t * P:(t + 1) * P],
                              kcT[r, 15 * (h // 8):15 * (h // 8) + 15])
            last.then_inc(S("cmp_scores"), 1)
            pe.wait_ge(*nth("pc_ready", 1))
            for g_ in range(2):
                for t in range(NT):
                    last = pe.transpose(bank[5][:, g_ * 256 + t * P:g_ * 256 + t * P + P],
                                        pc[:, t, 8 * g_:8 * g_ + 8, :].rearrange("p h n -> p (h n)"), ident)
            last.then_inc(S("pc_turned"), 1)
            pe.wait_ge(*nth("cmp_ready", 1))
            attend("a1")
            project_out("a1")
            transposes("m1", xn, "m1_xn")
            hT_ready("m1")
            experts("m1")
            for l in range(2):
                tag, ffn = f"s{l}", f"f{l}"
                transposes(tag, x, "first_tile" if l == 0 else "ln2_0_tile")
                hT_ready(tag)
                for j in range(10):
                    project(tag, j)
                pe.wait_ge(*nth("mix_landed", 6 * 16 * (l + 1)))
                for g_ in range(4):
                    last = pe.transpose(bank[3][:, g_ * P:(g_ + 1) * P], sgw[:, g_, :], ident)
                last.then_inc(S("sgw_turned"), 1)
                pe.wait_ge(*nth("conv_landed", 4 * 16 * (l + 1)))
                for w in range(4):
                    last = pe.transpose(bank[2][:, w * 44:w * 44 + 44], cvrow[0:44, w, :], ident[0:44, 0:44])
                last.then_inc(S("conv_turned"), 1)
                pe.wait_ge(*nth("logf_ready", l + 1))
                mm(bank[1][0:4, 0:SEQ], fox[:, 3, 0:4], cst[:, C_TRI:C_TRI + SEQ], stop=False)
                mm(bank[1][0:4, P:SEQ], fox[:, 3, 4:8], tri, start=False).then_inc(S("cum_done"), 1)
                pe.wait_ge(*nth(f"{tag}_z", 10))
                for g_ in range(4):
                    o = bank[0][64 * (g_ % 2):64 * (g_ % 2) + 64, (g_ // 2) * SEQ:(g_ // 2 + 1) * SEQ]
                    for t in range(NT):
                        at = (t * 4 + g_) * SEQ
                        last = mm(o[:, t * P:SEQ], z[:, t, 2052 + 64 * g_:2116 + 64 * g_],
                                  bands[:, at + t * P:at + SEQ], start=t == 0, stop=t == 1)
                last.then_inc(S("pooled"), 1)
                pe.wait_ge(*nth("pool_ready", l + 1))
                for g_ in range(4):
                    r = slice(64 * (g_ % 2), 64 * (g_ % 2) + 64)
                    last = mm(bank[0][r, (g_ // 2) * SEQ:(g_ // 2 + 1) * SEQ], pw[r, g_ // 2, :],
                              pool[r, g_ // 2, :])
                last.then_inc(S("pool_mixed"), 1)
                pe.wait_ge(*nth("sgv_ready", l + 1))
                for t in range(NT):
                    for g_ in range(4):
                        at = t * SEQ + g_ * 64
                        last = mm(bank[4][:, at:at + 64], sgwT[:, g_, :], z[:, t, 1796 + 64 * g_:1860 + 64 * g_])
                last.then_inc(S("sg_mixed"), 1)
                pe.wait_ge(*nth("sgy_ready", l + 1))
                for c in range(2):
                    for t in range(NT):
                        last = pe.transpose(bank[5][:, c * SEQ + t * P:c * SEQ + t * P + P],
                                            sgt[:, t, c * P:(c + 1) * P], ident)
                last.then_inc(S("sg_turned"), 1)
                pe.wait_ge(*nth(f"{tag}_roped", 1))
                pe.wait_ge(*nth("mix_read", l + 1))
                head_transposes(tag, [(z, c) for c in (0, 128, 256, 384, 768, 896, 1024, 1152)])
                pe.wait_ge(*nth(f"{tag}_qk", 4))
                attend(tag)
                project_out(tag)
                transposes(ffn, x, f"ln1_{l}_tile")
                hT_ready(ffn)
                experts(ffn)

        @block.scalar
        def _(act):
            ch = Chain(act, "act_chain")

            def norm(tag):
                for t in range(NT):
                    ch(act.activation(xn[:, t, :], x[:, t, :], ACT.Square, accum_out=sm[:, t:t + 1]))
                ch.sync()
                act.activation(sm[:, 6:8], sm[:, 0:2], ACT.Copy).then_inc(S(f"{tag}_ssq"), 1)
                root(tag)

            def root(tag, at=2, n=2):
                act.wait_ge(*nth(f"{tag}_var", 1))
                act.activation(sm[:, at + n:at + 2 * n], sm[:, at:at + n], ACT.Sqrt).then_inc(S(f"{tag}_rstd"), 1)

            def hT_copy(tag, scale=None, bias=None):
                for c in (0, 1, 4, 5):
                    act.wait_ge(*nth(f"{tag}_xT", c // 2 + 1))
                    kw = {} if scale is None else dict(scale=scale[:, c:c + 1], bias=bias[:, c:c + 1])
                    f = ACT.Copy if scale is None else ACT.Identity
                    act.activation(hT[:, c, :], pair(4 + c // 2)[:, c % 2, :], f, **kw)\
                       .then_inc(S(f"{tag}_hT_act"), 1)

            def split(n, more=0):
                landed(act, n, more)
                for h in range(2):
                    if n >= FIRST + 2:
                        act.wait_ge(S("halves_used"), halves(n - 2) - 1 + h + 12 * more)
                    act.activation(half(n, h)[0], slot(n)[:, h * HALF:(h + 1) * HALF], ACT.Copy)\
                       .then_inc(S("high_parts"), 1)

            def z_copy(tag, j):
                split(unit_in(tag, j) + 2)
                c, w = COLS[tag][j]
                act.wait_ge(*nth(f"{tag}_in_done", j + 1))
                act.activation(z[:, :, c:c + w], pair(4 + j % 4)[:, :, 0:w], ACT.Copy).then_inc(S(f"{tag}_z"), 1)

            def hT_high(tag):
                for b in range(4):
                    if tag[0] != "o":
                        act.wait_ge(*nth(f"{tag}_hT_" + ("dve" if b % 2 else "act"), 2 + 2 * (b // 2)))
                    act.activation(hhi[:, 2 * b:2 * b + 2, :], hT[:, 2 * b:2 * b + 2, :], ACT.Copy)\
                       .then_inc(S(f"{tag}_hi"), 1)

            def out_splits(tag):
                for j in range(4):
                    split(N_OUT[tag] + j + 2)

            def qk_copy(tag, n, queries):
                for i in range(n):
                    act.wait_ge(*nth(f"{tag}_qkT", i + 1))
                    q = queries[i]
                    dst = (qkT[:, 2 * i:2 * i + 2, :] if tag != "a1" or i < 4
                           else kdT[:, 2 * i - 8:2 * i - 6, :])
                    act.activation(dst, pair(i % 4)[:, :, :], ACT.Copy, scale=0.125 if q else 1.0)\
                       .then_inc(S(f"{tag}_qk"), 1)

            def attend(tag):
                jobs, units, ends = attention(tag)
                unit_of = {j: n for n, u in enumerate(units) for j in u["jobs"]}
                for j in range(len(jobs) + 3):
                    if j < len(jobs):
                        act.wait_ge(*nth(f"{tag}_max", j + 1))
                        if j >= 4:
                            act.wait_ge(*nth(f"{tag}_turned", unit_of[j - 4] + 1))
                        ch(act.activation(prob[:, j % 4, 0:P], bank[j % 4][:, 0:P], ACT.Exp,
                                          bias=nmax[:, j % 4, 0:1], accum_out=psum_[:, j % 4, 0:1]))
                        act.activation(prob[:, j % 4, P:384], bank[j % 4][:, P:384], ACT.Exp,
                                       bias=nmax[:, j % 4, 1:2], accum_out=psum_[:, j % 4, 1:2])\
                           .then_inc(S(f"{tag}_exp"), 1)
                    if j - 2 in ends:
                        u = ends[j - 2]
                        act.wait_ge(*nth(f"{tag}_turned", u + 1))
                        if u >= 2:
                            act.wait_ge(*nth(f"{tag}_pv", u - 1))
                        act.activation(probT[:, u % 2, :], bank[4 + u % 2][:, 0:384], ACT.Copy)\
                           .then_inc(S(f"{tag}_probT"), 1)

            def experts(tag):
                count = COUNT[tag]

                def silu(e, i=0, wait=True):
                    used(act, unit_up(tag, e, 1), i)
                    if wait:
                        act.wait_ge(*nth(f"{tag}_aT", i * 2 + e - 1))
                    src = bank[4 + 2 * (e % 2)][:, :]
                    if tag[0] == "f":
                        act.wait_ge(*nth(f"{tag}_taps", i * 2 + e + 1))
                        for c in range(4):
                            act.activation(cvt[:, e % 2, c, :], pair(4 + 2 * (e % 2) + c // 2)[:, c % 2, :],
                                           ACT.Identity, scale=cvcur[:, e % 2, 2, c:c + 1],
                                           bias=cvcur[:, e % 2, 3, c:c + 1]).then_inc(S(f"{tag}_tap2"), 1)
                        act.wait_ge(*nth(f"{tag}_conv", i * 2 + e + 1))
                        src = cvt[:, e % 2, 0:2, :].rearrange("p c n -> p (c n)")
                    act.activation(sil[:, e % 2, :], src, ACT.Silu).then_inc(S(f"{tag}_silu"), 1)

                def step(e, i=0):
                    for k in range(3):
                        split(unit_down(tag, e) + 2 + k, i)
                    silu(e + 2, i)

                first = N_EXP[tag]
                split(first + 2)
                split(first + 3)
                silu(0, wait=False)
                split(first + 4)
                split(first + 5)
                silu(1, wait=False)
                with act.Fori(0, (count - 2) // 2) as i:
                    step(0, i)
                    step(1, i)
                if count % 2:
                    step(count - 3)
                for e in (count - 2, count - 1):
                    if unit_down(tag, e) + 2 < N_END:
                        split(unit_down(tag, e) + 2)

            experts_m = experts_f = experts

            act.wait_ge(*nth("c_turned", 1))
            act.activation(csil[:, :], bank[6][:, 0:NC], ACT.Silu).then_inc(S("csil_ready"), 1)
            act.wait_ge(*nth("lam_dots", 1))
            act.activation(sm[:, 12:14], sm[:, 10:12], ACT.Exp).then_inc(S("lam_exp"), 1)
            act.wait_ge(*nth("angles", 1))
            act.activation(rope[:, 0:2, :], rope[:, 2:4, :], ACT.Sin).then_inc(S("rope_ready"), 1)
            split(FIRST)
            split(FIRST + 1)
            act.wait_ge(*nth("x_landed", 16))
            norm("a0")
            act.wait_ge(*nth("ng_ready", 1))
            hT_copy("a0", ng[:, 0, :], modc[:, 0:8])
            hT_high("a0")
            for j in range(12):
                z_copy("a0", j)
            qk_copy("a0", 8, [True] * 4 + [False] * 4)
            attend("a0")
            act.wait_ge(*nth("sub_var", 1))
            act.activation(xn[:, :, :], xn[:, :, :], ACT.Sqrt).then_inc(S("sub_rstd"), 1)
            act.wait_ge(*nth("a0_oT", 1))
            hT_high("oa0")
            out_splits("a0")
            act.wait_ge(*nth("a0_x_done", 1))
            norm("m0")
            act.wait_ge(*nth("ng_ready", 2))
            hT_copy("m0", ng[:, 1, :], modc[:, 24:32])
            hT_high("m0")

            def route(l):
                act.wait_ge(*nth("route_diff", l + 1))
                act.activation(rs[:, 6, 0:8], rs[:, 5, 0:8], ACT.Exp).then_inc(S("route_exp"), 1)
                act.activation(rs[:, 6, 8:10], rs[:, 5, 8:10], ACT.Exp).then_inc(S("route_exp"), 1)

            route(0)
            experts_m("m0")
            act.wait_ge(*nth("m0_x_done", 1))
            norm("a1")
            act.wait_ge(*nth("ng_ready", 3))
            hT_copy("a1", ng[:, 0, :], modc[:, 0:8])
            hT_high("a1")
            for j in range(4):
                z_copy("a1", j)
            act.wait_ge(*nth("a1_z", 4))
            act.activation(gate[:, :, :], z[:, :, 1792:1840], ACT.Exp, scale=-1.0).then_inc(S("gate_exp"), 1)
            z_copy("a1", 4)
            z_copy("a1", 5)
            for v in range(2):
                for n in (N_CMP + 2 * v + 2, N_CMP + 2 * v + 3):
                    split(n)
                act.wait_ge(*nth("a1_hidden_done", v + 1))
                for c in range(2):
                    at = R_B1 + 2 * v + c
                    last = act.activation(hid[:, v, c, :], bank[1 + 2 * v][:, c * 32:c * 32 + 30],
                                          ACT.Gelu_apprx_tanh, bias=colA[:, at:at + 1])
                    if (v, c) != (1, 1):
                        ch(last)
            last.then_inc(S("hid_ready"), 1)
            z_copy("a1", 6)
            z_copy("a1", 7)
            qk_copy("a1", 6, [True] * 4 + [False] * 2)
            act.wait_ge(*nth("pc_diff", 1))
            act.activation(pc[:, :, :, 0:CMP_N], pc[:, :, :, 0:CMP_N], ACT.Exp).then_inc(S("pc_exp"), 1)
            act.wait_ge(*nth("pc_turned", 1))
            act.activation(pcT[:, :, :], pair(5)[:, :, :], ACT.Copy).then_inc(S("cmp_ready"), 1)
            act.wait_ge(*nth("cmp_ready", 1))
            act.activation(sm[:, 20:21], sm[:, 0:1], ACT.Copy).then_inc(S("cmp_ready"), 1)
            attend("a1")
            act.wait_ge(*nth("a1_o", 8))
            hT_high("oa1")
            out_splits("a1")
            act.wait_ge(*nth("a1_x_done", 1))
            norm("m1")
            hT_copy("m1", ng[:, 1, :], modc[:, 24:32])
            hT_high("m1")
            route(1)
            experts_m("m1")
            act.wait_ge(*nth("m1_x_done", 1))
            norm("first")
            for l in range(2):
                tag, ffn = f"s{l}", f"f{l}"
                hT_copy(tag)
                hT_high(tag)
                for j in range(10):
                    z_copy(tag, j)
                act.wait_ge(*nth("absf", l + 1))
                ch(act.activation(fox[:, 1, :], fox[:, 1, :], ACT.Exp, scale=-1.0))
                ch.sync()
                act.activation(fox[:, 2, :], fox[:, 1, :], ACT.Ln, bias=1.0).then_inc(S("ln1p"), 1)
                act.wait_ge(*nth(f"{tag}_z", 10))
                act.activation(z[:, :, 1796:2052], z[:, :, 1796:2052], ACT.Gelu).then_inc(S("gelu"), 1)
                act.activation(z[:, :, 1540:1796], z[:, :, 1540:1796], ACT.Gelu).then_inc(S("gelu"), 1)
                act.wait_ge(*nth("sg_var", l + 1))
                act.activation(sm[:, 40:48], sm[:, 32:40], ACT.Sqrt).then_inc(S("sg_rstd"), 1)
                qk_copy(tag, 4, [True, False, True, False])
                attend(tag)
                act.wait_ge(*nth(f"{tag}_o", 4))
                hT_high("o" + tag)
                out_splits(tag)
                root(f"ln1_{l}")
                hT_copy(ffn)
                hT_high(ffn)
                experts_f(ffn)
                root(f"ln2_{l}")

        @block.vector
        def _(dve):
            ch = Chain(dve, "dve_chain")
            TT, TS, STT = dve.tensor_tensor, dve.tensor_scalar, dve.scalar_tensor_tensor

            def ts(o, a, s1, op0, s2=None, op1=None):
                if op1 is None:
                    return TS(out=o, in0=a, scalar1=s1, scalar2=None, op0=op0)
                return TS(out=o, in0=a, scalar1=s1, scalar2=s2, op0=op0, op1=op1)

            def stt(o, a, s, b, op0, op1):
                return STT(out=o, in0=a, scalar=s, in1=b, op0=op0, op1=op1)

            def norm(tag):
                dve.wait_ge(*nth(f"{tag}_ssq", 1))
                ch(ts(sm[:, 2:4], sm[:, 6:8], 1.0 / D, ALU.mult, ROT_EPS, ALU.add))
                ch.sync()
                dve.reciprocal(sm[:, 2:4], sm[:, 2:4]).then_inc(S(f"{tag}_var"), 1)
                dve.wait_ge(*nth(f"{tag}_rstd", 1))

            def norm_x(tag):
                norm(tag)
                for t in range(NT):
                    ts(xn[:, t, :], x[:, t, :], sm[:, 4 + t:5 + t], ALU.mult).then_inc(S(f"{tag}_xn"), 1)

            def hT_copy(tag, scale=None, bias=None):
                for c in (2, 3, 6, 7):
                    dve.wait_ge(*nth(f"{tag}_xT", c // 2 + 1))
                    src = pair(4 + c // 2)[:, c % 2, :]
                    if scale is None:
                        ins = dve.tensor_copy(hT[:, c, :], src)
                    else:
                        ins = ts(hT[:, c, :], src, scale[:, c:c + 1], ALU.mult,
                                 bias[:, c:c + 1], ALU.add)
                    ins.then_inc(S(f"{tag}_hT_dve"), 1)

            def split(n, more=0):
                for h in range(2):
                    dve.wait_ge(S("high_parts"), halves(n) - 1 + h + 12 * more)
                    hi, lo = half(n, h)
                    TT(lo, slot(n)[:, h * HALF:(h + 1) * HALF], hi.bitcast(f32), ALU.subtract)\
                        .then_inc(S("halves_split"), 1)

            def splits(first, last):
                for n in range(first, last + 1):
                    split(n)

            def hT_low(tag):
                for b in range(4):
                    dve.wait_ge(*nth(f"{tag}_hi", b + 1))
                    c = slice(2 * b, 2 * b + 2)
                    TT(hlo[:, c, :], hT[:, c, :], hhi[:, c, :].bitcast(f32), ALU.subtract)\
                        .then_inc(S(f"{tag}_lo"), 1)

            def mod_columns(l, turn, sublayers, b):
                bias = colA[:, 0:48] if l == 0 else colB[:, 0:48]
                dve.wait_ge(S("modc_ready"), turn)
                for s_ in sublayers:
                    c = slice(24 * s_, 24 * s_ + 16)
                    ch(TT(modc[:, c], bank[b][:, c], bias[:, c], ALU.add))
                ch.sync()
                for s_ in sublayers:
                    at = R_NG + (2 * l + s_) * NC
                    ins = stt(ng[:, s_, :], modc[:, 24 * s_ + 8:24 * s_ + 16], 1.0, colA[:, at:at + NC],
                              ALU.add, ALU.mult)
                    if s_ != sublayers[-1]:
                        ch(ins)
                ins.then_inc(S("ng_ready"), 1)
                dve.wait_ge(S("ng_ready"), turn)

            def mod_gates(l, b):
                dve.wait_ge(S("modg_ready"), l + 1)
                dve.wait_ge(S("gbc_landed"), 32 * (l + 1))
                for n in range(2):
                    for h in range(2):
                        v = gbc[:, n, h * 512:(h + 1) * 512]
                        ins = TT(v, v, bank[b + 2 * n + h][:, :], ALU.add)
                        if n * h == 0:
                            ch(ins)
                ins.then_inc(S("mod_done"), 1)
                dve.wait_ge(S("mod_done"), l + 1)

            def ada_rest_part(q):
                k, part = divmod(q, 4)
                dve.wait_ge(S(f"ada_rest_landed{q % 2}"), 16 * (q // 2 + 1))
                o = acc[:, UNIT + part * HALF:UNIT + (part + 1) * HALF]
                if k == 0:
                    ins = ts(o, ada_rest[:, q % 2, :], csil[:, 0:1], ALU.mult)
                else:
                    dve.wait_ge(S("ada0_rest"), q - 3)
                    ins = stt(o, ada_rest[:, q % 2, :], csil[:, k:k + 1], o, ALU.mult, ALU.add)
                ins.then_inc(S("ada0_rest"), 1)

            def rotate(tag, spans, tables, units=()):
                units = list(units)
                for c, nh in spans:
                    for t in range(NT):
                        hv = z[:, t, c:c + 64 * nh].rearrange("p (h d) -> p h d", d=64)
                        x1, x2 = hv[:, :, 0:ROT], hv[:, :, ROT:2 * ROT]
                        co, si = (v[:, t, :].unsqueeze(1).broadcast_to([P, nh, ROT]) for v in tables)
                        tmp = [rt[:, k, 0:8 * nh].rearrange("p (h d) -> p h d", d=ROT) for k in range(4)]
                        ch.sync()
                        ch(TT(tmp[0], x1, co, ALU.mult))
                        ch(TT(tmp[1], x2, si, ALU.mult))
                        ch(TT(tmp[2], x2, co, ALU.mult))
                        ch(TT(tmp[3], x1, si, ALU.mult))
                        ch.sync()
                        ch(TT(x1, tmp[0], tmp[1], ALU.subtract))
                        ch(TT(x2, tmp[2], tmp[3], ALU.add))
                        for n in units[:2]:
                            split(n)
                        units = units[2:]
                for n in units:
                    split(n)
                ch.sync()
                dve.tensor_copy(sm[:, 62:63], sm[:, 4:5]).then_inc(S(f"{tag}_roped"), 1)

            def attend(tag):
                jobs, units, ends = attention(tag)
                J = len(jobs)
                for j in range(J + 5):
                    if j < J:
                        dve.wait_ge(*nth(f"{tag}_scores", j + 1))
                        ch(dve.tensor_reduce(out=nmax[:, j % 4, 0:1], in_=bank[j % 4][:, 0:P], axis=X,
                                             op=ALU.max, negate=True))
                        dve.tensor_reduce(out=nmax[:, j % 4, 1:2], in_=bank[j % 4][:, P:384], axis=X,
                                          op=ALU.max, negate=True).then_inc(S(f"{tag}_max"), 1)
                    if j - 1 in ends:
                        U = units[ends[j - 1]]
                        dve.wait_ge(*nth(f"{tag}_exp", j))
                        for jj in U["jobs"]:
                            ch(dve.reciprocal(rsum[:, jj % 4, :], psum_[:, jj % 4, :]))
                        ch.sync()
                        b0 = U["jobs"][0] % 4
                        if tag == "a0":
                            b1 = U["jobs"][1] % 4
                            ch(ts(rsum[:, b1, :], rsum[:, b1, :], sm[:, 14:15], ALU.mult))
                        if tag == "a1":
                            gv = gate[:, :, 3 * U["h"] + 1 + U["w"]:3 * U["h"] + 2 + U["w"]]
                            ch(TT(rsum[:, b0, :], rsum[:, b0, :], gv.rearrange("p t o -> p (t o)"), ALU.mult))
                            ch.sync()
                        for t, (a, b) in enumerate(((0, P), (P, 384))):
                            ins = ts(prob[:, b0, a:b], prob[:, b0, a:b], rsum[:, b0, t:t + 1], ALU.mult)
                            if tag == "a0" or t == 0:
                                ch(ins)
                        if tag == "a0":
                            ch.sync()
                            for t, (a, b) in enumerate(((0, P), (P, 384))):
                                ins = stt(prob[:, b0, a:b], prob[:, b1, a:b], rsum[:, b1, t:t + 1],
                                          prob[:, b0, a:b], ALU.mult, ALU.add)
                                if t == 0:
                                    ch(ins)
                        ins.then_inc(S(f"{tag}_norm"), 1)
                        if tag == "a0":
                            ada_rest_part(24 + ends[j - 1])
                    if j - 4 in ends and units[ends[j - 4]]["last"]:
                        u = ends[j - 4]
                        G = units[u]["group"]
                        dve.wait_ge(*nth(f"{tag}_pv", u + 1))
                        dve.tensor_copy(oT[:, G, :], bank[6 + G % 2][:, 0:SEQ]).then_inc(S(f"{tag}_o"), 1)

            def gated_residual(tag, n):
                hT_low("o" + tag)
                for j in range(4):
                    split(N_OUT[tag] + j + 2)
                    dve.wait_ge(*nth(f"{tag}_out_done", j + 1))
                    gv = gbc[:, n, 256 * j:256 * j + 256].unsqueeze(1).broadcast_to([P, NT, 256])
                    ch(TT(xn[:, :, 256 * j:256 * j + 256], pair(4 + j)[:, :, :], gv, ALU.mult))
                    ch.sync()
                    ins = TT(x[:, :, 256 * j:256 * j + 256], x[:, :, 256 * j:256 * j + 256],
                             xn[:, :, 256 * j:256 * j + 256], ALU.add)
                    if j < 3:
                        ch(ins)
                ins.then_inc(S(f"{tag}_x_done"), 1)
                dve.wait_ge(*nth(f"{tag}_x_done", 1))

            def route(l):
                dve.wait_ge(*nth("logits_done", l + 1))
                dve.wait_ge(*nth("router_landed", 7 * 16 * (l + 1)))
                lv = bank[6][:, 0:128].rearrange("p (t n) -> p t n", t=NT)[:, :, 0:36]
                TT(lg[:, :, :], lv, rb[:, :].unsqueeze(1).broadcast_to([P, NT, 36]), ALU.add)\
                    .then_inc(S("logits_read"), 1)
                dve.wait_ge(*nth("logits_read", l + 1))

                def R(k, n):
                    return rs[:, k, 0:NT * n].rearrange("p (t n) -> p t n", t=NT)

                def col(k, at=0):
                    return rs[:, k, at:at + NT].rearrange("p (t o) -> p t o", o=1)

                def step(ins):
                    ch(ins)
                    ch.sync()

                def first_max(o, v, n, rev, sc, m, r):
                    step(dve.tensor_reduce(out=m, in_=v, axis=X, op=ALU.max))
                    step(TT(sc, v, m.broadcast_to([P, NT, n]), ALU.is_ge))
                    step(TT(sc, sc, cst[:, rev:rev + n].unsqueeze(1).broadcast_to([P, NT, n]), ALU.mult))
                    step(dve.tensor_reduce(out=r, in_=sc, axis=X, op=ALU.max))
                    step(TT(o, sc, r.broadcast_to([P, NT, n]), ALU.is_equal))

                lgrp, lexp = lg[:, :, 0:4], lg[:, :, 4:36]
                first_max(R(1, 4), lgrp, 4, C_R4, R(2, 4), col(9, 0), col(9, 2))
                step(TT(R(5, 4), lgrp, col(9, 0).broadcast_to([P, NT, 4]), ALU.subtract))
                oh = rs[:, 1, 0:8].rearrange("p (t g o) -> p t g o", t=NT, o=1).broadcast_to([P, NT, 4, 8])
                ohx = rs[:, 2, 0:64].rearrange("p (t g o) -> p t g o", t=NT, g=4)
                step(dve.tensor_copy(ohx, oh))
                step(TT(R(3, 32), lexp, R(2, 32), ALU.mult))
                step(ts(R(2, 32), R(2, 32), 1.0, ALU.subtract, -NEG, ALU.mult))
                step(TT(R(3, 32), R(3, 32), R(2, 32), ALU.add))
                first_max(R(4, 32), R(3, 32), 32, C_R32, R(7, 32), col(9, 4), col(9, 6))
                step(stt(R(3, 32), R(4, 32), 3.0 * NEG, R(3, 32), ALU.mult, ALU.add))
                first_max(R(8, 32), R(3, 32), 32, C_R32, R(7, 32), col(9, 8), col(9, 10))
                TT(rs[:, 5, 8:10], rs[:, 9, 8:10], rs[:, 9, 4:6], ALU.subtract).then_inc(S("route_diff"), 1)
                dve.wait_ge(*nth("route_exp", 2 * (l + 1)))
                step(dve.tensor_reduce(out=col(9, 12), in_=rs[:, 6, 0:8].rearrange("p (t n) -> p t n", t=NT),
                                       axis=X, op=ALU.add))
                step(stt(rs[:, 9, 14:16], rs[:, 6, 8:10], 1.0, rs[:, 9, 12:14], ALU.add, ALU.mult))
                step(dve.reciprocal(rs[:, 9, 16:18], rs[:, 9, 14:16]))
                step(TT(rs[:, 9, 18:20], rs[:, 9, 16:18], rs[:, 6, 8:10], ALU.mult))
                step(TT(R(4, 32), R(4, 32), col(9, 16).broadcast_to([P, NT, 32]), ALU.mult))
                step(TT(R(8, 32), R(8, 32), col(9, 18).broadcast_to([P, NT, 32]), ALU.mult))
                TT(R(0, 32), R(4, 32), R(8, 32), ALU.add).then_inc(S("combine_ready"), 1)

            def combine_rows(l):
                dve.wait_ge(*nth("combine_turned", l + 1))
                if l:
                    dve.wait_ge(*nth("combine_stored", 16 * l))
                dve.tensor_copy(cbT[:, :], bank[0][0:32, 0:SEQ]).then_inc(S("combine_rows_ready"), 1)

            def experts(tag):
                l, count = int(tag[1]), COUNT[tag]

                def activated(e, i=0, wait=True):
                    b = e % 2
                    if tag[0] == "m":
                        used(dve, unit_up(tag, e, 1), i)
                        row = cmb[:, ds(i * 2 + e, 1), :].broadcast_to([P, 2, SEQ])
                        TT(upc[:, b, :].rearrange("p (c n) -> p c n", c=2), pair(5 + 2 * b)[:, :, :], row,
                           ALU.mult).then_inc(S(f"{tag}_upc"), 1)
                        dve.wait_ge(*nth(f"{tag}_upc", i * 2 + e + 1))
                        value = upc[:, b, :]
                    else:
                        convolve(e, i)
                        value = cvt[:, b, 2:4, :].rearrange("p c n -> p (c n)")
                    dve.wait_ge(*nth(f"{tag}_silu", i * 2 + e + 1))
                    TT(upc[:, b, :], sil[:, b, :], value, ALU.mult).then_inc(S(f"{tag}_prod"), 1)
                    dve.wait_ge(*nth(f"{tag}_prod", i * 2 + e + 1))
                    if wait:
                        used(dve, unit_down(tag, e - 2), i)
                    dve.tensor_copy(ahi[:, b, :], upc[:, b, :]).then_inc(S(f"{tag}_ahi"), 1)
                    dve.wait_ge(S(f"{tag}_ahi"), i * 2 + e + 1)
                    TT(alo[:, b, :], upc[:, b, :], ahi[:, b, :].bitcast(f32), ALU.subtract)\
                        .then_inc(S(f"{tag}_aT"), 1)

                def convolve(e, i=0):
                    dve.wait_ge(*nth(f"{tag}_taps", i * 2 + e + 1))
                    for tap, sh in ((1, 1), (0, 2)):
                        for c in range(4):
                            src = pair(4 + 2 * (e % 2) + c // 2)[:, c % 2, 0:SEQ - sh]
                            o = cvt[:, e % 2, c, sh:SEQ]
                            if tap == 1:
                                dve.wait_ge(*nth(f"{tag}_tap2", i * 8 + (4 * e + 2 * (c // 2) + 2)))
                            else:
                                dve.wait_ge(*nth(f"{tag}_tap1", i * 8 + (4 * e + c + 1)))
                            ins = stt(o, src, cvcur[:, e % 2, tap, c:c + 1], o, ALU.mult, ALU.add)
                            if tap == 1:
                                ins.then_inc(S(f"{tag}_tap1"), 1)
                            elif c in (1, 3):
                                ins.then_inc(S(f"{tag}_conv" if c == 1 else f"{tag}_conv_value"), 1)
                    dve.wait_ge(*nth(f"{tag}_conv_value", i * 2 + e + 1))

                def taps(e, i=0):
                    if tag[0] == "m":
                        return
                    for half_ in range(2):
                        src = cvc[:, :, ds(i * 4 + (2 * e + 22 * half_), 2)]
                        ins = dve.tensor_copy(cvcur[:, e % 2, :, 2 * half_:2 * half_ + 2], src)
                        ins.then_inc(S(f"{tag}_taps" if half_ else f"{tag}_taps_gate"), 1)

                def ada1(u, turn, block):
                    if tag != "m0":
                        return
                    for k in range(4):
                        b = k // 2
                        if k % 2 == 0:
                            dve.wait_ge(S(f"ada1_landed{b}"), turn * 32 + (16 * u + 16))
                        c = csil[:, 4 * u + k:4 * u + k + 1]
                        if k or u:
                            dve.wait_ge(S("ada1_step"), turn * 7 + (4 * u + k))
                        if u == 1 and k == 3:
                            o, sem = acc[:, ds(block * 384, 384)], "ada1_done"
                        else:
                            o, sem = adat[:, :], "ada1_step"
                        if k == 0 and u == 0:
                            if not isinstance(turn, int):
                                dve.wait_ge(S("ada1_done"), turn)
                            ins = ts(o, adaw[:, b, k % 2, :], c, ALU.mult)
                        else:
                            ins = stt(o, adaw[:, b, k % 2, :], c, adat[:, :], ALU.mult, ALU.add)
                        ins.then_inc(S(sem), 1)
                        if k % 2:
                            dve.tensor_copy(sm[:, 50:51], adaw[:, b, 1, 0:1]).then_inc(S("ada1_used"), 1)

                def step(e, i=0):
                    ada1(e % 2, i + 1, i)
                    for k in range(3):
                        split(unit_down(tag, e) + 2 + k, i)
                    taps(e + 2, i)
                    activated(e + 2, i)

                first = N_EXP[tag]
                split(first + 2)
                split(first + 3)
                if tag[0] == "m":
                    combine_rows(l)
                    dve.wait_ge(*nth("combine_landed", 16 * (l + 1)))
                taps(0)
                activated(0, wait=False)
                split(first + 4)
                split(first + 5)
                taps(1)
                activated(1, wait=False)
                ada1(0, 0, 15)
                ada1(1, 0, 15)
                with dve.Fori(0, (count - 2) // 2) as i:
                    step(0, i)
                    step(1, i)
                if count % 2:
                    step(count - 3)
                for e in (count - 2, count - 1):
                    if unit_down(tag, e) + 2 < N_END:
                        split(unit_down(tag, e) + 2)
                if tag == "m0":
                    mod_columns(1, 3, (0, 1), 4)
                used(dve, unit_down(tag, count - 1))
                for t in range(NT):
                    for h in range(2):
                        v = (xn if tag[0] == "m" else x)[:, t, h * 512:(h + 1) * 512]
                        if tag[0] == "m":
                            ch(TT(v, bank[2 * t + h][:, :], gbc[:, 1, h * 512:(h + 1) * 512], ALU.mult))
                        else:
                            ch(stt(v, v, ALPHA, bank[2 * t + h][:, :], ALU.mult, ALU.add))
                ch.sync()
                if tag[0] == "m":
                    TT(x[:, :, :], x[:, :, :], xn[:, :, :], ALU.add).then_inc(S(f"{tag}_x_done"), 1)
                    dve.wait_ge(*nth(f"{tag}_x_done", 1))

            experts_m = experts_f = experts

            def layer_norm(tag, l):
                name = f"{tag}_{l}"
                for t in range(NT):
                    for h in range(2):
                        ch(dve.bn_stats(out=stat[:, t, h, :], in_=x[:, t, h * 512:(h + 1) * 512]))
                ch.sync()
                for t in range(NT):
                    ch(dve.bn_aggr(out=mv[:, t, :], in_=stat[:, t, :, :]))
                ch.sync()
                ch(ts(sm[:, 2:4], mv[:, :, 1], LN_EPS, ALU.add))
                ch.sync()
                dve.reciprocal(sm[:, 2:4], sm[:, 2:4]).then_inc(S(f"{name}_var"), 1)
                dve.wait_ge(*nth(f"{name}_rstd", 1))
                dve.wait_ge(*nth(f"{tag}{l}_landed", 32))
                for t in range(NT):
                    v = x[:, t, :]
                    ch(ts(v, v, mv[:, t, 0:1], ALU.subtract, sm[:, 4 + t:5 + t], ALU.mult))
                    ch.sync()
                    ch(TT(v, v, gbc[:, 0, :], ALU.mult))
                    ch.sync()
                    TT(v, v, gbc[:, 1, :], ALU.add).then_inc(S(f"{name}_tile"), 1)
                dve.wait_ge(*nth(f"{name}_tile", 2))
                dve.tensor_copy(sm[:, 60:61], sm[:, 4:5]).then_inc(S(f"{name}_done"), 1)

            dve.wait_ge(*nth("lam_landed", 16))
            for n in range(2):
                ch(TT(rt[:, n, 0:64], lamt[:, 2 * n, :], lamt[:, 2 * n + 1, :], ALU.mult))
            ch.sync()
            dve.tensor_reduce(out=sm[:, 10:12], in_=rt[:, 0:2, 0:64], axis=X, op=ALU.add)\
                .then_inc(S("lam_dots"), 1)
            dve.wait_ge(*nth("pos_landed", 32))
            dve.wait_ge(*nth("const_landed", 16))
            ch(dve.tensor_copy(idb[:, :], ident))
            dve.tensor_copy(maskh[:, :], maskb).then_inc(S("mask_ready"), 1)
            ch(dve.tensor_copy(sm[:, 8:10], posi[:, :]))
            ch.sync()

            def step(ins):
                ch(ins)
                ch.sync()

            ang, k_, r_, rc = rope[:, 4, :], rope[:, 5, :], rope[:, 3, :], rope[:, 2, :]
            for t in range(NT):
                step(ts(ang[:, 8 * t:8 * t + 8], cst[:, C_INV:C_INV + 8], sm[:, 8 + t:9 + t], ALU.mult))
            step(ts(k_, ang, 1.0 / (2 * np.pi), ALU.mult, 12582912.0, ALU.add))
            step(ts(k_, k_, 12582912.0, ALU.subtract))
            c1 = 6.28125
            c2 = float(np.floor((2 * np.pi - c1) * 2 ** 21) / 2 ** 21)
            c3 = float(np.float32(2 * np.pi - c1 - c2))
            step(stt(r_, k_, -c1, ang, ALU.mult, ALU.add))
            step(stt(r_, k_, -c2, r_, ALU.mult, ALU.add))
            step(stt(r_, k_, -c3, r_, ALU.mult, ALU.add))
            lim = 3.1415925
            step(ts(rc, r_, float(np.pi / 2), ALU.add))
            step(ts(k_, rc, float(np.pi), ALU.is_gt))
            step(stt(rc, k_, float(-2 * np.pi), rc, ALU.mult, ALU.add))
            ts(rope[:, 2:4, :], rope[:, 2:4, :], lim, ALU.min, -lim, ALU.max).then_inc(S("angles"), 1)
            dve.wait_ge(*nth("lam_exp", 1))
            step(TT(sm[:, 14:15], sm[:, 13:14], sm[:, 12:13], ALU.subtract))
            step(ts(sm[:, 14:15], sm[:, 14:15], LAMBDA_INIT, ALU.subtract))
            dve.wait_ge(*nth("cols_turned", 1))
            ch(dve.tensor_copy(colA[:, :], bank[7][:, 0:R_END]))
            ch(dve.tensor_copy(colB[:, :], bank[7][:, P:P + 80]))
            ch.sync()
            step(ts(colA[:, R_SUB:R_SUB + 1], colA[:, R_SUB:R_SUB + 1], 1.0 - LAMBDA_INIT, ALU.mult))
            dve.wait_ge(*nth("csil_ready", 1))
            for k in range(NC):
                landed(dve, k)
                o = acc[:, 0:UNIT]
                if k == 0:
                    ins = ts(o, slot(k), csil[:, 0:1], ALU.mult)
                else:
                    dve.wait_ge(S("ada0_done"), k)
                    ins = stt(o, slot(k), csil[:, k:k + 1], o, ALU.mult, ALU.add)
                ins.then_inc(S("ada0_done"), 1)
            splits(FIRST, FIRST + 1)
            norm_x("a0")
            mod_columns(0, 1, (0,), 7)
            hT_copy("a0", ng[:, 0, :], modc[:, 0:8])
            hT_low("a0")
            for k in range(8):
                split(FIRST + 2 + k)
                if k:
                    ada_rest_part(2 * k - 2)
                    ada_rest_part(2 * k - 1)
            dve.wait_ge(*nth("rope_ready", 1))
            dve.wait_ge(*nth("a0_z", 8))
            tables = [rope[:, n, :].rearrange("p (t d) -> p t d", t=NT) for n in range(2)]
            split(FIRST + 10)
            rotate("a0", [(0, 32)], tables, [FIRST + 11, FIRST + 12, FIRST + 13])
            for q in range(14, 24):
                ada_rest_part(q)
            dve.wait_ge(*nth("a0_z", 12))
            attend("a0")
            mod_columns(0, 2, (1,), 0)
            mod_gates(0, 4)
            dve.wait_ge(*nth("a0_o", 8))
            oF = oT[:, :, :].rearrange("p c n -> p (c n)")
            xF = xn[:, :, :].rearrange("p t n -> p (t n)")
            TT(xF, oF, oF, ALU.mult).then_inc(S("sub_sq"), 1)
            dve.wait_ge(*nth("sub_sum", 1))
            for b in range(4):
                ch(ts(xF[:, b * 512:(b + 1) * 512], bank[b][:, :], 1.0 / P, ALU.mult, ROT_EPS, ALU.add))
            ch.sync()
            dve.reciprocal(xF, xF).then_inc(S("sub_var"), 1)
            dve.wait_ge(*nth("sub_rstd", 1))
            stt(oF, oF, colA[:, R_SUB:R_SUB + 1], xF, ALU.mult, ALU.mult).then_inc(S("a0_oT"), 1)
            gated_residual("a0", 0)
            norm_x("m0")
            hT_copy("m0", ng[:, 1, :], modc[:, 24:32])
            hT_low("m0")
            route(0)
            experts_m("m0")
            norm_x("a1")
            hT_copy("a1", ng[:, 0, :], modc[:, 0:8])
            hT_low("a1")
            mod_gates(1, 0)
            u = N_IN["a1"]
            splits(u + 2, u + 5)
            dve.wait_ge(*nth("a1_z", 4))
            rotate("a1", [(1280, 8)], tables, [u + 6])
            for w in range(2):
                for g_ in range(2):
                    src = z[:, :, 1280 + 256 * w + 64 * g_:1344 + 256 * w + 64 * g_]
                    for dup in range(2):
                        ch(dve.tensor_copy(kd[:, :, 2 * w + g_, 64 * dup:64 * dup + 64], src))
            split(u + 7)
            dve.wait_ge(*nth("gate_exp", 1))
            step(ts(gate[:, :, :], gate[:, :, :], 1.0, ALU.add))
            step(dve.reciprocal(gate[:, :, :], gate[:, :, :]))
            dve.wait_ge(*nth("cmp_split", 1))
            for v in range(2):
                for g_ in range(2):
                    xv = bank[0][:, (v * 2 + g_) * 128:(v * 2 + g_) * 128 + 128].rearrange("p (n j) -> p j n", j=8)
                    for jh in range(2):
                        pv = colB[:, 48 + v * 16 + 8 * jh:56 + v * 16 + 8 * jh].unsqueeze(2).broadcast_to([P, 8, 15])
                        ins = TT(blk[:, v, 8 * jh:8 * jh + 8, 15 * g_:15 * g_ + 15], xv[:, :, jh:jh + 15], pv, ALU.add)
                        if (g_, jh) != (1, 1):
                            ch(ins)
                ins.then_inc(S("blk_ready"), 1)
            splits(u + 8, u + 12)
            dve.wait_ge(*nth("cmp_kv", 1))
            ch(dve.tensor_copy(kcT, bank[2][:, 0:30]))
            dve.tensor_copy(vc[0:15, :, :], bank[2][0:15, 64:192].rearrange("p (g d) -> p g d", g=2))\
                .then_inc(S("cmp_kv_read"), 1)
            split(u + 13)
            dve.wait_ge(*nth("vc_spread", 1))
            for g_ in range(2):
                src = bank[3][:, g_ * 64:g_ * 64 + 64].unsqueeze(1).broadcast_to([P, 8, 64])
                msk = cst[:, C_BLK:C_BLK + 8].unsqueeze(2).broadcast_to([P, 8, 64])
                ins = TT(vblk[:, g_, :, :], src, msk, ALU.mult)
                if g_ == 0:
                    ch(ins)
            ins.then_inc(S("vblk_ready"), 1)
            dve.wait_ge(*nth("a1_z", 8))
            rotate("a1", [(0, 16)], tables)
            ch(dve.memset(pc[:, :, :, CMP_N:16], 0.0))
            dve.wait_ge(*nth("cmp_scores", 1))
            pch = pc.rearrange("p t (h a) n -> p t h a n", a=2)
            for par in range(2):
                src = bank[4 + par][:, 0:256].rearrange("p (t h n) -> p t h n", t=NT, h=8)
                for t in range(NT):
                    mk = cst[:, C_CB + CMP_N * t:C_CB + CMP_N * (t + 1)].unsqueeze(1).broadcast_to([P, 8, CMP_N])
                    ch(TT(pch[:, t, :, par, 0:CMP_N], src[:, t, :, 0:CMP_N], mk, ALU.add))
            ch.sync()
            pcm = pc.rearrange("p t h n -> p (t h) n")[:, :, 0:CMP_N]
            step(dve.tensor_reduce(out=cms[:, 0, :], in_=pcm, axis=X, op=ALU.max))
            TT(pcm, pcm, cms[:, 0, :].unsqueeze(2).broadcast_to([P, 32, CMP_N]), ALU.subtract)\
                .then_inc(S("pc_diff"), 1)
            dve.wait_ge(*nth("pc_exp", 1))
            for t in range(NT):
                mk = cst[:, C_C01 + CMP_N * t:C_C01 + CMP_N * (t + 1)].unsqueeze(1).broadcast_to([P, 16, CMP_N])
                ch(TT(pc[:, t, :, 0:CMP_N], pc[:, t, :, 0:CMP_N], mk, ALU.mult))
            ch.sync()
            step(dve.tensor_reduce(out=cms[:, 1, :], in_=pcm, axis=X, op=ALU.add))
            step(ts(cms[:, 1, :], cms[:, 1, :], 1e-30, ALU.max))
            step(dve.reciprocal(cms[:, 2, :], cms[:, 1, :]))
            for t in range(NT):
                gv = gate[:, t, :].rearrange("p (h a) -> p h a", a=3)[:, :, 0]
                ch(TT(cms[:, 3, 16 * t:16 * t + 16], cms[:, 2, 16 * t:16 * t + 16], gv, ALU.mult))
            ch.sync()
            TT(pcm, pcm, cms[:, 3, :].unsqueeze(2).broadcast_to([P, 32, CMP_N]), ALU.mult)\
                .then_inc(S("pc_ready"), 1)
            attend("a1")
            gated_residual("a1", 0)
            norm_x("m1")
            hT_copy("m1", ng[:, 1, :], modc[:, 24:32])
            hT_low("m1")
            route(1)
            experts_m("m1")
            norm("first")
            dve.wait_ge(*nth("final_landed", 16))
            for t in range(NT):
                stt(x[:, t, :], x[:, t, :], sm[:, 4 + t:5 + t], gbc[:, 0, :], ALU.mult, ALU.mult)\
                    .then_inc(S("first_tile"), 1)
            dve.wait_ge(*nth("first_tile", 2))
            dve.tensor_copy(sm[:, 61:62], sm[:, 4:5]).then_inc(S("first_done"), 1)
            tables2 = [cst[:, c:c + 16].rearrange("p (t d) -> p t d", t=NT) for c in (C_COS, C_SIN)]
            for l in range(2):
                tag, ffn = f"s{l}", f"f{l}"
                hT_copy(tag)
                hT_low(tag)
                splits(N_IN[tag] + 2, N_IN[tag] + 11)
                dve.wait_ge(*nth(f"{tag}_z", 10))
                dve.wait_ge(*nth("mix_landed", 6 * 16 * (l + 1)))
                step(TT(fox[:, 0, :].rearrange("p (t h) -> p t h", t=NT), z[:, :, 1536:1540],
                        bfor[:, :].unsqueeze(1).broadcast_to([P, NT, 4]), ALU.add))
                stt(fox[:, 1, :], fox[:, 0, :], -1.0, fox[:, 0, :], ALU.mult, ALU.max).then_inc(S("absf"), 1)
                dve.wait_ge(*nth("ln1p", l + 1))
                step(ts(fox[:, 0, :], fox[:, 0, :], 0.0, ALU.min))
                TT(fox[:, 3, :], fox[:, 0, :], fox[:, 2, :], ALU.subtract).then_inc(S("logf_ready"), 1)
                dve.wait_ge(*nth("sgw_turned", l + 1))
                step(TT(sgwT, bank[3][:, :].rearrange("p (g n) -> p g n", g=4),
                        tri.unsqueeze(1).broadcast_to([P, 4, P]), ALU.mult))
                dve.wait_ge(*nth("conv_turned", l + 1))
                step(dve.tensor_copy(cvc, bank[2][:, 0:176].rearrange("p (w n) -> p w n", w=4)))
                dve.wait_ge(*nth("cum_done", l + 1))
                ch(dve.tensor_copy(cum[:, 0, :], bank[1][0:4, 0:SEQ]))
                ch(ts(cum[:, 1, :], bank[1][0:4, 0:SEQ], -1.0, ALU.mult))
                dve.wait_ge(*nth("pooled", l + 1))
                dve.tensor_copy(pool, pair(0)[:, :, :]).then_inc(S("pool_ready"), 1)
                dve.wait_ge(*nth("gelu", 2 * l + 1))
                vv = z[:, :, 1796:2052].rearrange("p t (g c) -> p t g c", g=4)
                sq = sgt.rearrange("p t (g c) -> p t g c", g=4)

                def per(at, n=64):
                    return sm[:, at:at + 8].rearrange("p (t g o) -> p t g o", t=NT, o=1)\
                        .broadcast_to([P, NT, 4, n])

                step(dve.tensor_reduce(out=sm[:, 16:24], in_=vv, axis=X, op=ALU.add))
                step(ts(sm[:, 16:24], sm[:, 16:24], 1.0 / 64, ALU.mult))
                step(TT(vv, vv, per(16), ALU.subtract))
                step(TT(sq, vv, vv, ALU.mult))
                step(dve.tensor_reduce(out=sm[:, 24:32], in_=sq, axis=X, op=ALU.add))
                step(ts(sm[:, 24:32], sm[:, 24:32], 1.0 / 64, ALU.mult, LN_EPS, ALU.add))
                dve.reciprocal(sm[:, 32:40], sm[:, 24:32]).then_inc(S("sg_var"), 1)
                dve.wait_ge(*nth("sg_rstd", l + 1))
                step(TT(vv, vv, per(40), ALU.mult))
                vt = z[:, :, 1796:2052]
                step(TT(vt, vt, sgl[:, 0, :].unsqueeze(1).broadcast_to([P, NT, 256]), ALU.mult))
                TT(vt, vt, sgl[:, 1, :].unsqueeze(1).broadcast_to([P, NT, 256]), ALU.add)\
                    .then_inc(S("sgv_ready"), 1)
                rotate(tag, [(0, 8)], tables2)
                dve.wait_ge(*nth("gelu", 2 * l + 2))
                dve.wait_ge(*nth("sg_mixed", l + 1))
                for g_ in range(4):
                    at = R_SB + 4 * l + g_
                    c = slice(64 * g_, 64 * g_ + 64)
                    ins = stt(sgt[:, :, c], pair(4)[:, :, c], colA[:, at:at + 1],
                              z[:, :, 1540 + 64 * g_:1604 + 64 * g_], ALU.add, ALU.mult)
                    if g_ < 3:
                        ch(ins)
                ins.then_inc(S("sgy_ready"), 1)
                dve.wait_ge(*nth("pool_mixed", l + 1))
                for c in range(2):
                    at = R_PS + 2 * l + c
                    ch(ts(oT[:, 6 + c, :], pair(0)[:, c, :], colA[:, at:at + 1], ALU.mult))
                dve.wait_ge(*nth("sg_turned", l + 1))
                dve.tensor_copy(oT[:, 4:6, :], pair(5)[:, :, :]).then_inc(S("mix_read"), 1)
                attend(tag)
                hT_low("o" + tag)
                for j in range(4):
                    split(N_OUT[tag] + j + 2)
                    dve.wait_ge(*nth(f"{tag}_out_done", j + 1))
                    v = x[:, :, 256 * j:256 * j + 256]
                    ch(stt(v, v, ALPHA, pair(4 + j)[:, :, :], ALU.mult, ALU.add))
                ch.sync()
                layer_norm("ln1", l)
                hT_copy(ffn)
                hT_low(ffn)
                experts_f(ffn)
                layer_norm("ln2", l)


_UNUSED = ()


def kernel(**inputs):
    import concourse.bacc as _bacc
    from concourse.bass_utils import run_bass_kernel_spmd as _run

    nc = _bacc.Bacc("TRN2", target_bir_lowering=False, num_devices=1)
    arrays, aps = {}, {}
    inputs = dict(inputs)
    for name, a in inputs.items():
        a = np.ascontiguousarray(a)
        arrays[f"in_{name}"] = a
        aps[name] = nc.dram_tensor(f"in_{name}", a.shape, mybir.dt.from_np(a.dtype), kind="ExternalInput").ap()
    c = constants()
    arrays["in_consts"] = c
    aps["consts"] = nc.dram_tensor("in_consts", c.shape, mybir.dt.float32, kind="ExternalInput").ap()
    out = nc.dram_tensor("out_x", (1, SEQ, D), mybir.dt.float32, kind="ExternalOutput").ap()
    build(nc, aps, out)
    r = _run(nc, [arrays], core_ids=[0])
    return r.results[0]["out_x"]
```

```python
from contextlib import ExitStack

import numpy as np
import concourse.bass as bass
from concourse import mybir

SEQ, D, P = 256, 1024, 128
NT, NC = SEQ // P, D // P
ROT = 8
EXPERTS, GROUPS, PER_GROUP, HID = 32, 4, 8, 256
FF = 2816
FF_GROUPS = FF // HID
NSA_IN, IN2 = 1840, 2308
CMP_N = 15
ROT_EPS, LN_EPS = 1e-6, 1e-5
ALPHA = 4.0 ** 0.25
LAMBDA_INIT = 0.2
NEG = -1e30
SLOTS, UNIT = 3, 2048
HALF = UNIT // 2

C_ID, C_TRI, C_ONE, C_MASK, C_EVEN = 0, 128, 256, 384, 512
C_CB, C_C01, C_R4, C_R32, C_INV = 640, 670, 700, 704, 736
C_COS, C_SIN, C_REP, C_BLK, C_PICK, C_BAND, C_END = 744, 760, 776, 904, 912, 928, 2976
R_ADAB, R_NG, R_C, R_SUB, R_B1, R_PS, R_SB, R_END = 0, 48, 80, 88, 89, 93, 97, 105
N_ADA = 0
FIRST = 8
N_IN = {"a0": FIRST, "a1": FIRST + 16 + 96}
N_OUT = {"a0": FIRST + 12, "a1": N_IN["a1"] + 12}
N_CMP = N_IN["a1"] + 6
N_EXP = {"m0": FIRST + 16, "m1": N_OUT["a1"] + 4}
N_IN["s0"] = N_EXP["m1"] + 96
N_OUT["s0"] = N_IN["s0"] + 10
N_EXP["f0"] = N_OUT["s0"] + 4
N_IN["s1"] = N_EXP["f0"] + 3 * FF_GROUPS
N_OUT["s1"] = N_IN["s1"] + 10
N_EXP["f1"] = N_OUT["s1"] + 4
N_END = N_EXP["f1"] + 3 * FF_GROUPS
COUNT = {"m0": EXPERTS, "m1": EXPERTS, "f0": FF_GROUPS, "f1": FF_GROUPS}
COLS = {
    "a0": [(c, 256) for c in range(0, 3072, 256)],
    "a1": [(1024, 256), (1280, 256), (1536, 256), (1792, 48)] + [(c, 256) for c in range(0, 1024, 256)],
    "s0": [(1536, 256), (1792, 256), (2048, 256), (2304, 4)] + [(c, 256) for c in range(0, 1536, 256)],
}
COLS["s1"] = COLS["s0"]
ATT = ("a0", "a1", "s0", "s1")


def unit_in(tag, j):
    return N_IN[tag] + j + (4 if tag == "a1" and j >= 6 else 0)


def unit_up(tag, e, part, later=False):
    return N_EXP[tag] + (3 * e + part - 1 if e >= 1 or later else part)


def unit_down(tag, e):
    return N_EXP[tag] + 4 + 3 * e - (2 if e == COUNT[tag] - 1 else 0)


def halves(n):
    return 2 * (n - FIRST) + 2


def recurring():
    att = {"a0": 16, "a1": 32, "s0": 8, "s1": 8}
    units = {"a0": 8, "a1": 32, "s0": 8, "s1": 8}
    subs = ("a0", "m0", "a1", "m1", "s0", "f0", "s1", "f1")
    lns = ("first", "ln1_0", "ln2_0", "ln1_1", "ln2_1")
    r = {}
    r["z"] = {t: len(COLS[t]) for t in ATT}
    for kind in ("qkT", "qk"):
        r[kind] = {"a0": 8, "a1": 6, "s0": 4, "s1": 4}
    for kind in ("scores", "max", "exp"):
        r[kind] = att
    for kind in ("norm", "turned", "probT", "pv"):
        r[kind] = units
    r["o"] = {"a0": 8, "a1": 8, "s0": 4, "s1": 4}
    r["roped"] = {"a0": 1, "a1": 3, "s0": 1, "s1": 1}
    for kind in ("xT", "hT_act", "hT_dve"):
        r[kind] = {t: 4 for t in subs}
    for kind in ("aT", "silu", "prod"):
        r[kind] = COUNT
    r["upc"] = {"m0": EXPERTS, "m1": EXPERTS}
    for kind in ("taps", "taps_gate", "conv", "conv_value"):
        r[kind] = {"f0": FF_GROUPS, "f1": FF_GROUPS}
    for kind in ("tap1", "tap2"):
        r[kind] = {"f0": 4 * FF_GROUPS, "f1": 4 * FF_GROUPS}
    for kind in ("hi", "lo"):
        r[kind] = {t: 4 for t in ("a0", "oa0", "m0", "a1", "oa1", "m1", "s0", "os0", "f0", "s1", "os1", "f1")}
    norms = ("a0", "m0", "a1", "m1", "first")
    r["diag"] = {t: NT for t in norms}
    r["x_part"] = {t: 4 for t in norms[1:]}
    r["ssq"] = {"a0": 2, "m0": 8, "a1": 4, "m1": 8, "first": 4}
    for kind in ("var", "rstd"):
        r[kind] = {t: 1 for t in subs[:4] + lns}
    r["tile"] = {t: NT for t in lns[1:]}
    r["down_tile"] = {t: 1 for t in COUNT}
    r["done"] = {t: 1 for t in lns if t != "ln2_1"}
    return r


RECUR = recurring()


def split(name):
    parts = name.split("_")
    for n in range(1, len(parts)):
        tag, kind = "_".join(parts[:n]), "_".join(parts[n:])
        if kind in RECUR and tag in RECUR[kind]:
            return tag, kind
    return None, name


def constants():
    c = np.zeros((P, C_END), np.float32)
    i = np.arange(P)
    c[:, C_ID:C_ID + P] = np.eye(P)
    c[:, C_TRI:C_TRI + P] = i[:, None] <= i[None, :]
    c[:, C_ONE:C_ONE + P] = 1.0
    c[:, C_MASK:C_MASK + P] = np.where(i[None, :] <= i[:, None], 0.0, NEG)
    m = np.arange(64)
    for tp in range(2):
        c[:, C_EVEN + 64 * tp:C_EVEN + 64 * tp + 64] = i[:, None] == 2 * m[None, :] + tp
    n = np.arange(CMP_N)
    for t in range(NT):
        seen = 16 * n[None, :] + 31 <= (t * P + i)[:, None]
        c[:, C_CB + t * CMP_N:C_CB + (t + 1) * CMP_N] = np.where(seen, 0.0, NEG)
        c[:, C_C01 + t * CMP_N:C_C01 + (t + 1) * CMP_N] = seen
    c[:, C_R4:C_R4 + 4] = 4 - np.arange(4)
    c[:, C_R32:C_R32 + 32] = 32 - np.arange(32)
    inv = 500000.0 ** (-np.arange(0, 16, 2) / 16.0)
    c[:, C_INV:C_INV + 8] = inv
    inv = inv.astype(np.float32)
    for t in range(NT):
        ang = (t * P + i).astype(np.float32)[:, None] * inv[None, :]
        c[:, C_COS + 8 * t:C_COS + 8 * t + 8] = np.cos(ang)
        c[:, C_SIN + 8 * t:C_SIN + 8 * t + 8] = np.sin(ang)
    for h in range(8):
        for k in range(CMP_N):
            c[k, C_REP + 16 * h + k] = 1.0
        c[16 * h:16 * h + 16, C_BLK + h] = 1.0
    c[:, C_PICK + 7] = 1.0
    s, t = np.arange(SEQ), np.arange(SEQ)
    for g, win in enumerate((2, 4, 8, 16)):
        inside = (s[:, None] <= t[None, :]) & (s[:, None] > t[None, :] - win)
        band = inside / np.minimum(t + 1, win)[None, :] - (s[:, None] == t[None, :])
        for a in range(NT):
            at = C_BAND + (a * 4 + g) * SEQ
            c[:, at:at + SEQ] = band[a * P:(a + 1) * P]
    return c


def build(nc, A, out):
    f32, i32 = mybir.dt.float32, mybir.dt.int32
    ACT, ALU = mybir.ActivationFunctionType, mybir.AluOpType
    X = mybir.AxisListType.X
    ds = bass.ds

    with ExitStack() as ctx:
        sems = {}

        def S(name):
            name = split(name)[1]
            if name not in sems:
                sems[name] = ctx.enter_context(nc.semaphore(name))
            return sems[name]

        def nth(name, n):
            tag, kind = split(name)
            if kind == "a1_hidden_done":
                return S("halves_used"), halves(N_CMP + 2 * n - 1)
            if kind.endswith("_in_done"):
                return S("halves_used"), halves(unit_in(kind[:2], n - 1))
            if kind.endswith("_out_done"):
                return S("halves_used"), halves(N_OUT[kind[:2]] + n - 1)
            if tag is None:
                return S(name), n
            order = list(RECUR[kind])
            return S(name), n + sum(RECUR[kind][t] for t in order[:order.index(tag)])

        def sb(name, shape, dt=f32):
            return ctx.enter_context(nc.sbuf_tensor(name, shape, dt))

        ring = sb("ring", [P, SLOTS, UNIT])
        cst = sb("cst", [P, C_BAND])
        x = sb("x", [P, NT, D])
        xn = sb("xn", [P, NT, D])
        fr = mybir.dt.float32r
        whi, wlo = sb("whi", [P, 4, HALF], fr), sb("wlo", [P, 4, HALF], fr)
        hhi, hlo = sb("hhi", [P, NC, SEQ], fr), sb("hlo", [P, NC, SEQ], fr)
        hT = sb("hT", [P, NC, SEQ])
        oT = hT
        work = sb("work", [P, 10240])
        z = work[:, 0:6144].rearrange("p (t n) -> p t n", t=NT)
        qkT = work[:, 6144:10240].rearrange("p (c n) -> p c n", c=16)
        cmb = work[:, 0:8192].rearrange("p (e n) -> p e n", e=EXPERTS)
        acc = sb("acc", [P, 6 * D])
        gbc = sb("gbc", [P, 2, D])
        mixed = sb("mixed", [P, 2304])
        prob = mixed[:, 0:1536].rearrange("p (j n) -> p j n", j=4)
        probT = mixed[:, 1536:2304].rearrange("p (j n) -> p j n", j=2)
        hF = hT[:, :, :].rearrange("p c n -> p (c n)")
        sil = hF[:, 0:1024].rearrange("p (b n) -> p b n", b=2)
        upc = hF[:, 1024:2048].rearrange("p (b n) -> p b n", b=2)
        ahi, alo = sb("ahi", [P, 2, 512], fr), sb("alo", [P, 2, 512], fr)
        adaw = mixed[:, 0:1536].rearrange("p (b k n) -> p b k n", b=2, k=2)
        ada_rest = [mixed[:, 0:HALF], mixed[:, HALF:2 * HALF], xn[:, 0, :], xn[:, 1, :]]
        rest_place = [q % 4 if q < 24 else 2 + q % 2 for q in range(32)]
        idb, maskh = sb("idb", [P, P], mybir.dt.bfloat16), sb("maskh", [P, P], mybir.dt.bfloat16)
        adat = sb("adat", [P, 384])
        rows = sb("rows", [P, 3, P])
        colA = sb("colA", [P, R_END])
        colB = sb("colB", [P, 80])
        csil = sb("csil", [P, NC])
        modc = sb("modc", [P, 48])
        ng = sb("ng", [P, 2, NC])
        rw = sb("rw", [P, NC, 36])
        rb = sb("rb", [P, 36])
        lamt = sb("lamt", [P, 4, 64])
        sm = sb("sm", [P, 64])
        posi = sb("posi", [P, NT], i32)
        rope = sb("rope", [P, 6, 16])
        rt = hF[:, 0:1024].rearrange("p (k n) -> p k n", k=4)
        nmax = sb("nmax", [P, 4, 2])
        psum_ = sb("psum_", [P, 4, 2])
        rsum = sb("rsum", [P, 4, 2])
        lg = sb("lg", [P, NT, 36])
        rs = sb("rs", [P, 10, 64])
        sub_squares = [rows[:, 0:2, :].rearrange("p a n -> p (a n)"), lamt[:, :, :].rearrange("p a n -> p (a n)")]
        sub_squares += [rs[:, 4 * i:4 * i + 4, :].rearrange("p a n -> p (a n)") for i in range(2)]
        sub_squares += [xn[:, 0, SEQ * i:SEQ * i + SEQ] for i in range(4)]
        cbT = sb("cbT", [32, SEQ])
        gate = sb("gate", [P, NT, 48])
        stat = sb("stat", [P, NT, 4, 6])
        ssq = sb("ssq", [P, NT, 4])
        diag = sb("diag", [P, NT, P])
        colC = sb("colC", [P, 88])
        mv = sb("mv", [P, NT, 2])
        fox = sb("fox", [P, 4, 8])
        cum = sb("cum", [4, 2, SEQ])
        bfor = sb("bfor", [P, 4])
        pw = sb("pw", [P, 2, 64])
        kd = acc[:, 0:1024].rearrange("p (t a n) -> p t a n", t=NT, a=4)
        kdT = acc[:, 1024:2048].rearrange("p (a n) -> p a n", a=4)
        blk = acc[:, 2048:3008].rearrange("p (v j n) -> p v j n", v=2, j=16)
        vblk = acc[:, 3008:4032].rearrange("p (g h d) -> p g h d", g=2, h=8)
        pc = acc[:, 4032:4544].rearrange("p (t h n) -> p t h n", t=NT, h=16)
        pcT = acc[:, 4544:5056].rearrange("p (g n) -> p g n", g=2)
        blk_parts = [v[:, :, 0:480].rearrange("p v (j n) -> p v j n", j=16) for v in (ahi, alo)]
        hraw = work[:, 6144:6656].rearrange("p (v n) -> p v n", v=2)
        hid = acc[:, 5056:5176].rearrange("p (v c n) -> p v c n", v=2, c=2)
        kcT = acc[:, 5176:5206]
        vc = acc[:, 5206:5334].rearrange("p (g d) -> p g d", g=2)
        cw2 = acc[:, 5334:5718].rearrange("p (c n) -> p c n", c=2)
        cms = acc[:, 5718:5846].rearrange("p (a n) -> p a n", a=4)
        sgw = acc[:, 0:512].rearrange("p (g n) -> p g n", g=4)
        sgwT = acc[:, 512:1024].rearrange("p (g n) -> p g n", g=4)
        sgl = acc[:, 1024:1536].rearrange("p (a n) -> p a n", a=2)
        sgt = acc[:, 1536:2048].rearrange("p (t n) -> p t n", t=NT)
        pool = acc[:, 2048:2560].rearrange("p (c n) -> p c n", c=2)
        cvt = acc[:, 2560:4608].rearrange("p (b c n) -> p b c n", b=2, c=4)
        bands = acc[:, 2560:4608]
        cvrow = acc[:, 4608:5120].rearrange("p (w n) -> p w n", w=4)
        cvc = acc[:, 5120:5296].rearrange("p (w n) -> p w n", w=4)
        cvcur = acc[:, 5296:5328].rearrange("p (b w n) -> p b w n", b=2, w=4)

        bank = [ctx.enter_context(nc.psum_tensor(f"bank{i}", [P, 512], f32)) for i in range(8)]
        scratch = nc.dram_tensor("combine_rows", (2, EXPERTS * SEQ), f32, kind="Internal").ap()

        norm_columns_of = {"s0": (colC[:, 72:80], colC[:, 80:88]), "s1": (colC[:, 40:48], colC[:, 56:64]),
                           "f0": (colC[:, 8:16], colC[:, 24:32]), "f1": (colC[:, 16:24], colC[:, 32:40])}
        ident, ones = cst[:, C_ID:C_ID + P], cst[:, C_ONE:C_ONE + P]
        tri, maskb = cst[:, C_TRI:C_TRI + P], cst[:, C_MASK:C_MASK + P]

        def pair(b):
            return bank[b][:, :].rearrange("p (c n) -> p c n", c=2)

        def slot(n):
            return ring[:, n % SLOTS, :]

        def half(n, h):
            b = (2 * n + h) % 4
            return whi[:, b, :], wlo[:, b, :]

        def landed(eng, n, more=0):
            eng.wait_ge(*nth(f"weights_landed{n % SLOTS}", 16 * (n // SLOTS + 1) + 32 * more))

        def used(eng, n, more=0):
            eng.wait_ge(S("halves_used"), halves(n) + 12 * more)

        class Chain:
            def __init__(self, eng, name):
                self.eng, self.sem, self.n = eng, S(name), 0

            def __call__(self, ins):
                self.n += 1
                ins.then_inc(self.sem, 1)

            def sync(self):
                self.eng.wait_ge(self.sem, self.n)

        def attention(tag):
            jobs, units = [], []
            if tag == "a0":
                for j in range(16):
                    jobs.append(dict(par=j % 2, q=qkT[:, j // 2, :], k=qkT[:, 8 + j // 2, :], fox=None))
                for u in range(8):
                    units.append(dict(jobs=(2 * u, 2 * u + 1), v=2048 + 128 * u, M=128, off=0,
                                      group=u, first=True, last=True))
            elif tag == "a1":
                for j in range(32):
                    h, w = j // 2, j % 2
                    jobs.append(dict(par=h % 2, q=qkT[:, h // 2, :], k=kdT[:, 2 * w + h // 8, :], fox=None))
                    units.append(dict(jobs=(j,), v=(1664 if w else 1408) + 64 * (h // 8), M=64,
                                      off=64 * (h % 2), group=h // 2, first=w == 0,
                                      last=h % 2 == 1 and w == 1, h=h, w=w))
            else:
                for j in range(8):
                    b, h = j // 4, j % 4
                    jobs.append(dict(par=h % 2, q=qkT[:, 4 * b + h // 2, :],
                                     k=qkT[:, 4 * b + 2 + h // 2, :], fox=h if b else None))
                    units.append(dict(jobs=(j,), v=(1280 if b else 512) + 64 * h, M=64,
                                      off=64 * (h % 2), group=j // 2, first=True, last=h % 2 == 1))
            ends = {u["jobs"][-1]: n for n, u in enumerate(units)}
            return jobs, units, ends

        def w_in(tag, c, w):
            src = A["diff_w_in"][0] if tag == "a0" else A["nsa_w_in"][0] if tag == "a1" else A["w_in_2"][int(tag[1])]
            return src[:, c:c + w].rearrange("(k p) n -> p k n", p=P)

        def w_out(tag, j):
            src = A["diff_w_out"][0] if tag == "a0" else A["nsa_w_out"][0] if tag == "a1" else A["w_o_2"][int(tag[1])]
            return src[:, 256 * j:256 * j + 256].rearrange("(k p) n -> p k n", p=P)

        block = ctx.enter_context(nc.Block())

        @block.sync
        def _(sp):
            def load(n, src, width=256, more=0):
                dst = slot(n)[:, 0:src_free(src)]
                if len(src.shape) == 3:
                    dst = dst.rearrange("p (k n) -> p k n", k=src.shape[1])
                sp.dma_start(dst, src).then_inc(S(f"weights_landed{n % SLOTS}"), 16)

            def src_free(src):
                r = 1
                for s in src.shape[1:]:
                    r *= s
                return r

            def stream(n, src, more=0):
                m = n - SLOTS
                if m >= FIRST:
                    sp.wait_ge(S("halves_split"), halves(m) + 12 * more)
                elif m >= 0:
                    sp.wait_ge(S("ada0_done"), m + 1)
                load(n, src)

            def projection(tag):
                for j, (c, w) in enumerate(COLS[tag]):
                    if tag == "a1" and j == 6:
                        for m in range(4):
                            src = A["nsa_cmp_w1"][0, m // 2, (m % 2) * 1024:(m % 2) * 1024 + 1024, :]
                            stream(N_CMP + m, src.rearrange("(k p) n -> p k n", p=P))
                    stream(unit_in(tag, j), w_in(tag, c, w))
                for j in range(4):
                    stream(N_OUT[tag] + j, w_out(tag, j))

            def up_source(tag, e, part):
                l = int(tag[1])
                if tag[0] == "m":
                    w = A[("moe_w_gate", "moe_w_up")[part]][l, ds(e, 1)]
                    return w.rearrange("o (k p) n -> p (o k) n", p=P)
                return A["w_up_2"][l][:, ds(e * HID + part * FF, HID)].rearrange("(k p) n -> p k n", p=P)

            def down_source(tag, e):
                l = int(tag[1])
                if tag[0] == "m":
                    return A["moe_w_down"][l, ds(e, 1)].rearrange("o (k p) n -> p (o k) n", p=P)
                return A["w_down_2"][l][ds(e * HID, HID), :].rearrange("(k p) n -> p k n", p=P)

            def experts(tag):
                count = COUNT[tag]

                def step(e, i=0):
                    stream(N_EXP[tag] + 4 + 3 * e, down_source(tag, i * 2 + e), i)
                    for part in range(2):
                        stream(unit_up(tag, e + 2, part), up_source(tag, i * 2 + (e + 2), part), i)

                for e in range(2):
                    for part in range(2):
                        stream(unit_up(tag, e, part), up_source(tag, e, part))
                step(0)
                step(1)
                with sp.Fori(1, (count - 2) // 2) as i:
                    step(0, i)
                    step(1, i)
                if count % 2:
                    step(count - 3)
                for e in (count - 2, count - 1):
                    stream(unit_down(tag, e), down_source(tag, e))

            for k in range(NC):
                stream(k, A["ada_w"][0, k * P:(k + 1) * P, 0:UNIT])
            projection("a0")
            experts("m0")
            projection("a1")
            experts("m1")
            for l in "01":
                projection("s" + l)
                experts("f" + l)

        @block.gpsimd
        def _(pool_eng):
            g = pool_eng

            def aux(name, dst, src):
                g.dma_start(dst, src).then_inc(S(name), 16)

            def row(src):
                return src.rearrange("(o n) -> o n", o=1)

            def everywhere(src):
                return row(src).broadcast_to([P, src.shape[0]])

            g.memset(rows[:, :, :], 0.0).then_inc(S("rows_clear"), 1)
            g.wait_ge(*nth("rows_clear", 1))
            aux("rowc_landed", rows[0:NC, 2, :], A["c"][0].rearrange("(c p) -> c p", p=P))
            aux("const_landed", cst[:, :], A["consts"][:, 0:C_BAND])
            ra = rows[:, 0, :]
            aux("rows_landed", ra[0:48, :], A["ada_b"][0].rearrange("(c p) -> c p", p=P))
            aux("rows_landed", ra[R_NG:R_NG + 32, :], A["norm_g"].rearrange("l s (c p) -> (l s c) p", p=P))
            aux("rows_landed", ra[R_SUB:R_SUB + 1, :], A["diff_subln_g"])
            aux("rows_landed", ra[R_B1:R_B1 + 4, :], A["nsa_cmp_b1"][0].rearrange("v (c p) -> (v c) p", p=P))
            aux("rows_landed", ra[R_PS:R_PS + 4, :], A["pool_scale_2"].rearrange("l (c p) -> (l c) p", p=P))
            aux("rows_landed", ra[R_SB:R_SB + 8, :], A["sgu_b_2"].rearrange("l g t -> (l g) t"))
            aux("rows_landed", rows[0:48, 1, :], A["ada_b"][1].rearrange("(c p) -> c p", p=P))
            aux("rows_landed", rows[48:80, 1, :],
                A["nsa_cmp_pos"][0].rearrange("v (j t) d -> (v j) (t d)", t=2))
            for n, v in enumerate(("ln1_g_2", "ln1_b_2", "ln2_g_2", "ln2_b_2")):
                at = 8 + 16 * n
                aux("rows_landed", rows[at:at + 16, 2, :], A[v].rearrange("l (c p) -> (l c) p", p=P))
            aux("rows_landed", rows[72:80, 2, :], A["final_g"].rearrange("(c p) -> c p", p=P))
            aux("x_landed", x[:, :, :], A["x"][0].rearrange("(t p) n -> p t n", p=P))
            for t in range(NT):
                aux("pos_landed", posi[:, t:t + 1], A["positions"][0, t * P:(t + 1) * P].rearrange("(p o) -> p o", o=1))
            aux("lam_landed", lamt[:, :, :].rearrange("p a b -> p (a b)"),
                everywhere(A["diff_lambda"][0].rearrange("a b -> (a b)")))

            def gates(l):
                for n, v in enumerate((2, 5)):
                    aux("gbc_landed", gbc[:, n, :], everywhere(A["ada_b"][l, v * D:(v + 1) * D]))

            def router(l):
                aux("router_landed", rw[:, :, 0:4], A["moe_w_group"][l].rearrange("(k p) n -> p k n", p=P))
                for q in range(GROUPS):
                    aux("router_landed", rw[:, :, 4 + 8 * q:12 + 8 * q],
                        A["moe_w_expert"][l, q].rearrange("(k p) n -> p k n", p=P))
                aux("router_landed", rb[:, 0:4], everywhere(A["moe_b_group"][l]))
                aux("router_landed", rb[:, 4:36], everywhere(A["moe_b_expert"][l].rearrange("a b -> (a b)")))

            def combine(l):
                g.wait_ge(*nth("combine_rows_ready", l + 1))
                aux("combine_stored", scratch[l].rearrange("(e t) -> e t", e=EXPERTS), cbT[:, :])
                g.wait_ge(*nth("combine_stored", 16 * (l + 1)))
                n = 2 * SEQ
                aux("combine_first", work[:, 0:n], everywhere(scratch[l][0:n]))
                aux("combine_landed", work[:, n:8192], everywhere(scratch[l][n:8192]))

            gates(0)
            router(0)
            for q in range(32):
                b = rest_place[q]
                if q == 0:
                    g.wait_ge(S("ada0_done"), 4)
                elif q in (2, 3):
                    g.wait_ge(*nth("a0_xT", 4))
                elif b in rest_place[:q]:
                    g.wait_ge(S("ada0_rest"), max(r for r in range(q) if rest_place[r] == b) + 1)
                k, part = divmod(q, 4)
                at = UNIT + part * HALF
                aux(f"ada_rest_landed{b}", ada_rest[b], A["ada_w"][0, k * P:(k + 1) * P, at:at + HALF])
            layer1 = A["ada_w"][1].rearrange("(k p) n -> p k n", p=P)

            g.wait_ge(*nth("a0_turned", 8))
            for q in range(4):
                if q > 1:
                    g.wait_ge(S("ada1_used"), q - 1)
                aux(f"ada1_landed{q % 2}", adaw[:, q % 2], layer1[:, 2 * q:2 * q + 2, 15 * 384:16 * 384])
            combine(0)
            with g.Fori(0, 15) as i:
                for q in range(4):
                    g.wait_ge(S("ada1_used"), i * 4 + (q + 3))
                    aux(f"ada1_landed{q % 2}", adaw[:, q % 2], layer1[:, 2 * q:2 * q + 2, ds(i * 384, 384)])
            router(1)
            g.wait_ge(*nth("a1_x_part", 4))
            gates(1)
            g.wait_ge(*nth("mod_done", 2))
            aux("cmpw_landed", cw2[:, :, 0:64], A["nsa_cmp_w2"][0, 0].rearrange("(c p) n -> p c n", p=P))
            aux("cmpw_landed", cw2[:, :, 64:128], A["nsa_cmp_w2"][0, 0].rearrange("(c p) n -> p c n", p=P))
            aux("cmpw_landed", cw2[:, :, 128:192], A["nsa_cmp_w2"][0, 1].rearrange("(c p) n -> p c n", p=P))
            combine(1)
            aux("final_landed", gbc[:, 0, :], everywhere(A["final_g"]))

            def ln(name, l):
                for n, v in enumerate(("g", "b")):
                    aux(f"{name}{l}_landed", gbc[:, n, :], everywhere(A[f"{name}_{v}_2"][l]))

            for l in range(2):
                g.wait_ge(*(nth("ln2_0_tile", 1) if l else nth("first_x_part", 4)))
                aux("mix_landed", sgw[:, :, :], A["sgu_w_2"][l].rearrange("g t s -> t g s"))
                aux("mix_landed", sgl[:, 0, :], everywhere(A["sgu_ln_g_2"][l]))
                aux("mix_landed", sgl[:, 1, :], everywhere(A["sgu_ln_b_2"][l]))
                aux("mix_landed", bfor[:, :], everywhere(A["b_forget_2"][l]))
                aux("mix_landed", pw[:, :, :], A["pool_w_2"][l].rearrange("(b a) c d -> (a c) b d", a=2))
                aux("mix_landed", bands, A["consts"][:, C_BAND:C_END])
                for w in range(3):
                    aux("conv_landed", cvrow[0:44, w, :], A["conv_w_2"][l, w].rearrange("(c p) -> c p", p=P))
                aux("conv_landed", cvrow[0:44, 3, :], A["conv_b_2"][l].rearrange("(c p) -> c p", p=P))
                g.wait_ge(*nth("ln2_0_done" if l else "first_done", 1))
                ln("ln1", l)
                g.wait_ge(*nth(f"ln1_{l}_done", 1))
                ln("ln2", l)
            for t in range(NT):
                g.wait_ge(*nth("ln2_1_tile", t + 1))
                g.dma_start(out[0, t * P:(t + 1) * P, :], x[:, t, :]).then_inc(S("out_stored"), 16)
            g.wait_ge(*nth("out_stored", 32))

        @block.tensor
        def _(pe):
            def mm(o, l, r, start=True, stop=True):
                return pe.matmul(o, l, r, start=start, stop=stop, skip_group_check=True)

            def columns(first, n, tag):
                for i in range(first, first + n):
                    last = pe.transpose(bank[7][:, i * P:i * P + P], rows[:, i, :], ident)
                last.then_inc(S(tag), 1)

            def mod_columns(vectors, b):
                for v in vectors:
                    for c in range(NC):
                        at = v * D + c * P
                        last = mm(bank[b][:, v * 8 + c:v * 8 + c + 1], acc[:, at:at + P], ones[:, 0:1])
                last.then_inc(S("modc_ready"), 1)

            def mod_gates(b):
                for n, v in enumerate((2, 5)):
                    for h in range(2):
                        last = mm(bank[b + 2 * n + h][:, :], ones, acc[:, v * D + h * 512:v * D + h * 512 + 512])
                last.then_inc(S("modg_ready"), 1)

            def transposes(tag, ready):
                for b in range(4):
                    for c in (2 * b, 2 * b + 1):
                        for t in range(NT):
                            if c == 0:
                                pe.wait_ge(*nth(ready, t + 1))
                            if c == 6 and t == 0 and tag == "a0":
                                pe.wait_ge(*nth("ng_ready", 1))
                            if c == 6 and t == 0 and tag == "a1":
                                pe.wait_ge(*nth("ng_ready", 3))
                            o = bank[4 + b][:, (c % 2) * 256 + t * P:(c % 2) * 256 + t * P + P]
                            v = x[:, t, c * P:(c + 1) * P]
                            last = mm(o, v, diag[:, t, :]) if "diag" in ready else pe.transpose(o, v, ident)
                    last.then_inc(S(f"{tag}_xT"), 1)

            def hT_ready(tag, h):
                pe.wait_ge(*nth(f"{tag}_lo", 2 * h + 2))

            def split_ready(n, h, more=0):
                pe.wait_ge(S("halves_split"), halves(n) - 1 + h + 12 * more)

            def project(tag, j, n=None, out_of=None):
                if out_of is None:
                    w, n, b = COLS[tag][j][1], unit_in(tag, j), 4 + j % 4
                    if j >= 4:
                        pe.wait_ge(*nth(f"{tag}_z", j - 3))
                else:
                    w, n, b = 256, N_OUT[tag] + j, 4 + j
                ks = 4 if w == 256 else 8
                for h in range(2 if w == 256 else 1):
                    if j == 0:
                        hT_ready("o" + tag if out_of else tag, h)
                    split_ready(n, h if w == 256 else 1)
                    Wh, Wl = (v[:, 0:ks * w].rearrange("p (k n) -> p k n", k=ks) for v in half(n, h))
                    for t in range(NT):
                        for k in range(ks):
                            first = h == 0 and t == 0 and k == 0
                            c = 4 * h + k
                            xh, xl = hhi[:, c, t * P:(t + 1) * P], hlo[:, c, t * P:(t + 1) * P]
                            o = pair(b)[:, t, 0:w]
                            mm(o, xh, Wh[:, k, :], start=first)
                            mm(o, xh, Wl[:, k, :], start=False)
                            last = mm(o, xl, Wh[:, k, :], start=False)
                    last.then_inc(S("halves_used"), 1 if w == 256 else 2)

            def project_out(tag):
                for j in range(4):
                    project(tag, j, out_of=True)

            def head_transposes(tag, sources):
                for i, (view, c) in enumerate(sources):
                    b = (i // 2) % 4
                    if i % 2 == 0 and i >= 8:
                        pe.wait_ge(*nth(f"{tag}_qk", i // 2 - 3))
                    for t in range(NT):
                        last = pe.transpose(bank[b][:, (i % 2) * 256 + t * P:(i % 2) * 256 + t * P + P],
                                            view[:, t, c:c + P], ident)
                    if i % 2:
                        last.then_inc(S(f"{tag}_qkT"), 1)

            def attend(tag, after=None):
                jobs, units, ends = attention(tag)
                J = len(jobs)

                def scores(j):
                    job = jobs[j]
                    if j >= 4:
                        pe.wait_ge(*nth(f"{tag}_exp", j - 3))
                    rows_ = slice(64 * job["par"], 64 * job["par"] + 64)
                    for t, (at, kl) in enumerate(((0, P), (P, SEQ))):
                        o = bank[j % 4][:, at:at + kl]
                        mm(o, job["q"][rows_, t * P:(t + 1) * P], job["k"][rows_, 0:kl], stop=False)
                        if job["fox"] is not None:
                            h = job["fox"]
                            mm(o, ident[0:4, h:h + 1].broadcast_to([4, P]), cum[:, 1, 0:kl], False, False)
                            mm(o, cum[:, 0, t * P:(t + 1) * P], ident[0:4, h:h + 1].broadcast_to([4, kl]),
                               False, False)
                        last = mm(bank[j % 4][:, at + kl - P:at + kl], idb[:, :], maskh[:, :], start=False)
                    last.then_inc(S(f"{tag}_scores"), 1)

                def turn(u):
                    pe.wait_ge(*nth(f"{tag}_norm", u + 1))
                    if u >= 2:
                        pe.wait_ge(*nth(f"{tag}_probT", u - 1))
                    j = units[u]["jobs"][0]
                    for b in range(3):
                        last = pe.transpose(bank[4 + u % 2][:, b * P:(b + 1) * P],
                                            prob[:, j % 4, b * P:(b + 1) * P], ident)
                    last.then_inc(S(f"{tag}_turned"), 1)

                def values(u):
                    U = units[u]
                    pe.wait_ge(*nth(f"{tag}_probT", u + 1))
                    if U["first"] and U["group"] >= 2 and U["off"] == 0:
                        pe.wait_ge(*nth(f"{tag}_o", U["group"] - 1))
                    o = bank[6 + U["group"] % 2][U["off"]:U["off"] + U["M"], :]
                    mm(o[:, 0:SEQ], z[:, 0, U["v"]:U["v"] + U["M"]], probT[:, u % 2, 0:SEQ],
                       start=U["first"], stop=False)
                    last = mm(o[:, P:SEQ], z[:, 1, U["v"]:U["v"] + U["M"]], probT[:, u % 2, SEQ:384],
                              start=False, stop=tag != "a1")
                    if tag == "a1" and U["w"] == 1:
                        g_ = U["h"] // 8
                        if u == 1:
                            pe.wait_ge(*nth("cmp_ready", 2))
                        last = mm(o[:, 0:SEQ], vblk[:, g_, U["h"] % 8, :], pcT[:, g_, :], start=False)
                    last.then_inc(S(f"{tag}_pv"), 1)

                for j in range(J + 4):
                    if j < J:
                        scores(j)
                    if j - 2 in ends:
                        turn(ends[j - 2])
                    if j - 3 in ends:
                        values(ends[j - 3])

            def experts(tag):
                count = COUNT[tag]

                def up(e, i=0):
                    for part in range(2):
                        n = unit_up(tag, e, part)
                        b = 4 + 2 * (e % 2) + part
                        for h in range(2):
                            if e == part == 0:
                                hT_ready(tag, h)
                            split_ready(n, h, i)
                            Wh, Wl = (v.rearrange("p (k n) -> p k n", k=4) for v in half(n, h))
                            for c in range(2):
                                for k in range(4):
                                    xh, xl = hhi[:, 4 * h + k, :], hlo[:, 4 * h + k, :]
                                    o = pair(b)[:, c, :]
                                    mm(o, Wh[:, k, c * P:(c + 1) * P], xh, start=h + c + k == 0)
                                    mm(o, Wh[:, k, c * P:(c + 1) * P], xl, start=False)
                                    last = mm(o, Wl[:, k, c * P:(c + 1) * P], xh, start=False)
                            last.then_inc(S("halves_used"), 1)

                def down(e, i=0, start=False):
                    n = unit_down(tag, e)
                    pe.wait_ge(*nth(f"{tag}_aT", i * 2 + e + 1))
                    for c in range(2):
                        split_ready(n, c, i)
                        Wh, Wl = half(n, c)
                        for t in range(NT):
                            a = slice(c * SEQ + t * P, c * SEQ + t * P + P)
                            for j in range(2):
                                o, w = bank[2 * t + j][:, :], slice(j * 512, (j + 1) * 512)
                                mm(o, ahi[:, e % 2, a], Wh[:, w], start=start and c == 0)
                                mm(o, ahi[:, e % 2, a], Wl[:, w], start=False)
                                last = mm(o, alo[:, e % 2, a], Wh[:, w], start=False)
                        last.then_inc(S("halves_used"), 1)

                if tag[0] == "m":
                    l = int(tag[1])
                    pe.wait_ge(*nth("router_landed", 7 * 16 * (l + 1)))
                    pe.wait_ge(*nth(f"{tag}_hT_act", 4))
                    pe.wait_ge(*nth(f"{tag}_hT_dve", 4))
                    for t in range(NT):
                        for k in range(NC):
                            last = mm(bank[6][:, t * 64:t * 64 + 36], hT[:, k, t * P:(t + 1) * P], rw[:, k, :],
                                      start=k == 0, stop=k == NC - 1)
                    last.then_inc(S("logits_done"), 1)
                up(0)
                if tag[0] == "m":
                    pe.wait_ge(*nth("logits_read", l + 1))
                    pe.wait_ge(*nth("combine_ready", l + 1))
                    for t in range(NT):
                        last = pe.transpose(bank[0][0:32, t * P:(t + 1) * P], rs[:, 0, t * 32:(t + 1) * 32], ident)
                    last.then_inc(S("combine_turned"), 1)
                up(1)
                if tag[0] == "m":
                    pe.wait_ge(*nth("combine_rows_ready", l + 1))
                down(0, start=True)
                up(2)
                down(1)
                up(3)
                with pe.Fori(1, (count - 2) // 2) as i:
                    down(0, i)
                    up(2, i)
                    down(1, i)
                    up(3, i)
                if count % 2:
                    down(count - 3)
                    up(count - 1)
                down(count - 2)
                e, n = count - 1, unit_down(tag, count - 1)
                pe.wait_ge(*nth(f"{tag}_aT", count))
                for t in range(NT):
                    for c in range(2):
                        if t == 0:
                            split_ready(n, c)
                        Wh, Wl = half(n, c)
                        a = slice(c * SEQ + t * P, c * SEQ + t * P + P)
                        for j in range(2):
                            o, w = bank[2 * t + j][:, :], slice(j * 512, (j + 1) * 512)
                            mm(o, ahi[:, e % 2, a], Wh[:, w], start=False)
                            mm(o, ahi[:, e % 2, a], Wl[:, w], start=False)
                            last = mm(o, alo[:, e % 2, a], Wh[:, w], start=False)
                        if t == 1:
                            last.then_inc(S("halves_used"), 1)
                        elif c == 1:
                            last.then_inc(S(f"{tag}_down_tile"), 1)
                if tag == "m0":
                    pe.wait_ge(*nth("ada1_done", 16))
                    mod_columns((0, 1, 3, 4), 7)

            pe.wait_ge(*nth("rowc_landed", 16))
            pe.wait_ge(*nth("const_landed", 16))
            pe.transpose(bank[6][:, 0:NC], rows[0:NC, 2, :], ident[0:NC, 0:NC]).then_inc(S("c_turned"), 1)
            pe.wait_ge(*nth("rows_landed", 13 * 16))
            columns(0, 3, "cols_turned")
            pe.wait_ge(*nth("mask_ready", 1))
            pe.wait_ge(*nth("ada0_done", NC))
            mod_columns((0, 1), 7)
            transposes("a0", "a0_diag")
            for j in range(12):
                project("a0", j)
            pe.wait_ge(*nth("a0_roped", 1))
            head_transposes("a0", [(z, P * i) for i in range(16)])
            pe.wait_ge(*nth("a0_qk", 8))
            attend("a0")
            for u in range(8):
                pe.wait_ge(*nth("sub_sq", u + 1))
                last = mm(bank[1][0:8, 0:SEQ], cst[:, C_PICK + 7 - u:C_PICK + 15 - u], sub_squares[u],
                          start=u == 0)
            last.then_inc(S("sub_sum"), 1)
            pe.wait_ge(*nth("ada0_rest", 32))
            mod_columns((3, 4), 0)
            pe.wait_ge(*nth("ng_ready", 2))
            pe.wait_ge(*nth("sub_rstd", 1))
            for u in range(8):
                last = mm(pair(u // 2)[:, u % 2, :], ident[0:8, u:u + 1].broadcast_to([8, P]), cbT[0:8, :])
                if u % 2:
                    last.then_inc(S("sub_spread"), 1)
            pe.wait_ge(*nth("a0_o", 8))
            mod_gates(4)
            pe.wait_ge(*nth("mod_done", 1))
            project_out("a0")
            transposes("m0", "m0_diag")
            experts("m0")
            transposes("a1", "a1_diag")
            mod_gates(0)
            for j in range(4):
                project("a1", j)
            project("a1", 4)
            pe.wait_ge(*nth("a1_z", 4))
            for v in range(2):
                for g_ in range(2):
                    for tp in range(2):
                        for t in range(NT):
                            c = 1024 + v * 128 + g_ * 64
                            at = (v * 2 + g_) * 128 + t * 64
                            last = mm(bank[0][64 * tp:64 * tp + 64, at:at + 64], z[:, t, c:c + 64],
                                      cst[:, C_EVEN + 64 * tp:C_EVEN + 64 * tp + 64])
            last.then_inc(S("cmp_split"), 1)
            project("a1", 5)
            for v in range(2):
                pe.wait_ge(*nth("blk_ready", v + 1))
                o = bank[1 + 2 * v][0:30, 0:HID]
                for m in range(4):
                    n, h = N_CMP + 2 * v + m // 2, m % 2
                    split_ready(n, h)
                    Wh, Wl = (w.rearrange("p (k n) -> p k n", k=4) for w in half(n, h))
                    for j in range(4):
                        bh, bl = (blk_parts[s_][:, v, 4 * m + j, :] for s_ in range(2))
                        mm(o, bh, Wh[:, j, :], start=m + j == 0)
                        mm(o, bh, Wl[:, j, :], start=False)
                        last = mm(o, bl, Wh[:, j, :], start=False)
                    last.then_inc(S("halves_used"), 1)
            for v in range(2):
                pe.wait_ge(*nth("hid_raw", v + 1))
                for c in range(2):
                    last = pe.transpose(bank[1 + 2 * v][:, 256 + c * 32:256 + c * 32 + 30],
                                        hraw[0:30, v, c * P:(c + 1) * P], ident[0:30, 0:30])
                last.then_inc(S("hid_turned"), 1)
            project("a1", 6)
            pe.wait_ge(*nth("hid_ready", 1))
            pe.wait_ge(*nth("cmpw_landed", 48))
            for c in range(2):
                mm(bank[2][:, 0:30], cw2[:, c, 0:128], hid[:, 0, c, :], start=c == 0, stop=c == 1)
            for g_ in range(2):
                for c in range(2):
                    last = mm(bank[2][0:15, 64 + 64 * g_:128 + 64 * g_], hid[:, 1, c, 15 * g_:15 * g_ + 15],
                              cw2[:, c, 128:192], start=c == 0, stop=c == 1)
            last.then_inc(S("cmp_kv"), 1)
            project("a1", 7)
            pe.wait_ge(*nth("cmp_kv_read", 1))
            for g_ in range(2):
                last = mm(bank[3][:, g_ * 64:g_ * 64 + 64], cst[0:15, C_REP:C_REP + P], vc[0:15, g_, :])
            last.then_inc(S("vc_spread"), 1)
            pe.wait_ge(*nth("a1_roped", 3))
            pe.wait_ge(*nth("vblk_ready", 1))
            kd_ = kd.rearrange("p t a n -> p t (a n)")
            head_transposes("a1", [(z, P * i) for i in range(8)] + [(kd_, P * i) for i in range(4)])
            pe.wait_ge(*nth("a1_qk", 6))
            pe.wait_ge(*nth("a1_z", 8))
            for t in range(NT):
                for h in range(16):
                    r = slice(64 * (h % 2), 64 * (h % 2) + 64)
                    at = (t * 8 + h // 2) * 16
                    last = mm(bank[4 + h % 2][:, at:at + CMP_N], qkT[r, h // 2, t * P:(t + 1) * P],
                              kcT[r, 15 * (h // 8):15 * (h // 8) + 15])
            last.then_inc(S("cmp_scores"), 1)
            pe.wait_ge(*nth("pc_ready", 1))
            for g_ in range(2):
                for t in range(NT):
                    last = pe.transpose(bank[5][:, g_ * 256 + t * P:g_ * 256 + t * P + P],
                                        pc[:, t, 8 * g_:8 * g_ + 8, :].rearrange("p h n -> p (h n)"), ident)
            last.then_inc(S("pc_turned"), 1)
            pe.wait_ge(*nth("cmp_ready", 1))
            attend("a1")
            project_out("a1")
            transposes("m1", "m1_diag")
            experts("m1")
            for l in range(2):
                tag, ffn = f"s{l}", f"f{l}"
                transposes(tag, "first_diag" if l == 0 else "ln2_0_tile")
                for j in range(5):
                    project(tag, j)
                pe.wait_ge(*nth("mix_landed", 6 * 16 * (l + 1)))
                for g_ in range(4):
                    last = pe.transpose(bank[3][:, g_ * P:(g_ + 1) * P], sgw[:, g_, :], ident)
                last.then_inc(S("sgw_turned"), 1)
                pe.wait_ge(*nth("conv_landed", 4 * 16 * (l + 1)))
                for w in range(4):
                    last = pe.transpose(bank[2][:, w * 44:w * 44 + 44], cvrow[0:44, w, :], ident[0:44, 0:44])
                last.then_inc(S("conv_turned"), 1)
                project(tag, 5)
                pe.wait_ge(*nth("logf_ready", l + 1))
                mm(bank[1][0:4, 0:SEQ], fox[:, 3, 0:4], cst[:, C_TRI:C_TRI + SEQ], stop=False)
                mm(bank[1][0:4, P:SEQ], fox[:, 3, 4:8], tri, start=False).then_inc(S("cum_done"), 1)
                pe.wait_ge(*nth(f"{tag}_z", 4))
                for g_ in range(4):
                    o = bank[0][64 * (g_ % 2):64 * (g_ % 2) + 64, (g_ // 2) * SEQ:(g_ // 2 + 1) * SEQ]
                    for t in range(NT):
                        at = (t * 4 + g_) * SEQ
                        last = mm(o[:, t * P:SEQ], z[:, t, 2052 + 64 * g_:2116 + 64 * g_],
                                  bands[:, at + t * P:at + SEQ], start=t == 0, stop=t == 1)
                last.then_inc(S("pooled"), 1)
                project(tag, 6)
                pe.wait_ge(*nth("pool_ready", l + 1))
                for g_ in range(4):
                    r = slice(64 * (g_ % 2), 64 * (g_ % 2) + 64)
                    last = mm(bank[0][r, (g_ // 2) * SEQ:(g_ // 2 + 1) * SEQ], pw[r, g_ // 2, :],
                              pool[r, g_ // 2, :])
                last.then_inc(S("pool_mixed"), 1)
                project(tag, 7)
                project(tag, 8)
                pe.wait_ge(*nth("sgv_ready", l + 1))
                for t in range(NT):
                    for g_ in range(4):
                        at = t * SEQ + g_ * 64
                        last = mm(bank[2][:, at:at + 64], sgwT[:, g_, :], z[:, t, 1796 + 64 * g_:1860 + 64 * g_])
                last.then_inc(S("sg_mixed"), 1)
                project(tag, 9)
                pe.wait_ge(*nth("sgy_ready", l + 1))
                for c in range(2):
                    for t in range(NT):
                        last = pe.transpose(bank[3][:, c * SEQ + t * P:c * SEQ + t * P + P],
                                            sgt[:, t, c * P:(c + 1) * P], ident)
                last.then_inc(S("sg_turned"), 1)
                pe.wait_ge(*nth(f"{tag}_roped", 1))
                pe.wait_ge(*nth("mix_read", l + 1))
                pe.wait_ge(*nth(f"{tag}_z", 10))
                head_transposes(tag, [(z, c) for c in (0, 128, 256, 384, 768, 896, 1024, 1152)])
                pe.wait_ge(*nth(f"{tag}_qk", 4))
                attend(tag)
                project_out(tag)
                transposes(ffn, f"ln1_{l}_tile")
                experts(ffn)

        @block.scalar
        def _(act):
            ch = Chain(act, "act_chain")

            def square(tag, t, part, lo, hi):
                act.activation(xn[:, t, lo:hi], x[:, t, lo:hi], ACT.Square, accum_out=ssq[:, t, part:part + 1])\
                    .then_inc(S(f"{tag}_ssq"), 1)

            def root_table():
                ch.sync()
                ch(act.activation(sm[:, 51:52], cst[:, C_ONE:C_ONE + 1], ACT.Sqrt))

            def norm_columns(mixer, tag):
                for j in range(4):
                    split(N_OUT[mixer] + j + 2)
                    if j == 3:
                        root_table()
                    act.wait_ge(*nth(f"{tag}_x_part", j + 1))
                    for t in range(NT):
                        square(tag, t, j, 256 * j, 256 * j + 256)
                root(tag)

            def norm_tiles(tag):
                root_table()
                for t in range(NT):
                    for h in range(2):
                        act.wait_ge(*nth(f"{tag}_x_part", 2 * t + h + 1))
                        square(tag, t, h, 512 * h, 512 * h + 512)
                root(tag)

            def root(tag, at=2, n=2):
                act.wait_ge(*nth(f"{tag}_var", 1))
                act.activation(sm[:, at + n:at + 2 * n], sm[:, at:at + n], ACT.Sqrt).then_inc(S(f"{tag}_rstd"), 1)

            def hT_copy(tag, scale=None, bias=None):
                for c in (0, 1, 4, 5):
                    act.wait_ge(*nth(f"{tag}_xT", c // 2 + 1))
                    kw = {} if scale is None else dict(scale=scale[:, c:c + 1], bias=bias[:, c:c + 1])
                    f = ACT.Copy if scale is None else ACT.Identity
                    act.activation(hT[:, c, :], pair(4 + c // 2)[:, c % 2, :], f, **kw)\
                       .then_inc(S(f"{tag}_hT_act"), 1)

            def split(n, more=0):
                landed(act, n, more)
                for h in range(2):
                    if n >= FIRST + 2:
                        act.wait_ge(S("halves_used"), halves(n - 2) - 1 + h + 12 * more)
                    act.activation(half(n, h)[0], slot(n)[:, h * HALF:(h + 1) * HALF], ACT.Copy)\
                       .then_inc(S("high_parts"), 1)

            def z_copy(tag, j):
                split(unit_in(tag, j) + 2)
                c, w = COLS[tag][j]
                act.wait_ge(*nth(f"{tag}_in_done", j + 1))
                act.activation(z[:, :, c:c + w], pair(4 + j % 4)[:, :, 0:w], ACT.Copy).then_inc(S(f"{tag}_z"), 1)

            def hT_high(tag):
                for b in range(4):
                    if tag == "oa0":
                        act.wait_ge(*nth("a0_oT", b + 1))
                    if tag[0] != "o":
                        act.wait_ge(*nth(f"{tag}_hT_" + ("dve" if b % 2 else "act"), 2 + 2 * (b // 2)))
                    act.activation(hhi[:, 2 * b:2 * b + 2, :], hT[:, 2 * b:2 * b + 2, :], ACT.Copy)\
                       .then_inc(S(f"{tag}_hi"), 1)

            def out_splits(tag):
                for j in range(4):
                    split(N_OUT[tag] + j + 2)

            def qk_copy(tag, n, queries):
                for i in range(n):
                    act.wait_ge(*nth(f"{tag}_qkT", i + 1))
                    q = queries[i]
                    dst = (qkT[:, 2 * i:2 * i + 2, :] if tag != "a1" or i < 4
                           else kdT[:, 2 * i - 8:2 * i - 6, :])
                    act.activation(dst, pair(i % 4)[:, :, :], ACT.Copy, scale=0.125 if q else 1.0)\
                       .then_inc(S(f"{tag}_qk"), 1)

            def attend(tag):
                jobs, units, ends = attention(tag)
                unit_of = {j: n for n, u in enumerate(units) for j in u["jobs"]}
                for j in range(len(jobs) + (5 if tag == "a0" else 3)):
                    if j < len(jobs):
                        act.wait_ge(*nth(f"{tag}_max", j + 1))
                        if j >= 4:
                            act.wait_ge(*nth(f"{tag}_turned", unit_of[j - 4] + 1))
                        ch(act.activation(prob[:, j % 4, 0:P], bank[j % 4][:, 0:P], ACT.Exp,
                                          bias=nmax[:, j % 4, 0:1], accum_out=psum_[:, j % 4, 0:1]))
                        act.activation(prob[:, j % 4, P:384], bank[j % 4][:, P:384], ACT.Exp,
                                       bias=nmax[:, j % 4, 1:2], accum_out=psum_[:, j % 4, 1:2])\
                           .then_inc(S(f"{tag}_exp"), 1)
                    if j - 2 in ends:
                        u = ends[j - 2]
                        act.wait_ge(*nth(f"{tag}_turned", u + 1))
                        if u >= 2:
                            act.wait_ge(*nth(f"{tag}_pv", u - 1))
                        act.activation(probT[:, u % 2, :], bank[4 + u % 2][:, 0:384], ACT.Copy)\
                           .then_inc(S(f"{tag}_probT"), 1)
                    if tag == "a0" and j - 4 in ends:
                        u = ends[j - 4]
                        act.wait_ge(*nth("a0_o", u + 1))
                        act.activation(sub_squares[u], oT[:, u, :], ACT.Square).then_inc(S("sub_sq"), 1)

            def experts(tag):
                count = COUNT[tag]

                def silu(e, i=0, wait=True):
                    used(act, unit_up(tag, e, 1), i)
                    if wait:
                        act.wait_ge(*nth(f"{tag}_aT", i * 2 + e - 1))
                    src = bank[4 + 2 * (e % 2)][:, :]
                    if tag[0] == "f":
                        act.wait_ge(*nth(f"{tag}_taps", i * 2 + e + 1))
                        for c in range(4):
                            act.activation(cvt[:, e % 2, c, :], pair(4 + 2 * (e % 2) + c // 2)[:, c % 2, :],
                                           ACT.Identity, scale=cvcur[:, e % 2, 2, c:c + 1],
                                           bias=cvcur[:, e % 2, 3, c:c + 1]).then_inc(S(f"{tag}_tap2"), 1)
                        act.wait_ge(*nth(f"{tag}_conv", i * 2 + e + 1))
                        src = cvt[:, e % 2, 0:2, :].rearrange("p c n -> p (c n)")
                    act.activation(sil[:, e % 2, :], src, ACT.Silu).then_inc(S(f"{tag}_silu"), 1)

                def step(e, i=0):
                    for k in range(3):
                        split(unit_down(tag, e) + 2 + k, i)
                    silu(e + 2, i)

                first = N_EXP[tag]
                split(first + 2)
                split(first + 3)
                silu(0, wait=False)
                split(first + 4)
                split(first + 5)
                silu(1, wait=False)
                with act.Fori(0, (count - 2) // 2) as i:
                    step(0, i)
                    step(1, i)
                if count % 2:
                    step(count - 3)
                for e in (count - 2, count - 1):
                    if unit_down(tag, e) + 2 < N_END:
                        split(unit_down(tag, e) + 2)

            experts_m = experts_f = experts

            act.wait_ge(*nth("c_turned", 1))
            act.activation(csil[:, :], bank[6][:, 0:NC], ACT.Silu).then_inc(S("csil_ready"), 1)
            act.wait_ge(*nth("lam_dots", 1))
            act.activation(sm[:, 12:14], sm[:, 10:12], ACT.Exp).then_inc(S("lam_exp"), 1)
            act.wait_ge(*nth("angles", 1))
            act.activation(rope[:, 0:2, :], rope[:, 2:4, :], ACT.Sin).then_inc(S("rope_ready"), 1)
            split(FIRST)
            split(FIRST + 1)
            act.wait_ge(*nth("const_landed", 16))
            root_table()
            act.wait_ge(*nth("x_landed", 16))
            for t in range(NT):
                square("a0", t, 0, 0, D)
            root("a0")
            act.wait_ge(*nth("ng_ready", 1))
            hT_copy("a0", ng[:, 0, :], modc[:, 0:8])
            hT_high("a0")
            for j in range(12):
                z_copy("a0", j)
            qk_copy("a0", 8, [True] * 4 + [False] * 4)
            attend("a0")
            act.wait_ge(*nth("sub_var", 1))
            act.activation(cbT[0:8, :], cbT[0:8, :], ACT.Sqrt).then_inc(S("sub_rstd"), 1)
            hT_high("oa0")
            norm_columns("a0", "m0")
            act.wait_ge(*nth("ng_ready", 2))
            hT_copy("m0", ng[:, 1, :], modc[:, 24:32])
            hT_high("m0")

            def route(l):
                act.wait_ge(*nth("route_diff", l + 1))
                act.activation(rs[:, 6, 0:8], rs[:, 5, 0:8], ACT.Exp).then_inc(S("route_exp"), 1)
                act.activation(rs[:, 6, 8:10], rs[:, 5, 8:10], ACT.Exp).then_inc(S("route_exp"), 1)

            route(0)
            experts_m("m0")
            norm_tiles("a1")
            act.wait_ge(*nth("ng_ready", 3))
            hT_copy("a1", ng[:, 0, :], modc[:, 0:8])
            hT_high("a1")
            for j in range(4):
                z_copy("a1", j)
            act.wait_ge(*nth("a1_z", 4))
            act.activation(gate[:, :, :], z[:, :, 1792:1840], ACT.Exp, scale=-1.0).then_inc(S("gate_exp"), 1)
            z_copy("a1", 4)
            z_copy("a1", 5)
            for v in range(2):
                for n in (N_CMP + 2 * v + 2, N_CMP + 2 * v + 3):
                    split(n)
                act.wait_ge(*nth("a1_hidden_done", v + 1))
                act.activation(hraw[0:30, v, :], bank[1 + 2 * v][0:30, 0:HID], ACT.Copy).then_inc(S("hid_raw"), 1)
            for v in range(2):
                act.wait_ge(*nth("hid_turned", v + 1))
                for c in range(2):
                    at = R_B1 + 2 * v + c
                    last = act.activation(hid[:, v, c, :], bank[1 + 2 * v][:, 256 + c * 32:256 + c * 32 + 30],
                                          ACT.Gelu_apprx_tanh, bias=colA[:, at:at + 1])
                    if (v, c) != (1, 1):
                        ch(last)
            last.then_inc(S("hid_ready"), 1)
            z_copy("a1", 6)
            z_copy("a1", 7)
            qk_copy("a1", 6, [True] * 4 + [False] * 2)
            act.wait_ge(*nth("pc_diff", 1))
            act.activation(pc[:, :, :, 0:CMP_N], pc[:, :, :, 0:CMP_N], ACT.Exp).then_inc(S("pc_exp"), 1)
            act.wait_ge(*nth("pc_turned", 1))
            act.activation(pcT[:, :, :], pair(5)[:, :, :], ACT.Copy).then_inc(S("cmp_ready"), 1)
            act.wait_ge(*nth("cmp_ready", 1))
            act.activation(sm[:, 20:21], sm[:, 4:5], ACT.Copy).then_inc(S("cmp_ready"), 1)
            attend("a1")
            act.wait_ge(*nth("a1_o", 8))
            hT_high("oa1")
            norm_columns("a1", "m1")
            hT_copy("m1", ng[:, 1, :], modc[:, 24:32])
            hT_high("m1")
            route(1)
            experts_m("m1")
            norm_tiles("first")
            for l in range(2):
                tag, ffn = f"s{l}", f"f{l}"
                hT_copy(tag, *norm_columns_of[tag])
                hT_high(tag)
                for j in range(5):
                    z_copy(tag, j)
                act.wait_ge(*nth("absf", l + 1))
                ch(act.activation(fox[:, 1, :], fox[:, 1, :], ACT.Exp, scale=-1.0))
                ch.sync()
                act.activation(fox[:, 2, :], fox[:, 1, :], ACT.Ln, bias=1.0).then_inc(S("ln1p"), 1)
                z_copy(tag, 5)
                act.activation(z[:, :, 1796:2052], z[:, :, 1796:2052], ACT.Gelu).then_inc(S("gelu"), 1)
                act.activation(z[:, :, 1540:1796], z[:, :, 1540:1796], ACT.Gelu).then_inc(S("gelu"), 1)
                z_copy(tag, 6)
                act.wait_ge(*nth("sg_var", l + 1))
                act.activation(sm[:, 40:48], sm[:, 32:40], ACT.Sqrt).then_inc(S("sg_rstd"), 1)
                for j in range(7, 10):
                    z_copy(tag, j)
                qk_copy(tag, 4, [True, False, True, False])
                attend(tag)
                act.wait_ge(*nth(f"{tag}_o", 4))
                hT_high("o" + tag)
                out_splits(tag)
                root(f"ln1_{l}")
                hT_copy(ffn, *norm_columns_of[ffn])
                hT_high(ffn)
                experts_f(ffn)
                root(f"ln2_{l}")

        @block.vector
        def _(dve):
            ch = Chain(dve, "dve_chain")
            TT, TS, STT = dve.tensor_tensor, dve.tensor_scalar, dve.scalar_tensor_tensor

            def ts(o, a, s1, op0, s2=None, op1=None):
                if op1 is None:
                    return TS(out=o, in0=a, scalar1=s1, scalar2=None, op0=op0)
                return TS(out=o, in0=a, scalar1=s1, scalar2=s2, op0=op0, op1=op1)

            def stt(o, a, s, b, op0, op1):
                return STT(out=o, in0=a, scalar=s, in1=b, op0=op0, op1=op1)

            def norm(tag, parts):
                dve.wait_ge(*nth(f"{tag}_ssq", RECUR["ssq"][tag]))
                ch(dve.tensor_reduce(out=sm[:, 6:8], in_=ssq[:, :, 0:parts], axis=X, op=ALU.add))
                ch.sync()
                ch(ts(sm[:, 2:4], sm[:, 6:8], 1.0 / D, ALU.mult, ROT_EPS, ALU.add))
                ch.sync()
                dve.reciprocal(sm[:, 2:4], sm[:, 2:4]).then_inc(S(f"{tag}_var"), 1)
                dve.wait_ge(*nth(f"{tag}_rstd", 1))
                for t in range(NT):
                    ts(diag[:, t, :], ident, sm[:, 4 + t:5 + t], ALU.mult).then_inc(S(f"{tag}_diag"), 1)

            def hT_copy(tag, scale=None, bias=None):
                for c in (2, 3, 6, 7):
                    dve.wait_ge(*nth(f"{tag}_xT", c // 2 + 1))
                    src = pair(4 + c // 2)[:, c % 2, :]
                    if scale is None:
                        ins = dve.tensor_copy(hT[:, c, :], src)
                    else:
                        ins = ts(hT[:, c, :], src, scale[:, c:c + 1], ALU.mult,
                                 bias[:, c:c + 1], ALU.add)
                    ins.then_inc(S(f"{tag}_hT_dve"), 1)

            def split(n, more=0):
                for h in range(2):
                    dve.wait_ge(S("high_parts"), halves(n) - 1 + h + 12 * more)
                    hi, lo = half(n, h)
                    TT(lo, slot(n)[:, h * HALF:(h + 1) * HALF], hi.bitcast(f32), ALU.subtract)\
                        .then_inc(S("halves_split"), 1)

            def splits(first, last):
                for n in range(first, last + 1):
                    split(n)

            def hT_low(tag):
                for b in range(4):
                    dve.wait_ge(*nth(f"{tag}_hi", b + 1))
                    c = slice(2 * b, 2 * b + 2)
                    TT(hlo[:, c, :], hT[:, c, :], hhi[:, c, :].bitcast(f32), ALU.subtract)\
                        .then_inc(S(f"{tag}_lo"), 1)

            def mod_columns(l, turn, sublayers, b):
                bias = colA[:, 0:48] if l == 0 else colB[:, 0:48]
                dve.wait_ge(S("modc_ready"), turn)
                for s_ in sublayers:
                    c = slice(24 * s_, 24 * s_ + 16)
                    ch(TT(modc[:, c], bank[b][:, c], bias[:, c], ALU.add))
                ch.sync()
                for s_ in sublayers:
                    at = R_NG + (2 * l + s_) * NC
                    ins = stt(ng[:, s_, :], modc[:, 24 * s_ + 8:24 * s_ + 16], 1.0, colA[:, at:at + NC],
                              ALU.add, ALU.mult)
                    if s_ != sublayers[-1]:
                        ch(ins)
                ins.then_inc(S("ng_ready"), 1)
                dve.wait_ge(S("ng_ready"), turn)

            def mod_gates(l, b):
                dve.wait_ge(S("modg_ready"), l + 1)
                dve.wait_ge(S("gbc_landed"), 32 * (l + 1))
                for n in range(2):
                    for h in range(2):
                        v = gbc[:, n, h * 512:(h + 1) * 512]
                        ins = TT(v, v, bank[b + 2 * n + h][:, :], ALU.add)
                        if n * h == 0:
                            ch(ins)
                ins.then_inc(S("mod_done"), 1)
                dve.wait_ge(S("mod_done"), l + 1)

            def ada_rest_part(q):
                k, part = divmod(q, 4)
                b = rest_place[q]
                dve.wait_ge(S(f"ada_rest_landed{b}"), 16 * rest_place[:q + 1].count(b))
                o = acc[:, UNIT + part * HALF:UNIT + (part + 1) * HALF]
                if k == 0:
                    ins = ts(o, ada_rest[b], csil[:, 0:1], ALU.mult)
                else:
                    dve.wait_ge(S("ada0_rest"), q - 3)
                    ins = stt(o, ada_rest[b], csil[:, k:k + 1], o, ALU.mult, ALU.add)
                ins.then_inc(S("ada0_rest"), 1)

            def ada1(u, turn, block):
                for k in range(4):
                    b = k // 2
                    if k % 2 == 0:
                        dve.wait_ge(S(f"ada1_landed{b}"), turn * 32 + (16 * u + 16))
                    c = csil[:, 4 * u + k:4 * u + k + 1]
                    if k or u:
                        dve.wait_ge(S("ada1_step"), turn * 7 + (4 * u + k))
                    if u == 1 and k == 3:
                        o, sem = acc[:, ds(block * 384, 384)], "ada1_done"
                    else:
                        o, sem = adat[:, :], "ada1_step"
                    if k == 0 and u == 0:
                        if not isinstance(turn, int):
                            dve.wait_ge(S("ada1_done"), turn)
                        ins = ts(o, adaw[:, b, k % 2, :], c, ALU.mult)
                    else:
                        ins = stt(o, adaw[:, b, k % 2, :], c, adat[:, :], ALU.mult, ALU.add)
                    ins.then_inc(S(sem), 1)
                    if k % 2:
                        dve.tensor_copy(sm[:, 50:51], adaw[:, b, 1, 0:1]).then_inc(S("ada1_used"), 1)

            def rotate(tag, spans, tables, units=()):
                units = list(units)
                for c, nh in spans:
                    for t in range(NT):
                        hv = z[:, t, c:c + 64 * nh].rearrange("p (h d) -> p h d", d=64)
                        x1, x2 = hv[:, :, 0:ROT], hv[:, :, ROT:2 * ROT]
                        co, si = (v[:, t, :].unsqueeze(1).broadcast_to([P, nh, ROT]) for v in tables)
                        tmp = [rt[:, k, 0:8 * nh].rearrange("p (h d) -> p h d", d=ROT) for k in range(4)]
                        ch.sync()
                        ch(TT(tmp[0], x1, co, ALU.mult))
                        ch(TT(tmp[1], x2, si, ALU.mult))
                        ch(TT(tmp[2], x2, co, ALU.mult))
                        ch(TT(tmp[3], x1, si, ALU.mult))
                        ch.sync()
                        ch(TT(x1, tmp[0], tmp[1], ALU.subtract))
                        ch(TT(x2, tmp[2], tmp[3], ALU.add))
                        for n in units[:2]:
                            split(n)
                        units = units[2:]
                for n in units:
                    split(n)
                ch.sync()
                dve.tensor_copy(sm[:, 62:63], sm[:, 4:5]).then_inc(S(f"{tag}_roped"), 1)

            def attend(tag):
                jobs, units, ends = attention(tag)
                J = len(jobs)
                for j in range(J + 5):
                    if j < J:
                        dve.wait_ge(*nth(f"{tag}_scores", j + 1))
                        ch(dve.tensor_reduce(out=nmax[:, j % 4, 0:1], in_=bank[j % 4][:, 0:P], axis=X,
                                             op=ALU.max, negate=True))
                        dve.tensor_reduce(out=nmax[:, j % 4, 1:2], in_=bank[j % 4][:, P:384], axis=X,
                                          op=ALU.max, negate=True).then_inc(S(f"{tag}_max"), 1)
                    if j - 1 in ends:
                        U = units[ends[j - 1]]
                        dve.wait_ge(*nth(f"{tag}_exp", j))
                        for jj in U["jobs"]:
                            ch(dve.reciprocal(rsum[:, jj % 4, :], psum_[:, jj % 4, :]))
                        ch.sync()
                        b0 = U["jobs"][0] % 4
                        if tag == "a0":
                            b1 = U["jobs"][1] % 4
                            ch(ts(rsum[:, b1, :], rsum[:, b1, :], sm[:, 14:15], ALU.mult))
                        if tag == "a1":
                            gv = gate[:, :, 3 * U["h"] + 1 + U["w"]:3 * U["h"] + 2 + U["w"]]
                            ch(TT(rsum[:, b0, :], rsum[:, b0, :], gv.rearrange("p t o -> p (t o)"), ALU.mult))
                            ch.sync()
                        for t, (a, b) in enumerate(((0, P), (P, 384))):
                            ins = ts(prob[:, b0, a:b], prob[:, b0, a:b], rsum[:, b0, t:t + 1], ALU.mult)
                            if tag == "a0" or t == 0:
                                ch(ins)
                        if tag == "a0":
                            ch.sync()
                            for t, (a, b) in enumerate(((0, P), (P, 384))):
                                ins = stt(prob[:, b0, a:b], prob[:, b1, a:b], rsum[:, b1, t:t + 1],
                                          prob[:, b0, a:b], ALU.mult, ALU.add)
                                if t == 0:
                                    ch(ins)
                        ins.then_inc(S(f"{tag}_norm"), 1)
                        if tag == "a0":
                            n = ends[j - 1]
                            for q in {0: (24, 25), 1: (26, 27)}.get(n, (26 + n,) if n < 6 else ()):
                                ada_rest_part(q)
                    if j - 4 in ends and units[ends[j - 4]]["last"]:
                        u = ends[j - 4]
                        G = units[u]["group"]
                        dve.wait_ge(*nth(f"{tag}_pv", u + 1))
                        dve.tensor_copy(oT[:, G, :], bank[6 + G % 2][:, 0:SEQ]).then_inc(S(f"{tag}_o"), 1)

            def gated_residual(tag, n, following):
                for j in range(4):
                    split(N_OUT[tag] + j + 2)
                    dve.wait_ge(*nth(f"{tag}_out_done", j + 1))
                    gv = gbc[:, n, 256 * j:256 * j + 256].unsqueeze(1).broadcast_to([P, NT, 256])
                    ch(TT(xn[:, :, 256 * j:256 * j + 256], pair(4 + j)[:, :, :], gv, ALU.mult))
                    ch.sync()
                    TT(x[:, :, 256 * j:256 * j + 256], x[:, :, 256 * j:256 * j + 256],
                       xn[:, :, 256 * j:256 * j + 256], ALU.add).then_inc(S(f"{following}_x_part"), 1)

            def route(l):
                dve.wait_ge(*nth("logits_done", l + 1))
                dve.wait_ge(*nth("router_landed", 7 * 16 * (l + 1)))
                lv = bank[6][:, 0:128].rearrange("p (t n) -> p t n", t=NT)[:, :, 0:36]
                TT(lg[:, :, :], lv, rb[:, :].unsqueeze(1).broadcast_to([P, NT, 36]), ALU.add)\
                    .then_inc(S("logits_read"), 1)
                dve.wait_ge(*nth("logits_read", l + 1))

                def R(k, n):
                    return rs[:, k, 0:NT * n].rearrange("p (t n) -> p t n", t=NT)

                def col(k, at=0):
                    return rs[:, k, at:at + NT].rearrange("p (t o) -> p t o", o=1)

                def step(ins):
                    ch(ins)
                    ch.sync()

                def first_max(o, v, n, rev, sc, m, r):
                    step(dve.tensor_reduce(out=m, in_=v, axis=X, op=ALU.max))
                    step(TT(sc, v, m.broadcast_to([P, NT, n]), ALU.is_ge))
                    step(TT(sc, sc, cst[:, rev:rev + n].unsqueeze(1).broadcast_to([P, NT, n]), ALU.mult))
                    step(dve.tensor_reduce(out=r, in_=sc, axis=X, op=ALU.max))
                    step(TT(o, sc, r.broadcast_to([P, NT, n]), ALU.is_equal))

                lgrp, lexp = lg[:, :, 0:4], lg[:, :, 4:36]
                first_max(R(1, 4), lgrp, 4, C_R4, R(2, 4), col(9, 0), col(9, 2))
                step(TT(R(5, 4), lgrp, col(9, 0).broadcast_to([P, NT, 4]), ALU.subtract))
                oh = rs[:, 1, 0:8].rearrange("p (t g o) -> p t g o", t=NT, o=1).broadcast_to([P, NT, 4, 8])
                ohx = rs[:, 2, 0:64].rearrange("p (t g o) -> p t g o", t=NT, g=4)
                step(dve.tensor_copy(ohx, oh))
                step(TT(R(3, 32), lexp, R(2, 32), ALU.mult))
                step(ts(R(2, 32), R(2, 32), 1.0, ALU.subtract, -NEG, ALU.mult))
                step(TT(R(3, 32), R(3, 32), R(2, 32), ALU.add))
                first_max(R(4, 32), R(3, 32), 32, C_R32, R(7, 32), col(9, 4), col(9, 6))
                step(stt(R(3, 32), R(4, 32), 3.0 * NEG, R(3, 32), ALU.mult, ALU.add))
                first_max(R(8, 32), R(3, 32), 32, C_R32, R(7, 32), col(9, 8), col(9, 10))
                TT(rs[:, 5, 8:10], rs[:, 9, 8:10], rs[:, 9, 4:6], ALU.subtract).then_inc(S("route_diff"), 1)
                dve.wait_ge(*nth("route_exp", 2 * (l + 1)))
                step(dve.tensor_reduce(out=col(9, 12), in_=rs[:, 6, 0:8].rearrange("p (t n) -> p t n", t=NT),
                                       axis=X, op=ALU.add))
                step(stt(rs[:, 9, 14:16], rs[:, 6, 8:10], 1.0, rs[:, 9, 12:14], ALU.add, ALU.mult))
                step(dve.reciprocal(rs[:, 9, 16:18], rs[:, 9, 14:16]))
                step(TT(rs[:, 9, 18:20], rs[:, 9, 16:18], rs[:, 6, 8:10], ALU.mult))
                step(TT(R(4, 32), R(4, 32), col(9, 16).broadcast_to([P, NT, 32]), ALU.mult))
                step(TT(R(8, 32), R(8, 32), col(9, 18).broadcast_to([P, NT, 32]), ALU.mult))
                TT(R(0, 32), R(4, 32), R(8, 32), ALU.add).then_inc(S("combine_ready"), 1)

            def combine_rows(l):
                dve.wait_ge(*nth("combine_turned", l + 1))
                if l:
                    dve.wait_ge(*nth("combine_stored", 16 * l))
                dve.tensor_copy(cbT[:, :], bank[0][0:32, 0:SEQ]).then_inc(S("combine_rows_ready"), 1)

            def experts(tag):
                l, count = int(tag[1]), COUNT[tag]

                def activated(e, i=0, wait=True):
                    b = e % 2
                    if tag[0] == "m":
                        used(dve, unit_up(tag, e, 1), i)
                        row = cmb[:, ds(i * 2 + e, 1), :].broadcast_to([P, 2, SEQ])
                        TT(upc[:, b, :].rearrange("p (c n) -> p c n", c=2), pair(5 + 2 * b)[:, :, :], row,
                           ALU.mult).then_inc(S(f"{tag}_upc"), 1)
                        dve.wait_ge(*nth(f"{tag}_upc", i * 2 + e + 1))
                        value = upc[:, b, :]
                    else:
                        convolve(e, i)
                        value = cvt[:, b, 2:4, :].rearrange("p c n -> p (c n)")
                    dve.wait_ge(*nth(f"{tag}_silu", i * 2 + e + 1))
                    TT(upc[:, b, :], sil[:, b, :], value, ALU.mult).then_inc(S(f"{tag}_prod"), 1)
                    dve.wait_ge(*nth(f"{tag}_prod", i * 2 + e + 1))
                    if wait:
                        used(dve, unit_down(tag, e - 2), i)
                    dve.tensor_copy(ahi[:, b, :], upc[:, b, :]).then_inc(S(f"{tag}_ahi"), 1)
                    dve.wait_ge(S(f"{tag}_ahi"), i * 2 + e + 1)
                    TT(alo[:, b, :], upc[:, b, :], ahi[:, b, :].bitcast(f32), ALU.subtract)\
                        .then_inc(S(f"{tag}_aT"), 1)

                def convolve(e, i=0):
                    dve.wait_ge(*nth(f"{tag}_taps", i * 2 + e + 1))
                    for tap, sh in ((1, 1), (0, 2)):
                        for c in range(4):
                            src = pair(4 + 2 * (e % 2) + c // 2)[:, c % 2, 0:SEQ - sh]
                            o = cvt[:, e % 2, c, sh:SEQ]
                            if tap == 1:
                                dve.wait_ge(*nth(f"{tag}_tap2", i * 8 + (4 * e + 2 * (c // 2) + 2)))
                            else:
                                dve.wait_ge(*nth(f"{tag}_tap1", i * 8 + (4 * e + c + 1)))
                            ins = stt(o, src, cvcur[:, e % 2, tap, c:c + 1], o, ALU.mult, ALU.add)
                            if tap == 1:
                                ins.then_inc(S(f"{tag}_tap1"), 1)
                            elif c in (1, 3):
                                ins.then_inc(S(f"{tag}_conv" if c == 1 else f"{tag}_conv_value"), 1)
                    dve.wait_ge(*nth(f"{tag}_conv_value", i * 2 + e + 1))

                def taps(e, i=0):
                    if tag[0] == "m":
                        return
                    for half_ in range(2):
                        src = cvc[:, :, ds(i * 4 + (2 * e + 22 * half_), 2)]
                        ins = dve.tensor_copy(cvcur[:, e % 2, :, 2 * half_:2 * half_ + 2], src)
                        ins.then_inc(S(f"{tag}_taps" if half_ else f"{tag}_taps_gate"), 1)

                def step(e, i=0):
                    if tag == "m0":
                        ada1(e % 2, i + 1, i)
                    for k in range(3):
                        split(unit_down(tag, e) + 2 + k, i)
                    taps(e + 2, i)
                    activated(e + 2, i)

                first = N_EXP[tag]
                split(first + 2)
                split(first + 3)
                if tag[0] == "m":
                    combine_rows(l)
                    if tag == "m0":
                        ada1(1, 0, 15)
                    dve.wait_ge(*nth("combine_first", 16 * (l + 1)))
                taps(0)
                activated(0, wait=False)
                split(first + 4)
                split(first + 5)
                taps(1)
                activated(1, wait=False)
                if tag[0] == "m":
                    dve.wait_ge(*nth("combine_landed", 16 * (l + 1)))
                with dve.Fori(0, (count - 2) // 2) as i:
                    step(0, i)
                    step(1, i)
                if count % 2:
                    step(count - 3)
                for e in (count - 2, count - 1):
                    if unit_down(tag, e) + 2 < N_END:
                        split(unit_down(tag, e) + 2)
                following = {"m0": "a1", "m1": "first"}.get(tag)
                for t in range(NT):
                    if t == 0:
                        dve.wait_ge(*nth(f"{tag}_down_tile", 1))
                    else:
                        used(dve, unit_down(tag, count - 1))
                    for h in range(2):
                        cols = slice(h * 512, (h + 1) * 512)
                        if tag[0] == "m":
                            ch(TT(xn[:, t, cols], bank[2 * t + h][:, :], gbc[:, 1, cols], ALU.mult))
                            ch.sync()
                            TT(x[:, t, cols], x[:, t, cols], xn[:, t, cols], ALU.add)\
                                .then_inc(S(f"{following}_x_part"), 1)
                        else:
                            ch(stt(x[:, t, cols], x[:, t, cols], ALPHA, bank[2 * t + h][:, :], ALU.mult, ALU.add))
                            ch.sync()
                            ch(dve.bn_stats(out=stat[:, t, h, :], in_=x[:, t, cols]))

            experts_m = experts_f = experts

            def layer_norm(tag, l, parts):
                name = f"{tag}_{l}"
                ch.sync()
                for t in range(NT):
                    ch(dve.bn_aggr(out=mv[:, t, :], in_=stat[:, t, 0:parts, :]))
                ch.sync()
                ch(ts(sm[:, 2:4], mv[:, :, 1], LN_EPS, ALU.add))
                ch.sync()
                dve.reciprocal(sm[:, 2:4], sm[:, 2:4]).then_inc(S(f"{name}_var"), 1)
                dve.wait_ge(*nth(f"{name}_rstd", 1))
                for t in range(NT):
                    v = x[:, t, :]
                    ins = ts(v, v, mv[:, t, 0:1], ALU.subtract, sm[:, 4 + t:5 + t], ALU.mult)
                    if name != "ln2_1":
                        ins.then_inc(S(f"{name}_tile"), 1)
                    else:
                        ch(ins)
                        ch.sync()
                        dve.wait_ge(*nth(f"{tag}{l}_landed", 32))
                        ch(TT(v, v, gbc[:, 0, :], ALU.mult))
                        ch.sync()
                        TT(v, v, gbc[:, 1, :], ALU.add).then_inc(S(f"{name}_tile"), 1)

            def gain(tag, l):
                if tag == "first":
                    dve.wait_ge(*nth("s0_xT", 4))
                    dve.wait_ge(*nth("final_landed", 16))
                    for t in range(NT):
                        ch(stt(x[:, t, :], x[:, t, :], sm[:, 4 + t:5 + t], gbc[:, 0, :], ALU.mult, ALU.mult))
                    ch.sync()
                    dve.tensor_copy(sm[:, 61:62], sm[:, 4:5]).then_inc(S("first_done"), 1)
                    return
                name = f"{tag}_{l}"
                dve.wait_ge(*nth(f"f{l}_xT" if tag == "ln1" else f"s{l + 1}_xT", 4))
                dve.wait_ge(*nth(f"{tag}{l}_landed", 32))
                for op, n in ((ALU.mult, 0), (ALU.add, 1)):
                    ch(TT(x[:, :, :], x[:, :, :], gbc[:, n, :].unsqueeze(1).broadcast_to([P, NT, D]), op))
                    ch.sync()
                dve.tensor_copy(sm[:, 60:61], sm[:, 4:5]).then_inc(S(f"{name}_done"), 1)

            def ada_first(k):
                landed(dve, k)
                o = acc[:, 0:UNIT]
                if k == 0:
                    ins = ts(o, slot(k), csil[:, 0:1], ALU.mult)
                else:
                    dve.wait_ge(S("ada0_done"), k)
                    ins = stt(o, slot(k), csil[:, k:k + 1], o, ALU.mult, ALU.add)
                ins.then_inc(S("ada0_done"), 1)

            dve.wait_ge(*nth("csil_ready", 1))
            for k in range(4):
                ada_first(k)
            dve.wait_ge(*nth("lam_landed", 16))
            for n in range(2):
                ch(TT(rt[:, n, 0:64], lamt[:, 2 * n, :], lamt[:, 2 * n + 1, :], ALU.mult))
            ch.sync()
            dve.tensor_reduce(out=sm[:, 10:12], in_=rt[:, 0:2, 0:64], axis=X, op=ALU.add)\
                .then_inc(S("lam_dots"), 1)
            dve.wait_ge(*nth("pos_landed", 32))
            dve.wait_ge(*nth("const_landed", 16))
            ch(dve.tensor_copy(idb[:, :], ident))
            dve.tensor_copy(maskh[:, :], maskb).then_inc(S("mask_ready"), 1)
            ch(dve.tensor_copy(sm[:, 8:10], posi[:, :]))
            ch.sync()

            def step(ins):
                ch(ins)
                ch.sync()

            ang, k_, r_, rc = rope[:, 4, :], rope[:, 5, :], rope[:, 3, :], rope[:, 2, :]
            for t in range(NT):
                step(ts(ang[:, 8 * t:8 * t + 8], cst[:, C_INV:C_INV + 8], sm[:, 8 + t:9 + t], ALU.mult))
            step(ts(k_, ang, 1.0 / (2 * np.pi), ALU.mult, 12582912.0, ALU.add))
            step(ts(k_, k_, 12582912.0, ALU.subtract))
            c1 = 6.28125
            c2 = float(np.floor((2 * np.pi - c1) * 2 ** 21) / 2 ** 21)
            c3 = float(np.float32(2 * np.pi - c1 - c2))
            step(stt(r_, k_, -c1, ang, ALU.mult, ALU.add))
            step(stt(r_, k_, -c2, r_, ALU.mult, ALU.add))
            step(stt(r_, k_, -c3, r_, ALU.mult, ALU.add))
            lim = 3.1415925
            step(ts(rc, r_, float(np.pi / 2), ALU.add))
            step(ts(k_, rc, float(np.pi), ALU.is_gt))
            step(stt(rc, k_, float(-2 * np.pi), rc, ALU.mult, ALU.add))
            ts(rope[:, 2:4, :], rope[:, 2:4, :], lim, ALU.min, -lim, ALU.max).then_inc(S("angles"), 1)
            dve.wait_ge(*nth("lam_exp", 1))
            step(TT(sm[:, 14:15], sm[:, 13:14], sm[:, 12:13], ALU.subtract))
            step(ts(sm[:, 14:15], sm[:, 14:15], LAMBDA_INIT, ALU.subtract))
            dve.wait_ge(*nth("cols_turned", 1))
            ch(dve.tensor_copy(colA[:, :], bank[7][:, 0:R_END]))
            ch(dve.tensor_copy(colB[:, :], bank[7][:, P:P + 80]))
            ch(dve.tensor_copy(colC[:, :], bank[7][:, 2 * P:2 * P + 88]))
            ch.sync()
            step(ts(colA[:, R_SUB:R_SUB + 1], colA[:, R_SUB:R_SUB + 1], 1.0 - LAMBDA_INIT, ALU.mult))
            for k in range(4, NC):
                ada_first(k)
            splits(FIRST, FIRST + 1)
            norm("a0", 1)
            mod_columns(0, 1, (0,), 7)
            hT_copy("a0", ng[:, 0, :], modc[:, 0:8])
            hT_low("a0")
            for k in range(9):
                if k:
                    split(FIRST + 1 + k)
                ada_rest_part(2 * k)
                ada_rest_part(2 * k + 1)
            dve.wait_ge(*nth("rope_ready", 1))
            dve.wait_ge(*nth("a0_z", 8))
            tables = [rope[:, n, :].rearrange("p (t d) -> p t d", t=NT) for n in range(2)]
            split(FIRST + 10)
            ada_rest_part(18)
            ada_rest_part(19)
            rotate("a0", [(0, 32)], tables, [FIRST + 11, FIRST + 12, FIRST + 13])
            for q in range(20, 24):
                ada_rest_part(q)
            dve.wait_ge(*nth("a0_z", 12))
            attend("a0")
            dve.wait_ge(*nth("sub_sum", 1))
            step(ts(cbT[0:8, :], bank[1][0:8, 0:SEQ], 1.0 / P, ALU.mult, ROT_EPS, ALU.add))
            dve.reciprocal(cbT[0:8, :], cbT[0:8, :]).then_inc(S("sub_var"), 1)
            mod_columns(0, 2, (1,), 0)
            dve.wait_ge(*nth("a0_o", 8))
            for b in range(4):
                dve.wait_ge(*nth("sub_spread", b + 1))
                v = oT[:, 2 * b:2 * b + 2, :]
                stt(v, v, colA[:, R_SUB:R_SUB + 1], pair(b)[:, :, :], ALU.mult, ALU.mult)\
                    .then_inc(S("a0_oT"), 1)
            hT_low("oa0")
            mod_gates(0, 4)
            gated_residual("a0", 0, "m0")
            norm("m0", 4)
            hT_copy("m0", ng[:, 1, :], modc[:, 24:32])
            hT_low("m0")
            ada1(0, 0, 15)
            route(0)
            experts_m("m0")
            norm("a1", 2)
            mod_columns(1, 3, (0, 1), 7)
            hT_copy("a1", ng[:, 0, :], modc[:, 0:8])
            hT_low("a1")
            mod_gates(1, 0)
            u = N_IN["a1"]
            splits(u + 2, u + 5)
            dve.wait_ge(*nth("a1_z", 4))
            rotate("a1", [(1280, 8)], tables, [u + 6])
            for w in range(2):
                for g_ in range(2):
                    src = z[:, :, 1280 + 256 * w + 64 * g_:1344 + 256 * w + 64 * g_]
                    for dup in range(2):
                        ch(dve.tensor_copy(kd[:, :, 2 * w + g_, 64 * dup:64 * dup + 64], src))
            split(u + 7)
            dve.wait_ge(*nth("gate_exp", 1))
            step(ts(gate[:, :, :], gate[:, :, :], 1.0, ALU.add))
            step(dve.reciprocal(gate[:, :, :], gate[:, :, :]))
            dve.wait_ge(*nth("cmp_split", 1))
            for v in range(2):
                for g_ in range(2):
                    xv = bank[0][:, (v * 2 + g_) * 128:(v * 2 + g_) * 128 + 128].rearrange("p (n j) -> p j n", j=8)
                    for jh in range(2):
                        pv = colB[:, 48 + v * 16 + 8 * jh:56 + v * 16 + 8 * jh].unsqueeze(2).broadcast_to([P, 8, 15])
                        ch(TT(blk[:, v, 8 * jh:8 * jh + 8, 15 * g_:15 * g_ + 15], xv[:, :, jh:jh + 15], pv, ALU.add))
                ch.sync()
                step(dve.tensor_copy(blk_parts[0][:, v], blk[:, v]))
                TT(blk_parts[1][:, v], blk[:, v], blk_parts[0][:, v].bitcast(f32), ALU.subtract)\
                    .then_inc(S("blk_ready"), 1)
            splits(u + 8, u + 10)
            dve.wait_ge(*nth("a1_z", 6))
            rotate("a1", [(0, 8)], tables, [u + 11, u + 12])
            dve.wait_ge(*nth("cmp_kv", 1))
            ch(dve.tensor_copy(kcT, bank[2][:, 0:30]))
            dve.tensor_copy(vc[0:15, :, :], bank[2][0:15, 64:192].rearrange("p (g d) -> p g d", g=2))\
                .then_inc(S("cmp_kv_read"), 1)
            split(u + 13)
            dve.wait_ge(*nth("vc_spread", 1))
            for g_ in range(2):
                src = bank[3][:, g_ * 64:g_ * 64 + 64].unsqueeze(1).broadcast_to([P, 8, 64])
                msk = cst[:, C_BLK:C_BLK + 8].unsqueeze(2).broadcast_to([P, 8, 64])
                ins = TT(vblk[:, g_, :, :], src, msk, ALU.mult)
                if g_ == 0:
                    ch(ins)
            ins.then_inc(S("vblk_ready"), 1)
            dve.wait_ge(*nth("a1_z", 8))
            rotate("a1", [(512, 8)], tables)
            ch(dve.memset(pc[:, :, :, CMP_N:16], 0.0))
            dve.wait_ge(*nth("cmp_scores", 1))
            pch = pc.rearrange("p t (h a) n -> p t h a n", a=2)
            for par in range(2):
                src = bank[4 + par][:, 0:256].rearrange("p (t h n) -> p t h n", t=NT, h=8)
                for t in range(NT):
                    mk = cst[:, C_CB + CMP_N * t:C_CB + CMP_N * (t + 1)].unsqueeze(1).broadcast_to([P, 8, CMP_N])
                    ch(TT(pch[:, t, :, par, 0:CMP_N], src[:, t, :, 0:CMP_N], mk, ALU.add))
            ch.sync()
            pcm = pc.rearrange("p t h n -> p (t h) n")[:, :, 0:CMP_N]
            step(dve.tensor_reduce(out=cms[:, 0, :], in_=pcm, axis=X, op=ALU.max))
            TT(pcm, pcm, cms[:, 0, :].unsqueeze(2).broadcast_to([P, 32, CMP_N]), ALU.subtract)\
                .then_inc(S("pc_diff"), 1)
            dve.wait_ge(*nth("pc_exp", 1))
            for t in range(NT):
                mk = cst[:, C_C01 + CMP_N * t:C_C01 + CMP_N * (t + 1)].unsqueeze(1).broadcast_to([P, 16, CMP_N])
                ch(TT(pc[:, t, :, 0:CMP_N], pc[:, t, :, 0:CMP_N], mk, ALU.mult))
            ch.sync()
            step(dve.tensor_reduce(out=cms[:, 1, :], in_=pcm, axis=X, op=ALU.add))
            step(ts(cms[:, 1, :], cms[:, 1, :], 1e-30, ALU.max))
            step(dve.reciprocal(cms[:, 2, :], cms[:, 1, :]))
            for t in range(NT):
                gv = gate[:, t, :].rearrange("p (h a) -> p h a", a=3)[:, :, 0]
                ch(TT(cms[:, 3, 16 * t:16 * t + 16], cms[:, 2, 16 * t:16 * t + 16], gv, ALU.mult))
            ch.sync()
            TT(pcm, pcm, cms[:, 3, :].unsqueeze(2).broadcast_to([P, 32, CMP_N]), ALU.mult)\
                .then_inc(S("pc_ready"), 1)
            attend("a1")
            hT_low("oa1")
            gated_residual("a1", 0, "m1")
            norm("m1", 4)
            hT_copy("m1", ng[:, 1, :], modc[:, 24:32])
            hT_low("m1")
            route(1)
            experts_m("m1")
            norm("first", 2)
            tables2 = [cst[:, c:c + 16].rearrange("p (t d) -> p t d", t=NT) for c in (C_COS, C_SIN)]
            for l in range(2):
                tag, ffn = f"s{l}", f"f{l}"
                hT_copy(tag, *norm_columns_of[tag])
                hT_low(tag)
                u = N_IN[tag]
                splits(u + 2, u + 5)
                dve.wait_ge(*nth(f"{tag}_z", 4))
                dve.wait_ge(*nth("mix_landed", 6 * 16 * (l + 1)))
                step(TT(fox[:, 0, :].rearrange("p (t h) -> p t h", t=NT), z[:, :, 1536:1540],
                        bfor[:, :].unsqueeze(1).broadcast_to([P, NT, 4]), ALU.add))
                stt(fox[:, 1, :], fox[:, 0, :], -1.0, fox[:, 0, :], ALU.mult, ALU.max).then_inc(S("absf"), 1)
                split(u + 6)
                dve.wait_ge(*nth("ln1p", l + 1))
                step(ts(fox[:, 0, :], fox[:, 0, :], 0.0, ALU.min))
                TT(fox[:, 3, :], fox[:, 0, :], fox[:, 2, :], ALU.subtract).then_inc(S("logf_ready"), 1)
                dve.wait_ge(*nth("sgw_turned", l + 1))
                step(TT(sgwT, bank[3][:, :].rearrange("p (g n) -> p g n", g=4),
                        tri.unsqueeze(1).broadcast_to([P, 4, P]), ALU.mult))
                dve.wait_ge(*nth("conv_turned", l + 1))
                step(dve.tensor_copy(cvc, bank[2][:, 0:176].rearrange("p (w n) -> p w n", w=4)))
                split(u + 7)
                dve.wait_ge(*nth("cum_done", l + 1))
                ch(dve.tensor_copy(cum[:, 0, :], bank[1][0:4, 0:SEQ]))
                ch(ts(cum[:, 1, :], bank[1][0:4, 0:SEQ], -1.0, ALU.mult))
                dve.wait_ge(*nth("pooled", l + 1))
                dve.tensor_copy(pool, pair(0)[:, :, :]).then_inc(S("pool_ready"), 1)
                dve.wait_ge(*nth("gelu", 2 * l + 1))
                vv = z[:, :, 1796:2052].rearrange("p t (g c) -> p t g c", g=4)
                sq = sgt.rearrange("p t (g c) -> p t g c", g=4)

                def per(at, n=64):
                    return sm[:, at:at + 8].rearrange("p (t g o) -> p t g o", t=NT, o=1)\
                        .broadcast_to([P, NT, 4, n])

                step(dve.tensor_reduce(out=sm[:, 16:24], in_=vv, axis=X, op=ALU.add))
                step(ts(sm[:, 16:24], sm[:, 16:24], 1.0 / 64, ALU.mult))
                step(TT(vv, vv, per(16), ALU.subtract))
                step(TT(sq, vv, vv, ALU.mult))
                step(dve.tensor_reduce(out=sm[:, 24:32], in_=sq, axis=X, op=ALU.add))
                step(ts(sm[:, 24:32], sm[:, 24:32], 1.0 / 64, ALU.mult, LN_EPS, ALU.add))
                dve.reciprocal(sm[:, 32:40], sm[:, 24:32]).then_inc(S("sg_var"), 1)
                split(u + 8)
                dve.wait_ge(*nth("sg_rstd", l + 1))
                step(TT(vv, vv, per(40), ALU.mult))
                vt = z[:, :, 1796:2052]
                step(TT(vt, vt, sgl[:, 0, :].unsqueeze(1).broadcast_to([P, NT, 256]), ALU.mult))
                TT(vt, vt, sgl[:, 1, :].unsqueeze(1).broadcast_to([P, NT, 256]), ALU.add)\
                    .then_inc(S("sgv_ready"), 1)
                split(u + 9)
                dve.wait_ge(*nth(f"{tag}_z", 6))
                rotate(tag, [(0, 8)], tables2)
                dve.wait_ge(*nth("gelu", 2 * l + 2))
                dve.wait_ge(*nth("sg_mixed", l + 1))
                for g_ in range(4):
                    at = R_SB + 4 * l + g_
                    c = slice(64 * g_, 64 * g_ + 64)
                    ins = stt(sgt[:, :, c], pair(2)[:, :, c], colA[:, at:at + 1],
                              z[:, :, 1540 + 64 * g_:1604 + 64 * g_], ALU.add, ALU.mult)
                    if g_ < 3:
                        ch(ins)
                ins.then_inc(S("sgy_ready"), 1)
                dve.wait_ge(*nth("pool_mixed", l + 1))
                for c in range(2):
                    at = R_PS + 2 * l + c
                    ch(ts(oT[:, 6 + c, :], pair(0)[:, c, :], colA[:, at:at + 1], ALU.mult))
                splits(u + 10, u + 11)
                dve.wait_ge(*nth("sg_turned", l + 1))
                dve.tensor_copy(oT[:, 4:6, :], pair(3)[:, :, :]).then_inc(S("mix_read"), 1)
                gain("first" if l == 0 else "ln2", 0)
                attend(tag)
                hT_low("o" + tag)
                for j in range(4):
                    split(N_OUT[tag] + j + 2)
                    dve.wait_ge(*nth(f"{tag}_out_done", j + 1))
                    v = x[:, :, 256 * j:256 * j + 256]
                    ch(stt(v, v, ALPHA, pair(4 + j)[:, :, :], ALU.mult, ALU.add))
                    ch.sync()
                    for t in range(NT):
                        ch(dve.bn_stats(out=stat[:, t, j, :], in_=v[:, t, :]))
                layer_norm("ln1", l, 4)
                hT_copy(ffn, *norm_columns_of[ffn])
                hT_low(ffn)
                gain("ln1", l)
                experts_f(ffn)
                layer_norm("ln2", l, 2)


_UNUSED = ()


def kernel(**inputs):
    import concourse.bacc as _bacc
    from concourse.bass_utils import run_bass_kernel_spmd as _run

    nc = _bacc.Bacc("TRN2", target_bir_lowering=False, num_devices=1)
    arrays, aps = {}, {}
    inputs = dict(inputs)
    for name, a in inputs.items():
        a = np.ascontiguousarray(a)
        arrays[f"in_{name}"] = a
        aps[name] = nc.dram_tensor(f"in_{name}", a.shape, mybir.dt.from_np(a.dtype), kind="ExternalInput").ap()
    c = constants()
    arrays["in_consts"] = c
    aps["consts"] = nc.dram_tensor("in_consts", c.shape, mybir.dt.float32, kind="ExternalInput").ap()
    out = nc.dram_tensor("out_x", (1, SEQ, D), mybir.dt.float32, kind="ExternalOutput").ap()
    build(nc, aps, out)
    r = _run(nc, [arrays], core_ids=[0])
    return r.results[0]["out_x"]
```
